# Optimizing a Trainium2 kernel written in Bass

```python
import jax, jax.numpy as jnp
from jax import lax
import numpy as np

D_MODEL = 1024
BATCH = 1
SEQ = 512
DEPTH = 2
DEC_BATCH = 8
DEC_SEQ = 8
PAST_LEN = 2048
PAGE_SIZE = 128

N_MIXERS = 2
HEAD_DIM = 64
MIX_W = D_MODEL
MEM_HEADS = 4
MEM_W = MEM_HEADS * HEAD_DIM
N_MEM = 256
FOX_W = MIX_W - MEM_W
FOX_HEADS = FOX_W // HEAD_DIM
CONV_CH = MIX_W - MEM_W
CONV_WIDTH = 31
D_FF = ((8 * D_MODEL + 3 * 256 - 1) // (3 * 256)) * 256
Q_BLOCK = 128
N_CONV_LAYERS = (DEPTH + 1) // 2
N_FOX_LAYERS = DEPTH // 2
FORGET_BIAS_MIN = 3.0
FORGET_BIAS_MAX = 12.0
EPS = 1e-6
NEG_INF = -1e30

kernel_name = 'hybrid_conformer_conv_fox_memory_decoder_step'

def rmsnorm(x, g):
    xf = x.astype(jnp.float32)
    y = xf * lax.rsqrt(jnp.mean(xf * xf, axis=-1, keepdims=True) + EPS)
    return (y * g.astype(jnp.float32)).astype(x.dtype)

def layernorm(x, g, b):
    xf = x.astype(jnp.float32)
    mu = jnp.mean(xf, axis=-1, keepdims=True)
    xc = xf - mu
    y = xc * lax.rsqrt(jnp.mean(xc * xc, axis=-1, keepdims=True) + EPS)
    return (y * g.astype(jnp.float32) + b.astype(jnp.float32)).astype(x.dtype)

def swiglu(h, w_gu, w_dn):
    gu = h @ w_gu
    return (jax.nn.silu(gu[..., :D_FF]) * gu[..., D_FF:]) @ w_dn

def conv_module(z, buf, dw, dw_b, ln_g, ln_b):
    u = z[..., :CONV_CH] * jax.nn.sigmoid(z[..., CONV_CH:])
    u_full = jnp.concatenate([buf.astype(u.dtype), u], axis=1)
    y = lax.conv_general_dilated(u_full, dw[:, None, :].astype(u.dtype), (1,), 'VALID',
                                 dimension_numbers=('NWC', 'WIO', 'NWC'),
                                 feature_group_count=CONV_CH) + dw_b.astype(u.dtype)
    y = jax.nn.silu(layernorm(y, ln_g, ln_b))
    return y, u_full[:, -(CONV_WIDTH - 1):]

def fox_heads(z, b_f, g_q, g_k):
    b, l, _ = z.shape
    shp = (b, l, FOX_HEADS, HEAD_DIM)
    q = rmsnorm(z[..., :FOX_W].reshape(shp), g_q)
    k = rmsnorm(z[..., FOX_W:2 * FOX_W].reshape(shp), g_k)
    v = z[..., 2 * FOX_W:3 * FOX_W].reshape(shp)
    logf = jax.nn.log_sigmoid(z[..., 3 * FOX_W:3 * FOX_W + FOX_HEADS].astype(jnp.float32)
                              + b_f.astype(jnp.float32))
    return q, k, v, logf

def fox_prompt(q, k, v, logf):
    b, s, h, d = q.shape
    nb = s // Q_BLOCK
    scale = HEAD_DIM ** -0.5
    c_k = jnp.transpose(lax.cumsum(logf, axis=1), (0, 2, 1))
    qb = q.reshape(b, nb, Q_BLOCK, h, d).transpose(1, 0, 2, 3, 4)
    cb = c_k.reshape(b, h, nb, Q_BLOCK).transpose(2, 0, 1, 3)
    pos = jnp.arange(s, dtype=jnp.int32)
    pb = pos.reshape(nb, Q_BLOCK)

    def block(args):
        qi, ci, pi = args
        sc = jnp.einsum('bqhd,bkhd->bhqk', qi, k).astype(jnp.float32) * scale
        sc = sc + ci[..., :, None] - c_k[:, :, None, :]
        sc = jnp.where((pi[:, None] >= pos[None, :])[None, None], sc, NEG_INF)
        p = jax.nn.softmax(sc, axis=-1)
        return jnp.einsum('bhqk,bkhd->bqhd', p.astype(v.dtype), v)

    out = lax.map(block, (qb, cb, pb))
    return out.transpose(1, 0, 2, 3, 4).reshape(b, s, h, d)

def fox_sample(q, k, v, logf, k_pool, v_pool, lf_pool, page_table):
    bd, t, h, d = q.shape
    p_len = page_table.shape[1] * k_pool.shape[1]
    scale = HEAD_DIM ** -0.5
    k_past = k_pool[page_table].reshape(bd, p_len, h, d)
    v_past = v_pool[page_table].reshape(bd, p_len, h, d)
    lf_past = lf_pool[page_table].reshape(bd, p_len, h).astype(jnp.float32)
    r_past = lax.cumsum(lf_past, axis=1, reverse=True) - lf_past
    cq = jnp.transpose(lax.cumsum(logf, axis=1), (0, 2, 1))
    s_past = (jnp.einsum('bqhd,bkhd->bhqk', q, k_past).astype(jnp.float32) * scale
              + cq[..., :, None] + jnp.transpose(r_past, (0, 2, 1))[:, :, None, :])
    s_new = (jnp.einsum('bqhd,bkhd->bhqk', q, k).astype(jnp.float32) * scale
             + cq[..., :, None] - cq[:, :, None, :])
    causal = jnp.tril(jnp.ones((t, t), dtype=bool))
    s_new = jnp.where(causal[None, None], s_new, NEG_INF)
    p = jax.nn.softmax(jnp.concatenate([s_past, s_new], axis=-1), axis=-1)
    return (jnp.einsum('bhqk,bkhd->bqhd', p[..., :p_len].astype(v.dtype), v_past)
            + jnp.einsum('bhqk,bkhd->bqhd', p[..., p_len:].astype(v.dtype), v))

def memory_kv(mem, g_norm, w_kv, g_k):
    kv = rmsnorm(mem, g_norm) @ w_kv
    b, n, _ = kv.shape
    k = rmsnorm(kv[..., :MEM_W].reshape(b, n, MEM_HEADS, HEAD_DIM), g_k)
    v = kv[..., MEM_W:].reshape(b, n, MEM_HEADS, HEAD_DIM)
    return k, v

def memory_attend(qm, km, vm):
    sc = jnp.einsum('bqhd,bmhd->bhqm', qm, km).astype(jnp.float32) * (HEAD_DIM ** -0.5)
    p = jax.nn.softmax(sc, axis=-1)
    return jnp.einsum('bhqm,bmhd->bqhd', p.astype(vm.dtype), vm)

def finish_layer(x, mix, qm, km, vm, g_qm, w_o, g2, w_gu, w_dn):
    b, l, _ = x.shape
    qm = rmsnorm(qm.reshape(b, l, MEM_HEADS, HEAD_DIM), g_qm)
    mo = memory_attend(qm, km, vm).reshape(b, l, MEM_W)
    x = x + jnp.concatenate([mix, mo], axis=-1) @ w_o
    return x + swiglu(rmsnorm(x, g2), w_gu, w_dn)

def setup_inputs(seed: int = 0) -> dict:
    key = jax.random.key(seed)
    ks = iter(jax.random.split(key, 40))

    def nrm(shape, scale=1.0):
        return jax.random.normal(next(ks), shape, jnp.float32) * scale

    def gain(shape):
        return 1.0 + nrm(shape, 0.02)

    nc, nf = N_CONV_LAYERS, N_FOX_LAYERS
    n_pages = PAST_LEN // PAGE_SIZE
    n_used = DEC_BATCH * n_pages
    n_phys = n_used + max(1, n_used // 4)
    perm = jax.random.permutation(next(ks), n_phys)
    page_table = perm[:n_used].reshape(DEC_BATCH, n_pages).astype(jnp.int32)
    head_bias = jnp.linspace(FORGET_BIAS_MIN, FORGET_BIAS_MAX, FOX_HEADS, dtype=jnp.float32)
    return {
        'x_prompt': nrm((BATCH, SEQ, D_MODEL)),
        'x_sample': nrm((DEC_BATCH, DEC_SEQ, D_MODEL)),
        'cache_conv': nrm((nc, DEC_BATCH, CONV_WIDTH - 1, CONV_CH), 0.5),
        'cache_fox_k': nrm((nf, n_phys, PAGE_SIZE, FOX_HEADS, HEAD_DIM)),
        'cache_fox_v': nrm((nf, n_phys, PAGE_SIZE, FOX_HEADS, HEAD_DIM)),
        'cache_fox_logf': jax.nn.log_sigmoid(head_bias + nrm((nf, n_phys, PAGE_SIZE, FOX_HEADS))),
        'cache_mem_k': nrm((DEPTH, DEC_BATCH, N_MEM, MEM_HEADS, HEAD_DIM)),
        'cache_mem_v': nrm((DEPTH, DEC_BATCH, N_MEM, MEM_HEADS, HEAD_DIM)),
        'page_table': page_table,
        'mem_prompt': nrm((BATCH, N_MEM, D_MODEL)),
        'norm1': gain((DEPTH, D_MODEL)),
        'conv_w_in': nrm((nc, D_MODEL, 2 * CONV_CH + MEM_W), D_MODEL ** -0.5),
        'conv_dw': nrm((nc, CONV_WIDTH, CONV_CH), CONV_WIDTH ** -0.5),
        'conv_dw_b': nrm((nc, CONV_CH), 0.02),
        'conv_ln_g': gain((nc, CONV_CH)),
        'conv_ln_b': nrm((nc, CONV_CH), 0.02),
        'fox_w_in': nrm((nf, D_MODEL, 3 * FOX_W + FOX_HEADS + MEM_W), D_MODEL ** -0.5),
        'fox_b_f': head_bias + nrm((nf, FOX_HEADS), 0.1),
        'fox_q_norm': gain((nf, HEAD_DIM)),
        'fox_k_norm': gain((nf, HEAD_DIM)),
        'mem_norm': gain((DEPTH, D_MODEL)),
        'w_mem_kv': nrm((DEPTH, D_MODEL, 2 * MEM_W), D_MODEL ** -0.5),
        'mem_q_norm': gain((DEPTH, HEAD_DIM)),
        'mem_k_norm': gain((DEPTH, HEAD_DIM)),
        'w_out': nrm((DEPTH, MIX_W, D_MODEL), MIX_W ** -0.5),
        'norm2': gain((DEPTH, D_MODEL)),
        'w_gate_up': nrm((DEPTH, D_MODEL, 2 * D_FF), D_MODEL ** -0.5),
        'w_down': nrm((DEPTH, D_FF, D_MODEL), D_FF ** -0.5),
    }

def reference(x_prompt, x_sample, cache_conv, cache_fox_k, cache_fox_v, cache_fox_logf,
              cache_mem_k, cache_mem_v, page_table, mem_prompt, norm1, conv_w_in, conv_dw,
              conv_dw_b, conv_ln_g, conv_ln_b, fox_w_in, fox_b_f, fox_q_norm, fox_k_norm,
              mem_norm, w_mem_kv, mem_q_norm, mem_k_norm, w_out, norm2, w_gate_up, w_down):
    xp, xs = x_prompt, x_sample
    conv_p, conv_s = [], []
    fk_p, fv_p, fl_p, fk_s, fv_s, fl_s = [], [], [], [], [], []
    mk_p, mv_p = [], []
    for i in range(DEPTH):
        hp = rmsnorm(xp, norm1[i])
        hs = rmsnorm(xs, norm1[i])
        km_p, vm_p = memory_kv(mem_prompt, mem_norm[i], w_mem_kv[i], mem_k_norm[i])
        mk_p.append(km_p)
        mv_p.append(vm_p)
        j = i // N_MIXERS
        if i % N_MIXERS == 0:
            zp = hp @ conv_w_in[j]
            zs = hs @ conv_w_in[j]
            buf0 = jnp.zeros((xp.shape[0], CONV_WIDTH - 1, CONV_CH), zp.dtype)
            mix_p, st_p = conv_module(zp[..., :2 * CONV_CH], buf0, conv_dw[j], conv_dw_b[j],
                                      conv_ln_g[j], conv_ln_b[j])
            mix_s, st_s = conv_module(zs[..., :2 * CONV_CH], cache_conv[j], conv_dw[j], conv_dw_b[j],
                                      conv_ln_g[j], conv_ln_b[j])
            conv_p.append(st_p)
            conv_s.append(st_s)
            qm_p = zp[..., 2 * CONV_CH:]
            qm_s = zs[..., 2 * CONV_CH:]
        else:
            zp = hp @ fox_w_in[j]
            zs = hs @ fox_w_in[j]
            qp, kp, vp, lfp = fox_heads(zp, fox_b_f[j], fox_q_norm[j], fox_k_norm[j])
            qs, ks_, vs, lfs = fox_heads(zs, fox_b_f[j], fox_q_norm[j], fox_k_norm[j])
            mix_p = fox_prompt(qp, kp, vp, lfp).reshape(xp.shape[0], xp.shape[1], FOX_W)
            mix_s = fox_sample(qs, ks_, vs, lfs, cache_fox_k[j], cache_fox_v[j], cache_fox_logf[j],
                               page_table).reshape(xs.shape[0], xs.shape[1], FOX_W)
            fk_p.append(kp)
            fv_p.append(vp)
            fl_p.append(lfp)
            fk_s.append(ks_)
            fv_s.append(vs)
            fl_s.append(lfs)
            qm_p = zp[..., 3 * FOX_W + FOX_HEADS:]
            qm_s = zs[..., 3 * FOX_W + FOX_HEADS:]
        xp = finish_layer(xp, mix_p, qm_p, km_p, vm_p, mem_q_norm[i], w_out[i], norm2[i],
                          w_gate_up[i], w_down[i])
        xs = finish_layer(xs, mix_s, qm_s, cache_mem_k[i], cache_mem_v[i], mem_q_norm[i], w_out[i],
                          norm2[i], w_gate_up[i], w_down[i])
    return (xp, xs, jnp.stack(conv_p), jnp.stack(fk_p), jnp.stack(fv_p), jnp.stack(fl_p),
            jnp.stack(mk_p), jnp.stack(mv_p), jnp.stack(conv_s), jnp.stack(fk_s), jnp.stack(fv_s),
            jnp.stack(fl_s))


_drawn_inputs = setup_inputs


def setup_inputs(seed=0):
    import zlib

    import numpy as np

    out = dict(_drawn_inputs(seed))
    spreads = {}
    factors = {'conv_ln_g': 4.097,
     'conv_ln_b': 4.502,
     'fox_q_norm': 37.65,
     'fox_k_norm': 7.827,
     'mem_norm': 2.861,
     'mem_q_norm': 8.0,
     'norm2': 2.864}
    for name, (base, spread) in spreads.items():
        noise = np.random.default_rng([zlib.crc32(name.encode()), seed]).standard_normal(out[name].shape)
        drawn = base * np.exp(spread * noise) if base else spread * noise
        out[name] = __import__('jax').numpy.asarray(drawn.astype(out[name].dtype))
    for name, factor in factors.items():
        out[name] = (out[name] * factor).astype(out[name].dtype)
    return out
```

```python
from contextlib import ExitStack

import concourse.bass as bass
from concourse import mybir

ALU = mybir.AluOpType
ACT = mybir.ActivationFunctionType
F32 = mybir.dt.float32
F32R = mybir.dt.float32r
I32 = mybir.dt.int32
AX_X = mybir.AxisListType.X

P = 128
EPS = 1e-6
NEG = -1e30
ATANH_TERMS = 8


class Steps:

    def __init__(self, semaphore):
        self.semaphore, self.n, self.per_pass, self.i = semaphore, 0, 0, None

    def inc(self, instruction):
        instruction.then_inc(self.semaphore, 1)
        self.n += 1

    def value(self):
        return self.n if self.i is None else self.i * self.per_pass + self.n

    def enter(self, i, per_pass):
        self.i, self.per_pass, self.first = i, per_pass, self.n

    def leave(self, passes):
        assert self.n - self.first == self.per_pass, (self.n - self.first, self.per_pass)
        self.i, self.n = None, self.first + passes * self.per_pass


def build(nc, x_prompt, x_sample, cache_conv, cache_fox_k, cache_fox_v, cache_fox_logf,
          cache_mem_k, cache_mem_v, page_table, mem_prompt, norm1, conv_w_in, conv_dw,
          conv_dw_b, conv_ln_g, conv_ln_b, fox_w_in, fox_b_f, fox_q_norm, fox_k_norm,
          mem_norm, w_mem_kv, mem_q_norm, mem_k_norm, w_out, norm2, w_gate_up, w_down,
          y_prompt, y_sample, new_conv_p, new_fox_k_p, new_fox_v_p, new_fox_logf_p,
          new_mem_k_p, new_mem_v_p, new_conv_s, new_fox_k_s, new_fox_v_s, new_fox_logf_s):
    SEQ, D = x_prompt.shape[1:]
    NB, NQ = x_sample.shape[:2]
    NS = NB * NQ
    T = SEQ + NS
    HT = T // 2
    KD = D // P
    TT = SEQ // P
    W = conv_dw.shape[1]
    H = W - 1
    CH = conv_dw.shape[2]
    KC = CH // P
    DF = w_down.shape[1]
    KF = DF // P
    KF2 = KF // 2
    NH, DH = cache_fox_k.shape[3:]
    HP = NH // 2
    NP, PG = page_table.shape[1], cache_fox_k.shape[2]
    N_PHYS = cache_fox_k.shape[1]
    MH = cache_mem_k.shape[3]
    NM = mem_prompt.shape[1]
    MT = NM // P
    MW = MH * DH
    MP = MH // 2
    GS = 4
    GR = NB // GS
    ROWS = NH * NQ
    QR = 4 * NQ
    SCALE = float(DH) ** -0.5
    NPAST = NP * PG
    CPG = 2
    NCH = NP // CPG
    KEYS = CPG * PG
    assert P == PG and T % 2 == 0 and HT <= 512 and KF % 2 == 0 and NS <= P and MH == 4
    assert QR == 32 and ROWS == 3 * QR and KC == HP and MP == MT == 2 and KD == KC + MP

    C_CONV = 0
    C_MEM0 = C_CONV + 2 * KC + MP
    N_MEM = 4
    C_WO0 = C_MEM0 + N_MEM
    C_GU0 = C_WO0 + KD
    C_DN0 = C_GU0 + 2 * KF
    C_FOX = C_DN0 + 2 * KD
    N_FOX = 1 + 3 * HP + MP
    C_MEM1 = C_FOX + N_FOX
    C_WO1 = C_MEM1 + N_MEM
    C_GU1 = C_WO1 + KD
    C_DN1 = C_GU1 + 2 * KF
    C_END = C_DN1 + 2 * KD
    C_MEM, C_WO, C_GU, C_DN = (C_MEM0, C_MEM1), (C_WO0, C_WO1), (C_GU0, C_GU1), (C_DN0, C_DN1)
    KM = KD // N_MEM
    SMALL, LARGE = KD * P, KF2 * P
    assert KM * 2 * MW == SMALL

    def chunk_size(n):
        return LARGE if C_DN0 <= n < C_FOX or C_DN1 <= n else SMALL

    VEC_LOADS = 6 + 8 + 1 + 2 + 1
    CONSTS0, CONSTS1 = 9, 12 + NB

    MEM_UNITS = [("mem", hp, t, NM) for hp in range(MP) for t in range(TT)]
    FOX_UNITS = [("fox", hp, t, (t + 1) * P) for hp in range(HP) for t in range(TT)]

    with ExitStack() as ctx:
        def sem(name):
            return ctx.enter_context(nc.semaphore(name))

        top = [nc.sbuf_base + (-nc.sbuf_base) % 32]

        def at(name, shape, offset, dt=F32):
            size = 4
            for n in shape[1:]:
                size *= n
            end = offset + size + (-size) % 32
            assert end <= nc.sbuf_usable_end, (name, end)
            return nc.alloc_sbuf_tensor_at(name, shape, dt, offset=offset), end

        def sb(name, shape, dt=F32):
            buffer, top[0] = at(name, shape, top[0], dt)
            return buffer

        xT = sb("xT", [P, KD, T])
        aH = sb("aH", [P, KD, T], F32R)
        aL = sb("aL", [P, KD, T], F32R)
        raw = sb("raw", [P, 2, LARGE])
        wH = [sb(f"wH{s}", [P, LARGE], F32R) for s in range(2)]
        wL = [sb(f"wL{s}", [P, LARGE], F32R) for s in range(2)]
        sq = sb("sq", [P, 2, T])
        tmp = sb("tmp", [P, 2, T])
        rb = sb("rb", [P, T])
        ident = sb("ident", [P, P])
        ones = sb("ones", [P, P])
        blocks = sb("blocks", [P, P])
        after = sb("after", [P, P])
        V_N1, V_N2, V_MEM = 0, 2 * KD, 4 * KD
        V_DWB, V_LNG, V_LNB = 6 * KD, 6 * KD + KC, 6 * KD + 2 * KC
        V_MQ = 6 * KD + 3 * KC
        N_VEC = V_MQ + 4
        vec = sb("vec", [P, N_VEC])
        dw = sb("dw", [P, KC, W])
        eps = sb("eps", [P, 3])
        dw2 = sb("dw2", [P, 2, W + 1])
        gk_row = sb("gk_row", [P, 2, DH])
        bf = sb("bf", [NH, 1])
        stat = sb("stat", [P, 64])
        pages = sb("pages", [1, NB * NP], I32)
        BASE = top[0]

        def memory_buffers(n, o, far):
            b = {}
            for name, shape in (("prob", [P, 2, 2, 512 if n else NM]), ("pT", [P, 2, 4, P]), ("km", [P, MT, MW]),
                                ("vm", [P, MT, MW]), ("kmT", [P, MP, NM]), ("qm", [P, MP, T]),
                                ("qd", [P, GS, MP, QR]), ("o", [P, MW])):
                b[name], o = at(f"{name}{n}", shape, o)
            end = o
            o = far or o
            b["mem"], o = at(f"mem{n}", [P, MT, D], o)
            b["mH"], o = at(f"mH{n}", [P, KD, NM], o, F32R)
            b["mL"], o = at(f"mL{n}", [P, KD, NM], o, F32R)
            far_end = o
            o = far or (end if not n else o)
            if not n:
                o = far_end
            b["ks"], o = at(f"ks{n}", [P, GS, MT, MW], o)
            b["vs"], o = at(f"vs{n}", [P, GS, MT, MW], o)
            b["ksT"], o = at(f"ksT{n}", [P, GS, MP, NM], o)
            return b, end, o

        uP, o = at("uP", [P, KC, H + SEQ], BASE)
        uS, o = at("uS", [P, KC, NB, H + NQ], o)
        yc_at = o
        yc, o = at("yc", [P, KC, T], o)
        mb0, _, o0 = memory_buffers(0, o, None)
        ks_at = o0 - 3 * 4 * GS * MT * MW
        stP, o = at("stP", [H, CH], ks_at)
        stS, o = at("stS", [GS * H, GR, CH], o)
        usc, o = at("usc", [P, KC, NB, H], o)
        xin, o = at("xin", [P, TT + 1, D], yc_at)
        vrow, o = at("vrow", [N_VEC, P], o)
        dwrow, o = at("dwrow", [W, CH], o)
        crow, o = at("crow", [GS * H, GR, CH], o)
        gH, o = at("gH", [P, KF, T], BASE, F32R)
        gL, o = at("gL", [P, KF, T], o, F32R)
        qkT, o = at("qkT", [P, 2 * HP, T], BASE)
        vtok, o = at("vtok", [P, TT + 1, CH], o)
        lf, o = at("lf", [P, TT + 1, NH], o)
        ctok, o = at("ctok", [P, TT + 1, NH], o)
        work, o = at("work", [P, 4, (TT + 1) * NH], o)
        maskd, o = at("maskd", [P, P], o)
        sameq, o = at("sameq", [NS, NS], o)
        mshift, o = at("mshift", [ROWS, NS - NQ + NS], o)
        maskb, o = at("maskb", [ROWS, NS], o)
        mshT, o = at("mshT", [NS - NQ + NS, ROWS], o)
        bm, o = at("bm", [NS, NB], o)
        dq, o = at("dq", [NS, NQ], o)
        cqA, o = at("cqA", [NS, NH, NQ], o)
        cqr, o = at("cqr", [ROWS, NB], o)
        ncx, o = at("ncx", [NS, NH, NQ], o)
        rx, o = at("rx", [P, 2, CPG, NH, NQ], o)
        qx, o = at("qx", [P, HP, QR], o)
        lfp, o = at("lfp", [P, NP, NH], o)
        lfa, o = at("lfa", [P, NP, NH], o)
        rtok, o = at("rtok", [P, NP, NH], o)
        ncT, o = at("ncT", [P, SEQ], o)
        mix_at = o
        assert mix_at % 32 == 0
        far1 = mix_at + 4 * (2 * 2 * 512 + 2 * 4 * P + 2 * MT * MW + MP * NM + MP * T + GS * MP * QR + MW)
        mb1, z_end, _ = memory_buffers(1, mix_at, far1)
        assert z_end == far1
        ktok, _ = at("ktok", [P, 2, CH], far1)
        lfd, e_ = at("lfd", [P, TT, P], far1 + 4 * 2 * CH)
        win, _ = at("win", [P, 2 * SEQ - P], e_)
        kT, o = at("kT", [P, 2, HP, KEYS], mix_at)
        S, o = at("S", [ROWS, NPAST + NS], o)
        pTs, o = at("pTs", [P, NP + 1, ROWS], o)
        kring, o = at("kring", [P, 2, CPG, CH], o)
        vring, o = at("vring", [P, 2, CPG, CH], o)
        os_, o = at("os_", [ROWS, 4 * DH], o)
        L1_END = o
        ystage, _ = at("ystage", [P, 2, D], BASE)
        MBS = (mb0, mb1)

        ps = ctx.enter_context(nc.psum_tensor("ps", [P, 8, 512], F32))

        def acc(slot):
            return ps[:, 2 * slot:2 * slot + 2, 0:HT]

        def halves(ap):
            return ap.rearrange("p (a n) -> p a n", a=2)

        x_in, vec_in, hist_in, mem_in, pages_in = (sem(n) for n in ("x_in", "vec_in", "hist_in", "mem_in", "pages_in"))
        raw_in = [sem(f"raw_in{s}") for s in range(2)]
        ks_in = sem("ks_in")
        k_in = [sem(f"k_in{s}") for s in range(2)]
        v_in = [sem(f"v_in{s}") for s in range(2)]
        lf_in = sem("lf_in")
        hi_done, lo_done, w_used, acc_ready, acc_free = (sem(n) for n in ("hi_done", "lo_done", "w_used", "acc_ready", "acc_free"))
        consts = sem("consts")
        consts1 = sem("consts1")
        vchain = sem("vchain")
        ysq_used, swish_done, usc_done = sem("ysq_used"), sem("swish_done"), sem("usc_done")
        x_new, sq_done, sq_used, ss_ready = (sem(n) for n in ("x_new", "sq_done", "sq_used", "ss_ready"))
        v_done, vH_done, a_ready = (sem(n) for n in ("v_done", "vH_done", "a_ready"))
        tr_ready, tr_free = sem("tr_ready"), sem("tr_free")
        sig_done, sig_used, u_done, y_done, ysq_done, ln_ready = (sem(n) for n in ("sig_done", "sig_used", "u_done", "y_done", "ysq_done", "ln_ready"))
        lny_done, mixf_done = sem("lny_done"), sem("mixf_done")
        norm_root, head_root, ln_root, mem_root, kss_done, k_root = (sem(n) for n in ("norm_root", "head_root", "ln_root", "mem_root", "kss_done", "k_root"))
        z_done, hn_ready, hn_done = (sem(n) for n in ("z_done", "hn_ready", "hn_done"))
        ms_done, mn_done, mt_done, mH_done, mL_done, kvsq_done, kv_done = (sem(n) for n in ("ms_done", "mn_done", "mt_done", "mH_done", "mL_done", "kvsq_done", "kv_done"))
        at_s, at_max, at_exp, at_prob, at_pv, at_hi, at_lo = (sem(n) for n in ("at_s", "at_max", "at_exp", "at_prob", "at_pv", "at_hi", "at_lo"))
        qd_done, oT_ready, oT_hi = sem("qd_done"), sem("oT_ready"), sem("oT_hi")
        silu_done, g_done, gH_done, gL_done = (sem(n) for n in ("silu_done", "g_done", "gH_done", "gL_done"))
        e_done, zab_done, c_ready, c_done, stage_done = (sem(n) for n in ("e_done", "zab_done", "c_ready", "c_done", "stage_done"))
        qx_done, lfa_done, r_ready, rx_done = (sem(n) for n in ("qx_done", "lfa_done", "r_ready", "rx_done"))
        kt_ready, kt_ev_v, kt_ev_a, kt_used = (sem(n) for n in ("kt_ready", "kt_ev_v", "kt_ev_a", "kt_used"))
        sc_ready, sc_free, sn_ready, sn_free = (sem(n) for n in ("sc_ready", "sc_free", "sn_ready", "sn_free"))
        smax_done, sexp_done, pt_ready, pt_free, o_ready, o_done = (sem(n) for n in ("smax_done", "sexp_done", "pt_ready", "pt_free", "o_ready", "o_done"))
        k_used, v_used = sem("k_used"), sem("v_used")
        stored = sem("stored")
        k_stored = [sem(f"k_stored{s}") for s in range(2)]
        y_stored = [sem(f"y_stored{s}") for s in range(2)]

        block = ctx.enter_context(nc.Block())

        marks = {}

        def columns(w, start, k0=0, ks=KD):
            return w.rearrange("(k p) n -> p k n", p=P)[:, k0:k0 + ks, bass.ds(start, P)]

        @block.vector
        def _(dve):
            steps = Steps(vchain)
            tr = [0]

            def link(instruction):
                steps.inc(instruction)
                dve.wait_ge(vchain, steps.value())

            def lo(n0, i=0):
                s, size = n0 % 2, chunk_size(n0)
                dve.wait_ge(hi_done, n0 + 1 + 2 * i)
                nc.vector.tensor_tensor(wL[s][:, 0:size], raw[:, s, 0:size], wH[s][:, 0:size].bitcast(F32),
                                        ALU.subtract).then_inc(lo_done, 1)

            def group():
                g = tr[0]
                tr[0] += 1
                dve.wait_ge(tr_ready, g + 1)
                return ps[:, 6 + g % 2, :]

            def norm(r):
                gain = (V_N1, V_N2)[r % 2] + (r // 2) * KD
                dve.wait_ge(norm_root, r + 1)
                link(nc.vector.reciprocal(rb[:], rb[:]))
                for k in range(KD + 1):
                    if k < KD:
                        if KD * r + k >= 2:
                            dve.wait_ge(a_ready, KD * r + k - 1)
                        nc.vector.scalar_tensor_tensor(out=tmp[:, k % 2], in0=xT[:, k], scalar=vec[:, gain + k:gain + k + 1],
                                                       in1=rb[:], op0=ALU.mult, op1=ALU.mult).then_inc(v_done, 1)
                    if k:
                        dve.wait_ge(vH_done, KD * r + k)
                        nc.vector.tensor_tensor(aL[:, k - 1], tmp[:, (k - 1) % 2], aH[:, k - 1].bitcast(F32),
                                                ALU.subtract).then_inc(a_ready, 1)

            def finish_head(z0, out, gain, h0, i=0):
                dve.wait_ge(head_root, h0 + 1 + 2 * i)
                link(nc.vector.reciprocal(rb[:], rb[:]))
                nc.vector.scalar_tensor_tensor(out=out, in0=tmp[:, z0 % 2], scalar=vec[:, gain:gain + 1], in1=rb[:],
                                               op0=ALU.mult, op1=ALU.mult).then_inc(hn_done, 1)

            def memory(l):
                mb = MBS[l]
                dve.wait_ge(mem_root, l + 1)
                link(nc.vector.reciprocal(stat[:, 34:34 + MT], stat[:, 34:34 + MT]))
                for t in range(MT):
                    last = nc.vector.tensor_scalar(mb["mem"][:, t], mb["mem"][:, t], stat[:, 34 + t:35 + t], None, ALU.mult)
                last.then_inc(mn_done, 1)
                for g in range(KD // 2):
                    bank = group()
                    if g >= 2:
                        dve.wait_ge(mL_done, l * KD // 2 + g - 1)
                    for k in range(2):
                        gain = V_MEM + l * KD + 2 * g + k
                        last = nc.vector.tensor_scalar(tmp[:, g % 2, k * NM:(k + 1) * NM], bank[:, k * NM:(k + 1) * NM],
                                                       vec[:, gain:gain + 1], None, ALU.mult)
                    last.then_inc(tr_free, 1)
                    marks["memory", l, g] = tr[0]
                    dve.wait_ge(mH_done, l * KD // 2 + g + 1)
                    nc.vector.tensor_tensor(mb["mL"][:, 2 * g:2 * g + 2, :].rearrange("p k n -> p (k n)"), tmp[:, g % 2, 0:2 * NM],
                                            mb["mH"][:, 2 * g:2 * g + 2, :].rearrange("p k n -> p (k n)").bitcast(F32),
                                            ALU.subtract).then_inc(mL_done, 1)
                for i in range(N_MEM):
                    lo(C_MEM[l] + 1 + i)
                dve.wait_ge(kvsq_done, l + 1)
                (nc.vector.tensor_reduce(stat[:, 36:36 + MT * MH].rearrange("p (t h) -> p t h", t=MT),
                                             sq[:, :, 0:MW].rearrange("p t (h d) -> p t h d", h=MH), AX_X, ALU.add)).then_inc(kss_done, 1)
                dve.wait_ge(k_root, l + 1)
                link(nc.vector.reciprocal(stat[:, 44:44 + MT * MH], stat[:, 44:44 + MT * MH]))
                for t in range(MT):
                    link(nc.vector.tensor_tensor(mb["km"][:, t].rearrange("p (h d) -> p h d", h=MH),
                                                 ps[:, t, 0:MW].rearrange("p (h d) -> p h d", h=MH),
                                                 stat[:, 44 + MH * t:44 + MH * t + MH].unsqueeze(2).broadcast_to([P, MH, DH]), ALU.mult))
                    last = nc.vector.tensor_tensor(mb["km"][:, t].rearrange("p (h d) -> p h d", h=MH),
                                                   mb["km"][:, t].rearrange("p (h d) -> p h d", h=MH),
                                                   gk_row[:, l:l + 1, :].broadcast_to([P, MH, DH]), ALU.mult)
                last.then_inc(kv_done, 1)
                bank = group()
                nc.vector.tensor_copy(mb["kmT"][:].rearrange("p a n -> p (a n)"), bank).then_inc(tr_free, 1)

            def top_of(u, unit, mb):
                kind, hp, t, keys = unit
                banks = ps[:, 2 * (u % 2):2 * (u % 2) + 2, 0:keys]
                st = stat[:, 8 * (u % 2):8 * (u % 2) + 8]
                dve.wait_ge(at_s, u + 1)
                if kind == "fox":
                    for e in range(2):
                        c_q = ctok[:, t, 2 * hp + e:2 * hp + e + 1]
                        if t:
                            nc.vector.tensor_scalar(mb["prob"][:, u % 2, e, 0:keys - P], banks[:, e, 0:keys - P], c_q, None, ALU.add)
                        last = nc.vector.scalar_tensor_tensor(out=mb["prob"][:, u % 2, e, keys - P:keys], in0=banks[:, e, keys - P:keys],
                                                              scalar=c_q, in1=maskd[:], op0=ALU.add, op1=ALU.add)
                    link(last)
                    banks = mb["prob"][:, u % 2, :, 0:keys]
                nc.vector.tensor_reduce(st[:, 0:2], banks, AX_X, ALU.max, negate=True).then_inc(at_max, 1)

            def attend(u0, units, mb, h0):
                top_of(u0, units[0], mb)
                for i, (kind, hp, t, keys) in enumerate(units):
                    u = u0 + i
                    st = stat[:, 8 * (u % 2):8 * (u % 2) + 8]
                    dve.wait_ge(at_exp, u + 1)
                    link(nc.vector.reciprocal(st[:, 4:6], st[:, 2:4]))
                    for e in range(2):
                        last = nc.vector.tensor_scalar(mb["prob"][:, u % 2, e, 0:keys], mb["prob"][:, u % 2, e, 0:keys],
                                                       st[:, 4 + e:5 + e], None, ALU.mult)
                    last.then_inc(at_prob, 1)
                    if i + 1 < len(units):
                        top_of(u + 1, units[i + 1], mb)
                    if kind == "mem":
                        bank = group()
                        nc.vector.tensor_copy(mb["pT"][:, :, 0:2, :].rearrange("p e k q -> p e (k q)"),
                                              bank.rearrange("p (e n) -> p e n", e=2)).then_inc(tr_free, 1)
                    else:
                        for e in range(2):
                            bank = group()
                            nc.vector.tensor_copy(mb["pT"][:, e, 0:t + 1, :].rearrange("p k q -> p (k q)"),
                                                  bank[:, 0:keys]).then_inc(tr_free, 1)
                    tile = hp if kind == "fox" else KC + hp
                    dve.wait_ge(at_hi, h0 + i + 1)
                    nc.vector.tensor_tensor(aL[:, tile, t * P:(t + 1) * P], ps[:, 4 + u % 2, 0:P],
                                            aH[:, tile, t * P:(t + 1) * P].bitcast(F32), ALU.subtract).then_inc(at_lo, 1)

            def sample_memory(l, u0):
                mb = MBS[l]
                link(nc.vector.memset(mb["qd"][:], 0.0))
                for G in range(GR):
                    u = u0 + G
                    st = stat[:, 8 * (u % 2):8 * (u % 2) + 8]
                    if G:
                        dve.wait_ge(at_s, u)
                    for hp in range(MP):
                        for e in range(2):
                            r = slice(DH * e, DH * e + DH)
                            col = (2 * hp + e) * NQ
                            src = mb["qm"][r, hp, SEQ + G * GS * NQ:SEQ + (G + 1) * GS * NQ].rearrange("p (b q) -> p b q", b=GS)
                            last = nc.vector.tensor_copy(mb["qd"][r, :, hp, col:col + NQ], src)
                    last.then_inc(qd_done, 1)
                    for b in range(GS):
                        bank = group()
                        nc.vector.tensor_copy(mb["ksT"][:, b].rearrange("p a n -> p (a n)"), bank).then_inc(tr_free, 1)
                    dve.wait_ge(at_s, u + 1)
                    nc.vector.tensor_reduce(st[:, 0:1], ps[:, 2 * (u % 2), 0:NM], AX_X, ALU.max, negate=True).then_inc(at_max, 1)
                    dve.wait_ge(at_exp, u + 1)
                    link(nc.vector.reciprocal(st[:, 4:5], st[:, 2:3]))
                    nc.vector.tensor_scalar(mb["prob"][:, u % 2, 0, 0:NM], mb["prob"][:, u % 2, 0, 0:NM], st[:, 4:5], None,
                                            ALU.mult).then_inc(at_prob, 1)
                    bank = group()
                    nc.vector.tensor_copy(mb["pT"][:, 0, 0:MT, :].rearrange("p k q -> p (k q)"), bank[:, 0:MT * P]).then_inc(tr_free, 1)
                    dve.wait_ge(at_pv, u + 1)
                    nc.vector.tensor_copy(mb["o"][:], ps[:, 4 + u % 2, 0:MW]).then_inc(at_lo, 1)
                    marks["sample memory", l, G] = tr[0]
                    bank = group()
                    dve.wait_ge(oT_hi, GR * l + G + 1)
                    for s in range(MP):
                        for e in range(2):
                            r = slice(DH * e, DH * e + DH)
                            src = bank[r, s * P:(s + 1) * P].rearrange("p (b h q) -> p b h q", b=GS, h=MH)[:, :, 2 * s + e, :]
                            to = slice(SEQ + G * GS * NQ, SEQ + (G + 1) * GS * NQ)
                            last = nc.vector.tensor_tensor(aL[r, KC + s, to].rearrange("p (b q) -> p b q", b=GS), src,
                                                           aH[r, KC + s, to].rearrange("p (b q) -> p b q", b=GS).bitcast(F32), ALU.subtract)
                    last.then_inc(tr_free, 1)

            def residual(c0, per_tile, r, last_norm=False):
                def tile(j0, i):
                    for s in range(per_tile):
                        n0 = c0 + per_tile * j0 + s + 1
                        if n0 < C_END:
                            lo(n0, i if per_tile == 1 else 2 * i)
                    dve.wait_ge(w_used, c0 + per_tile * (j0 + 1) + 2 * per_tile * i)
                    x = xT[:, bass.ds(j0 + 2 * i, 1), :].rearrange("p o (a n) -> p (o a) n", a=2)
                    nc.vector.tensor_tensor(x, x, acc(j0 % 2), ALU.add).then_inc(x_new, 1)
                with dve.Fori(0, KD // 2 - 1) as i:
                    for j in range(2):
                        tile(j, i)
                for j in range(KD - 2, KD):
                    tile(j, 0)

            def ffn(l):
                c0, g0 = C_GU[l], l * KF

                def tile(f0, i):
                    lo(c0 + 2 * f0 + 1, 2 * i)
                    lo(c0 + 2 * f0 + 2, 2 * i)
                    dve.wait_ge(silu_done, g0 + f0 + 1 + 2 * i)
                    dve.wait_ge(w_used, c0 + 2 * f0 + 2 + 4 * i)
                    if g0 + f0 >= 2:
                        dve.wait_ge(gL_done, g0 + f0 - 1 + 2 * i)
                    nc.vector.tensor_tensor(halves(tmp[:, f0 % 2]), acc(2 * (f0 % 2) + 1), halves(sq[:, f0 % 2]),
                                            ALU.mult).then_inc(g_done, 1)
                    dve.wait_ge(gH_done, g0 + f0 + 1 + 2 * i)
                    f = bass.ds(f0 + 2 * i, 1)
                    nc.vector.tensor_tensor(gL[:, f, :].rearrange("p o n -> p (o n)"), tmp[:, f0 % 2],
                                            gH[:, f, :].rearrange("p o n -> p (o n)").bitcast(F32), ALU.subtract).then_inc(gL_done, 1)
                for f in range(2):
                    tile(f, 0)
                with dve.Fori(0, KF2 - 2) as i:
                    for f in range(2, 4):
                        tile(f, i)
                for f in range(KF - 2, KF):
                    tile(f, 0)

            dve.wait_ge(consts, CONSTS0)
            for t in range(TT + 1):
                rows = P if t < TT else NS
                for q in range(KD // 4):
                    bank = group()
                    last = nc.vector.tensor_copy(xT[:, 4 * q:4 * q + 4, t * P:t * P + rows],
                                                 bank[:, 0:4 * rows].rearrange("p (k n) -> p k n", k=4))
                    last.then_inc(tr_free, 1)
            steps.inc(nc.vector.memset(uP[:, :, 0:H], 0.0))
            bank = group()
            nc.vector.tensor_copy(vec[:], bank[:, 0:N_VEC]).then_inc(tr_free, 1)
            dve.wait_ge(tr_free, tr[0])
            link(nc.vector.tensor_scalar(vec[:, 0:6 * KD], vec[:, 0:6 * KD], float(D) ** 0.5, None, ALU.mult))
            link(nc.vector.tensor_scalar(vec[:, V_MQ + 3:V_MQ + 4], vec[:, V_MQ + 3:V_MQ + 4], float(DH) ** 0.5, None, ALU.mult))
            dve.wait_ge(vec_in, VEC_LOADS * 16)
            link(nc.vector.tensor_scalar(gk_row[:], gk_row[:], float(DH) ** 0.5, None, ALU.mult))
            bank = group()
            nc.vector.tensor_copy(dw[:].rearrange("p c w -> p (c w)"), bank[:, 0:KC * W]).then_inc(tr_free, 1)
            for G in range(GR):
                for first, count in ((0, 4), (4, KC - 4)):
                    bank = group()
                    for c in range(count):
                        last = nc.vector.tensor_copy(uS[:, first + c, G * GS:(G + 1) * GS, 0:H],
                                                     bank[:, c * GS * H:(c + 1) * GS * H].rearrange("p (b n) -> p b n", b=GS))
                    last.then_inc(tr_free, 1)
            marks["start"] = tr[0]
            lo(0)
            norm(0)

            def glu(c0, i):
                c = bass.ds(c0 + 2 * i, 1)
                dve.wait_ge(sig_done, c0 + 1 + 2 * i)
                a = acc(2 * (c0 % 2))
                sg = halves(sq[:, c0 % 2])
                nc.vector.tensor_tensor(uP[:, c, H:H + HT].rearrange("p o n -> p (o n)"), a[:, 0, :], sg[:, 0, :], ALU.mult)
                nc.vector.tensor_tensor(uP[:, c, H + HT:H + SEQ].rearrange("p o n -> p (o n)"), a[:, 1, 0:SEQ - HT],
                                        sg[:, 1, 0:SEQ - HT], ALU.mult)
                nc.vector.tensor_tensor(uS[:, c, :, H:H + NQ].rearrange("p o b n -> p (o b) n"),
                                        a[:, 1, SEQ - HT:HT].rearrange("p (b n) -> p b n", b=NB),
                                        sg[:, 1, SEQ - HT:HT].rearrange("p (b n) -> p b n", b=NB), ALU.mult).then_inc(u_done, 1)
                dve.wait_ge(u_done, c0 + 1 + 2 * i)

            def taps(c0, i):
                c = bass.ds(c0 + 2 * i, 1)
                y = yc[:, c, :].rearrange("p o n -> p (o n)")
                for j in range(W):
                    w = dw2[:, c0 % 2, j:j + 1]
                    uj = uP[:, c, j:j + SEQ].rearrange("p o n -> p (o n)")
                    sj = uS[:, c, :, j:j + NQ].rearrange("p o b n -> p (o b) n")
                    yp, ysm = y[:, 0:SEQ], y[:, SEQ:T].rearrange("p (b n) -> p b n", b=NB)
                    if j == 0:
                        b = dw2[:, c0 % 2, W:W + 1]
                        one = nc.vector.tensor_scalar(yp, uj, w, b, ALU.mult, ALU.add)
                        two = nc.vector.tensor_scalar(ysm, sj, w, b, ALU.mult, ALU.add)
                    else:
                        one = nc.vector.scalar_tensor_tensor(out=yp, in0=uj, scalar=w, in1=yp, op0=ALU.mult, op1=ALU.add)
                        two = nc.vector.scalar_tensor_tensor(out=ysm, in0=sj, scalar=w, in1=ysm, op0=ALU.mult, op1=ALU.add)
                    if j < W - 1:
                        link(two)
                    else:
                        two.then_inc(y_done, 1)

            def conv_tile(c0, i):
                lo(C_CONV + 2 * c0 + 1, 2 * i)
                lo(C_CONV + 2 * c0 + 2, 2 * i)
                glu(c0, i)
                c = bass.ds(c0 + 2 * i, 1)
                nc.vector.tensor_copy(dw2[:, c0 % 2, 0:W], dw[:, c, :].rearrange("p o w -> p (o w)"))
                link(nc.vector.tensor_copy(dw2[:, c0 % 2, W:W + 1], vec[:, bass.ds(V_DWB + c0 + 2 * i, 1)]))
                taps(c0, i)
            with dve.Fori(0, KC // 2) as i:
                steps.enter(i, 2 * W)
                for c in range(2):
                    conv_tile(c, i)
            steps.leave(KC // 2)
            for z in range(MP):
                lo(C_CONV + 2 * KC + z + 1)
                if z:
                    finish_head(z - 1, mb0["qm"][:, z - 1], V_MQ, z - 1)
            finish_head(MP - 1, mb0["qm"][:, MP - 1], V_MQ, MP - 1)

            for first, count in ((0, 4), (4, KC - 4)):
                bank = group()
                nc.vector.tensor_copy(stP[:, first * P:(first + count) * P], bank[0:H, 0:count * P]).then_inc(tr_free, 1)
            for G in range(GR):
                for first, count in ((0, 4), (4, KC - 4)):
                    bank = group()
                    nc.vector.tensor_copy(stS[:, G, first * P:(first + count) * P], bank[0:GS * H, 0:count * P]).then_inc(tr_free, 1)
            marks["conv states"] = tr[0]
            memory(0)
            attend(0, MEM_UNITS, mb0, 0)
            sample_memory(0, len(MEM_UNITS))
            u = len(MEM_UNITS) + GR

            dve.wait_ge(ln_ready, 1)
            link(nc.vector.tensor_scalar(halves(rb[:]), ps[:, 0:2, 0:HT], 1.0 / CH, None, ALU.mult))
            for c in range(KC):
                nc.vector.tensor_tensor(yc[:, c], yc[:, c], rb[:], ALU.subtract).then_inc(lny_done, 1)
            dve.wait_ge(ln_root, 1)
            link(nc.vector.reciprocal(rb[:], rb[:]))
            for c in range(KC + 1):
                if c < KC:
                    nc.vector.scalar_tensor_tensor(out=yc[:, c], in0=yc[:, c], scalar=vec[:, V_LNG + c:V_LNG + c + 1], in1=rb[:],
                                                   op0=ALU.mult, op1=ALU.mult).then_inc(lny_done, 1)
                if c:
                    dve.wait_ge(mixf_done, c)
                    nc.vector.tensor_tensor(aL[:, c - 1], yc[:, c - 1], aH[:, c - 1].bitcast(F32), ALU.subtract).then_inc(stage_done, 1)
            residual(C_WO0, 1, 1)
            norm(1)
            ffn(0)
            residual(C_DN0, 2, 2)
            norm(2)

            dve.wait_ge(consts1, CONSTS1)
            link(nc.vector.memset(work[:, 0], 0.0))
            link(nc.vector.memset(lfd[:], 0.0))
            link(nc.vector.memset(qx[:], 0.0))
            Z = MP
            lo(C_FOX + 1)
            lo(C_FOX + 2)
            dve.wait_ge(hn_ready, Z + 1)
            nc.vector.tensor_copy(work[:, 0, 0:TT * NH], ps[:, 4, 0:TT * NH])
            nc.vector.tensor_copy(work[0:NS, 0, TT * NH:], ps[0:NS, 4, TT * NH:(TT + 1) * NH]).then_inc(hn_done, 1)
            dve.wait_ge(hn_done, Z + 1)
            nc.vector.scalar_tensor_tensor(out=work[:, 1], in0=work[:, 0], scalar=-1.0, in1=work[:, 0],
                                           op0=ALU.mult, op1=ALU.max).then_inc(zab_done, 1)
            z_, e_, s_, s2 = (work[:, n] for n in range(4))
            dve.wait_ge(e_done, 1)
            link(nc.vector.tensor_scalar(s2, e_, 2.0, None, ALU.add))
            link(nc.vector.reciprocal(s2, s2))
            link(nc.vector.tensor_tensor(s_, e_, s2, ALU.mult))
            link(nc.vector.tensor_tensor(s2, s_, s_, ALU.mult))
            link(nc.vector.tensor_scalar(e_, s2, 1.0 / (2 * ATANH_TERMS - 1), None, ALU.mult))
            for n in range(ATANH_TERMS - 2, 0, -1):
                link(nc.vector.scalar_tensor_tensor(out=e_, in0=e_, scalar=1.0 / (2 * n + 1), in1=s2, op0=ALU.add, op1=ALU.mult))
            link(nc.vector.scalar_tensor_tensor(out=s_, in0=e_, scalar=1.0, in1=s_, op0=ALU.add, op1=ALU.mult))
            link(nc.vector.tensor_scalar(z_, z_, 0.0, None, ALU.min))
            link(nc.vector.scalar_tensor_tensor(out=lf[:].rearrange("p t h -> p (t h)"), in0=s_, scalar=-2.0, in1=z_,
                                                op0=ALU.mult, op1=ALU.add))
            for e in range(2):
                last = nc.vector.tensor_copy(lfd[:, :, DH * e:DH * e + NH], lf[:, 0:TT, :])
            last.then_inc(c_ready, 1)

            def head_pass(z0, first, gain, i):
                lo(C_FOX - Z + z0 + 2, i)
                finish_head(z0, qkT[:, bass.ds(first + 2 * i, 1), :].rearrange("p o n -> p (o n)"), gain, z0 - 1, i)
            for first, gain in ((0, V_MQ + 2), (HP, V_MQ + 3)):
                with dve.Fori(0, HP // 2) as i:
                    steps.enter(i, 2)
                    for s in range(2):
                        head_pass(Z + 1 + first + s, first + s, gain, i)
                steps.leave(HP // 2)
            for hp in range(HP):
                z = Z + 1 + 2 * HP + hp
                lo(C_FOX - Z + z + 2)
                dve.wait_ge(hn_ready, z + 1)
                nc.vector.tensor_copy(vtok[:, 0:TT, hp * P:(hp + 1) * P], ps[:, 4, 0:TT * P].rearrange("p (t n) -> p t n", t=TT))
                nc.vector.tensor_copy(vtok[0:NS, TT, hp * P:(hp + 1) * P], ps[0:NS, 5, 0:P]).then_inc(hn_done, 1)
            for hp in range(MP):
                z = Z + 1 + 3 * HP + hp
                if z - Z + C_FOX + 2 <= C_MEM1:
                    lo(C_FOX - Z + z + 2)
                finish_head(z, mb1["qm"][:, hp], V_MQ + 1, MP + 2 * HP + hp)

            for t in range(TT + 1):
                rows = P if t < TT else NS
                if t >= 2:
                    dve.wait_ge(k_stored[t % 2], 16 * (t // 2))
                for first, count in ((0, 4), (4, HP - 4)):
                    bank = group()
                    nc.vector.tensor_copy(ktok[0:rows, t % 2, first * P:(first + count) * P], bank[0:rows, 0:count * P]).then_inc(tr_free, 1)
                marks["k", t] = tr[0]
            bank = group()
            nc.vector.tensor_copy(ctok[:, 0:TT, :].rearrange("p t h -> p (t h)"), bank[:, 0:TT * NH])
            nc.vector.tensor_copy(ctok[0:NS, TT, :], bank[0:NS, TT * NH:(TT + 1) * NH]).then_inc(tr_free, 1)
            dve.wait_ge(tr_free, tr[0])
            nc.vector.tensor_scalar(ncx[:], ctok[0:NS, TT, :].unsqueeze(2).broadcast_to([NS, NH, NQ]), -1.0, None, ALU.mult)
            nc.vector.tensor_tensor(cqA[:], ctok[0:NS, TT, :].unsqueeze(2).broadcast_to([NS, NH, NQ]),
                                    dq[:].unsqueeze(1).broadcast_to([NS, NH, NQ]), ALU.mult).then_inc(c_done, 1)
            bank = group()
            nc.vector.tensor_scalar(ncT[:], bank, -1.0, None, ALU.mult).then_inc(tr_free, 1)
            bank = group()
            nc.vector.tensor_copy(cqr[:], bank[0:ROWS, 0:NB])
            nc.vector.tensor_copy(mshift[:], bank[0:ROWS, NB:NB + NS - NQ + NS]).then_inc(tr_free, 1)
            marks["forget"] = tr[0]
            for s in range(2):
                dve.wait_ge(k_stored[s], 16 * ((TT + 2 - s) // 2))
            memory(1)
            attend(u, MEM_UNITS, mb1, len(MEM_UNITS))
            sample_memory(1, u + len(MEM_UNITS))
            marks["far"] = tr[0]
            u += len(MEM_UNITS) + GR
            attend(u, FOX_UNITS, mb1, 2 * len(MEM_UNITS))
            marks["prompt attention"] = u + len(FOX_UNITS)

            def sequence(b, first):
                dve.wait_ge(lf_in, 16 * NP * b + 16 * NP)
                if not first:
                    dve.wait_ge(r_ready, b)
                nc.vector.memset(lfa[:, NP - 1], 0.0)
                link(nc.vector.tensor_copy(maskb[:], mshift[:, bass.ds(NS - NQ - NQ * b, NS)]))
                for p in range(NP - 2, -1, -1):
                    step = nc.vector.tensor_tensor(lfa[:, p], lfa[:, p + 1], lfp[:, p + 1], ALU.add)
                    if p:
                        link(step)
                    else:
                        step.then_inc(lfa_done, 1)
                if not first:
                    dve.wait_ge(sn_ready, b)
                for e in range(2):
                    for odd in range(2):
                        r = slice(DH * e, DH * e + DH)
                        col = (2 * odd + e) * NQ
                        nc.vector.tensor_copy(qx[r, :, col:col + NQ].rearrange("p (a o) q -> p a o q", o=2)[:, :, odd, :],
                                              qkT[r, 0:HP, bass.ds(SEQ + NQ * b, NQ)].rearrange("p (a o) q -> p a o q", o=2)[:, :, odd, :])
                nc.vector.tensor_copy(stat[0:ROWS, 56:57], cqr[:, bass.ds(b, 1)]).then_inc(qx_done, 1)
                dve.wait_ge(qx_done, b + 1)
                dve.wait_ge(r_ready, b + 1)
                link(nc.vector.tensor_copy(rtok[:].rearrange("p g h -> p (g h)"), ps[:, 5, 0:NP * NH]))

                def keys_T(c):
                    dve.wait_ge(kt_ready, 3 * (NCH * b + c) + 1)
                    if not first or c >= 2:
                        dve.wait_ge(sc_ready, NCH * b + c - 1)
                    nc.vector.tensor_copy(kT[:, c % 2, 0:2, :].rearrange("p a n -> p (a n)"), ps[:, 0, :]).then_inc(kt_ev_v, 1)
                    r = rtok[:, CPG * c:CPG * c + CPG, :].rearrange("p g h -> p (g h)")
                    nc.vector.tensor_copy(rx[:, c % 2].rearrange("p g h q -> p (g h) q"),
                                          r.unsqueeze(2).broadcast_to([P, CPG * NH, NQ])).then_inc(rx_done, 1)
                keys_T(0)
                if not first:
                    dve.wait_ge(pt_ready, 4 * b)
                for c in range(NCH):
                    if c + 1 < NCH:
                        keys_T(c + 1)
                    dve.wait_ge(sc_ready, NCH * b + c + 1)
                    nc.vector.tensor_scalar(S[:, c * KEYS:(c + 1) * KEYS], ps[0:ROWS, 3 + c % 2, 0:KEYS], stat[0:ROWS, 56:57], None,
                                            ALU.add).then_inc(sc_free, 1)
                dve.wait_ge(sn_ready, b + 1)
                link(nc.vector.scalar_tensor_tensor(out=S[:, NPAST:NPAST + NS], in0=ps[0:ROWS, 5, 0:NS], scalar=stat[0:ROWS, 56:57],
                                                    in1=maskb[:], op0=ALU.add, op1=ALU.add))
                nc.vector.tensor_reduce(stat[0:ROWS, 60:61], S[:], AX_X, ALU.max, negate=True).then_inc(smax_done, 1)
                dve.wait_ge(sexp_done, b + 1)
                link(nc.vector.reciprocal(stat[0:ROWS, 62:63], stat[0:ROWS, 61:62]))
                if not first:
                    dve.wait_ge(o_ready, b)
                for g in range(4):
                    dve.wait_ge(pt_ready, 4 * b + g + 1)
                    n = min(5, NP - 5 * g)
                    last = nc.vector.tensor_copy(pTs[:, 5 * g:5 * g + n, :].rearrange("p k r -> p (k r)"), ps[:, 6 + g % 2, 0:n * ROWS])
                    if g == 3:
                        last = nc.vector.tensor_copy(pTs[0:NS, NP, :], ps[0:NS, 6 + g % 2, n * ROWS:(n + 1) * ROWS])
                    last.then_inc(pt_free, 1)
                dve.wait_ge(o_ready, b + 1)
                nc.vector.tensor_scalar(os_[:], ps[0:ROWS, 5, 0:4 * DH], stat[0:ROWS, 62:63], None, ALU.mult).then_inc(o_done, 1)
                dve.wait_ge(oT_hi, GR * 2 + 1 + b)
                for s in range(2):
                    for e in range(2):
                        r = slice(DH * e, DH * e + DH)
                        to = bass.ds(SEQ + NQ * b, NQ)
                        col = (2 * s + e) * NQ
                        src = ps[r, 6, s * ROWS:(s + 1) * ROWS].rearrange("p (j c) -> p j c", c=QR)[:, :, col:col + NQ]
                        last = nc.vector.tensor_tensor(aL[r, 0:HP, to].rearrange("p (j s) q -> p j s q", s=2)[:, :, s, :], src,
                                                       aH[r, 0:HP, to].rearrange("p (j s) q -> p j s q", s=2)[:, :, s, :].bitcast(F32), ALU.subtract)
                last.then_inc(stage_done, 1)
            sequence(0, True)
            with dve.Fori(0, NB - 1) as i:
                steps.enter(i, NP + 2)
                sequence(i + 1, False)
            steps.leave(NB - 1)
            residual(C_WO1, 1, 3)
            norm(3)
            ffn(1)
            residual(C_DN1, 2, 4)
            for t in range(TT + 1):
                rows = P if t < TT else NS
                if t >= 2:
                    dve.wait_ge(y_stored[t % 2], 16 * (t // 2))
                for q in range(KD // 4):
                    bank = group()
                    nc.vector.tensor_copy(ystage[0:rows, t % 2, 4 * q * P:4 * (q + 1) * P], bank[0:rows, :]).then_inc(tr_free, 1)
                marks["y", t] = tr[0]

        @block.scalar
        def _(act):
            def hi(n0, i=0):
                s, size = n0 % 2, chunk_size(n0)
                act.wait_ge(raw_in[s], 16 * (n0 // 2 + 1) + 16 * i)
                if n0 >= 2:
                    act.wait_ge(w_used, n0 - 1 + 2 * i)
                nc.scalar.activation(wH[s][:, 0:size], raw[:, s, 0:size], ACT.Copy).then_inc(hi_done, 1)

            def square(r, j0, i=0):
                act.wait_ge(x_new, KD * (r - 1) + j0 + 1 + 2 * i)
                if KD * r + j0 >= 2:
                    act.wait_ge(sq_used, KD * r + j0 - 1 + 2 * i)
                x = xT[:, bass.ds(j0 + 2 * i, 1), :].rearrange("p o n -> p (o n)")
                nc.scalar.activation(sq[:, j0 % 2], x, ACT.Square).then_inc(sq_done, 1)

            def norm(r):
                act.wait_ge(sq_used, KD * (r + 1))
                nc.scalar.activation(halves(rb[:]), ps[:, 4:6, 0:HT], ACT.Sqrt, bias=eps[:, 0:1]).then_inc(norm_root, 1)
                for k in range(KD):
                    act.wait_ge(v_done, KD * r + k + 1)
                    nc.scalar.activation(aH[:, k], tmp[:, k % 2], ACT.Copy).then_inc(vH_done, 1)

            def head_tile(z0, i=0):
                chunk = z0 + (2 * KC if z0 < MP else C_FOX - MP)
                act.wait_ge(w_used, chunk + 1 + 2 * i)
                if z0 >= 2:
                    act.wait_ge(hn_done, z0 - 1 + 2 * i)
                nc.scalar.activation(halves(tmp[:, z0 % 2]), acc(z0 % 2), ACT.Copy)
                nc.scalar.activation(halves(sq[:, z0 % 2]), acc(z0 % 2), ACT.Square).then_inc(z_done, 1)

            def head_norm(z0, i=0):
                act.wait_ge(hn_ready, z0 + 1 + 2 * i)
                if z0:
                    act.wait_ge(hn_done, z0 + 2 * i)
                nc.scalar.activation(halves(rb[:]), ps[:, 4:6, 0:HT], ACT.Sqrt, bias=eps[:, 1:2]).then_inc(head_root, 1)

            def memory(l):
                mb = MBS[l]
                act.wait_ge(mem_in, 16 * (l + 1))
                for t in range(MT):
                    nc.scalar.activation(mb["prob"][:].rearrange("p a b n -> p (a b n)")[:, 0:D], mb["mem"][:, t],
                                         ACT.Square, accum_out=stat[:, 32 + t:33 + t]).then_inc(ms_done, 1)
                    act.wait_ge(ms_done, MT * l + t + 1)
                nc.scalar.activation(stat[:, 34:34 + MT], stat[:, 32:32 + MT], ACT.Sqrt, bias=eps[:, 0:1]).then_inc(mem_root, 1)
                for g in range(KD // 2):
                    act.wait_ge(tr_free, marks["memory", l, g])
                    nc.scalar.activation(mb["mH"][:, 2 * g:2 * g + 2, :].rearrange("p k n -> p (k n)"), tmp[:, g % 2, 0:2 * NM],
                                         ACT.Copy).then_inc(mH_done, 1)
                for i in range(N_MEM):
                    hi(C_MEM[l] + 1 + i)
                act.wait_ge(w_used, C_MEM[l] + N_MEM)
                nc.scalar.activation(mb["vm"][:], ps[:, 0:MT, MW:2 * MW], ACT.Copy)
                nc.scalar.activation(sq[:, :, 0:MW], ps[:, 0:MT, 0:MW], ACT.Square).then_inc(kvsq_done, 1)
                act.wait_ge(kss_done, l + 1)
                nc.scalar.activation(stat[:, 44:44 + MT * MH], stat[:, 36:36 + MT * MH], ACT.Sqrt, bias=eps[:, 1:2]).then_inc(k_root, 1)

            def exps(u, unit, mb):
                kind, hp, t, keys = unit
                st = stat[:, 8 * (u % 2):8 * (u % 2) + 8]
                act.wait_ge(at_max, u + 1)
                for e in range(2):
                    src = mb["prob"][:, u % 2, e, 0:keys] if kind == "fox" else ps[:, 2 * (u % 2) + e, 0:keys]
                    last = nc.scalar.activation(mb["prob"][:, u % 2, e, 0:keys], src, ACT.Exp, bias=st[:, e:e + 1],
                                                accum_out=st[:, 2 + e:3 + e])
                last.then_inc(at_exp, 1)

            def attend(u0, units, mb):
                exps(u0, units[0], mb)
                for i, (kind, hp, t, keys) in enumerate(units):
                    u = u0 + i
                    if i + 1 < len(units):
                        exps(u + 1, units[i + 1], mb)
                    tile = hp if kind == "fox" else KC + hp
                    act.wait_ge(at_pv, u + 1)
                    nc.scalar.activation(aH[:, tile, t * P:(t + 1) * P], ps[:, 4 + u % 2, 0:P], ACT.Copy).then_inc(at_hi, 1)

            def sample_memory(l, u0):
                mb = MBS[l]
                for G in range(GR):
                    u = u0 + G
                    st = stat[:, 8 * (u % 2):8 * (u % 2) + 8]
                    act.wait_ge(at_max, u + 1)
                    nc.scalar.activation(mb["prob"][:, u % 2, 0, 0:NM], ps[:, 2 * (u % 2), 0:NM], ACT.Exp, bias=st[:, 0:1],
                                         accum_out=st[:, 2:3]).then_inc(at_exp, 1)
                    g = marks["sample memory", l, G]
                    act.wait_ge(tr_ready, g + 1)
                    bank = ps[:, 6 + g % 2, :]
                    for s in range(MP):
                        for e in range(2):
                            r = slice(DH * e, DH * e + DH)
                            src = bank[r, s * P:(s + 1) * P].rearrange("p (b h q) -> p b h q", b=GS, h=MH)[:, :, 2 * s + e, :]
                            to = slice(SEQ + G * GS * NQ, SEQ + (G + 1) * GS * NQ)
                            last = nc.scalar.activation(aH[r, KC + s, to].rearrange("p (b q) -> p b q", b=GS), src, ACT.Copy)
                    last.then_inc(oT_hi, 1)

            def residual(c0, per_tile, r):
                def tile(j0, i):
                    for s in range(per_tile):
                        n0 = c0 + per_tile * j0 + s + 1
                        if n0 < C_END:
                            hi(n0, i if per_tile == 1 else 2 * i)
                    if r < 4:
                        square(r, j0, i)
                with act.Fori(0, KD // 2 - 1) as i:
                    for j in range(2):
                        tile(j, i)
                for j in range(KD - 2, KD):
                    tile(j, 0)

            def ffn(l):
                c0, g0 = C_GU[l], l * KF

                def tile(f0, i):
                    hi(c0 + 2 * f0 + 1, 2 * i)
                    hi(c0 + 2 * f0 + 2, 2 * i)
                    if g0 + f0 >= 2:
                        act.wait_ge(g_done, g0 + f0 - 1 + 2 * i)
                    nc.scalar.activation(halves(sq[:, f0 % 2]), acc(2 * (f0 % 2)), ACT.Silu).then_inc(silu_done, 1)
                    act.wait_ge(g_done, g0 + f0 + 1 + 2 * i)
                    f = bass.ds(f0 + 2 * i, 1)
                    nc.scalar.activation(gH[:, f, :].rearrange("p o n -> p (o n)"), tmp[:, f0 % 2], ACT.Copy).then_inc(gH_done, 1)
                for f in range(2):
                    tile(f, 0)
                with act.Fori(0, KF2 - 2) as i:
                    for f in range(2, 4):
                        tile(f, i)
                for f in range(KF - 2, KF):
                    tile(f, 0)

            xp = x_prompt[0].rearrange("(t p) n -> p t n", p=P)
            for t in range(TT):
                act.dma_start(xin[:, t], xp[:, t]).then_inc(x_in, 16)
            act.dma_start(xin[0:NS, TT], x_sample.rearrange("b q n -> (b q) n")).then_inc(x_in, 16)
            loads = 0
            for at_row, v in ((V_N1, norm1), (V_N2, norm2), (V_MEM, mem_norm), (V_DWB, conv_dw_b), (V_LNG, conv_ln_g), (V_LNB, conv_ln_b)):
                rows = v.rearrange("l (k n) -> (l k) n", n=P)
                act.dma_start(vrow[at_row:at_row + rows.shape[0], :], rows).then_inc(vec_in, 16)
                loads += 1
            for row, v in ((V_MQ, mem_q_norm[0:1]), (V_MQ + 1, mem_q_norm[1:2]), (V_MQ + 2, fox_q_norm), (V_MQ + 3, fox_k_norm)):
                for e in range(2):
                    act.dma_start(vrow[row:row + 1, DH * e:DH * e + DH], v).then_inc(vec_in, 16)
                    loads += 1
            act.dma_start(dwrow[:], conv_dw[0]).then_inc(vec_in, 16)
            for l in range(2):
                act.dma_start(gk_row[:, l, :], mem_k_norm[l:l + 1, :].broadcast_to([P, DH])).then_inc(vec_in, 16)
            act.dma_start(bf[:], fox_b_f.rearrange("o h -> h o")).then_inc(vec_in, 16)
            assert loads + 4 == VEC_LOADS
            for G in range(GR):
                act.dma_start(crow[:, G, :], cache_conv[0, G * GS:(G + 1) * GS].rearrange("b n c -> (b n) c")).then_inc(hist_in, 16)

            act.wait_ge(consts, CONSTS0)
            hi(0)
            for j in range(KD):
                act.wait_ge(tr_free, 2 * (TT + 1))
                if j >= 2:
                    act.wait_ge(sq_used, j - 1)
                nc.scalar.activation(sq[:, j % 2], xT[:, j], ACT.Square).then_inc(sq_done, 1)
            norm(0)

            def gate(c0, i):
                hi(C_CONV + 2 * c0 + 1, 2 * i)
                hi(C_CONV + 2 * c0 + 2, 2 * i)
                act.wait_ge(w_used, 2 * c0 + 2 + 4 * i)
                if c0 >= 2:
                    act.wait_ge(u_done, c0 - 1 + 2 * i)
                nc.scalar.activation(halves(sq[:, c0 % 2]), acc(2 * (c0 % 2) + 1), ACT.Sigmoid).then_inc(sig_done, 1)
            for c in range(2):
                gate(c, 0)
            with act.Fori(0, KC // 2 - 1) as i:
                for c in range(2, 4):
                    gate(c, i)
            for z in range(MP):
                hi(C_CONV + 2 * KC + z + 1)
                if z == 0:
                    act.wait_ge(u_done, KC)
                head_tile(z)
                if z:
                    head_norm(z - 1)
            head_norm(MP - 1)
            for c in range(KC):
                last = nc.scalar.activation(usc[:, c], uS[:, c, :, NQ:NQ + H], ACT.Copy)
            last.then_inc(usc_done, 1)
            memory(0)
            attend(0, MEM_UNITS, mb0)
            sample_memory(0, len(MEM_UNITS))
            for c in range(KC):
                act.wait_ge(lny_done, c + 1)
                if c >= 2:
                    act.wait_ge(ysq_used, c - 1)
                nc.scalar.activation(sq[:, c % 2], yc[:, c], ACT.Square).then_inc(ysq_done, 1)
            act.wait_ge(ln_ready, 2)
            nc.scalar.activation(halves(rb[:]), ps[:, 2:4, 0:HT], ACT.Sqrt, bias=eps[:, 2:3], scale=1.0 / CH).then_inc(ln_root, 1)
            for c in range(KC):
                act.wait_ge(lny_done, KC + c + 1)
                nc.scalar.activation(yc[:, c], yc[:, c], ACT.Silu, bias=vec[:, V_LNB + c:V_LNB + c + 1]).then_inc(swish_done, 1)
                act.wait_ge(swish_done, c + 1)
                nc.scalar.activation(aH[:, c], yc[:, c], ACT.Copy).then_inc(mixf_done, 1)
            residual(C_WO0, 1, 1)
            norm(1)
            ffn(0)
            residual(C_DN0, 2, 2)
            norm(2)

            Z = MP
            hi(C_FOX + 1)
            act.wait_ge(w_used, C_FOX + 1)
            nc.scalar.activation(tmp[0:NH, Z % 2, :].rearrange("p (a n) -> p a n", a=2), acc(Z % 2)[0:NH], ACT.Identity,
                                 bias=bf[:, 0:1]).then_inc(z_done, 1)
            hi(C_FOX + 2)
            head_tile(Z + 1)
            act.wait_ge(zab_done, 1)
            nc.scalar.activation(work[:, 1], work[:, 1], ACT.Exp, scale=-1.0).then_inc(e_done, 1)

            def head_pass(z0, i=0):
                hi(z0 - Z + C_FOX + 1, i)
                head_tile(z0, i)
                head_norm(z0 - 1, i)
            with act.Fori(0, HP) as i:
                for z in range(2):
                    head_pass(Z + 2 + z, i)
            for n in range(2 * HP + 2, N_FOX):
                if n - 1 <= 3 * HP:
                    hi(C_FOX + n + 1)
                    head_tile(Z + n)
                else:
                    head_pass(Z + n)
            head_norm(Z + N_FOX - 1)
            memory(1)
            u = len(MEM_UNITS) + GR
            attend(u, MEM_UNITS, mb1)
            sample_memory(1, u + len(MEM_UNITS))
            u += len(MEM_UNITS) + GR
            attend(u, FOX_UNITS, mb1)

            def sequence(b, first):
                for c in range(NCH):
                    for g in (1, 2):
                        act.wait_ge(kt_ready, 3 * (NCH * b + c) + g + 1)
                        if g == 1 and (not first or c >= 2):
                            act.wait_ge(sc_ready, NCH * b + c - 1)
                        nc.scalar.activation(kT[:, c % 2, 2 * g:2 * g + 2, :].rearrange("p a n -> p (a n)"), ps[:, g, :],
                                             ACT.Copy).then_inc(kt_ev_a, 1)
                act.wait_ge(smax_done, b + 1)
                nc.scalar.activation(S[:], S[:], ACT.Exp, bias=stat[0:ROWS, 60:61],
                                     accum_out=stat[0:ROWS, 61:62]).then_inc(sexp_done, 1)
                act.wait_ge(oT_ready, b + 1)
                for s in range(2):
                    for e in range(2):
                        r = slice(DH * e, DH * e + DH)
                        to = bass.ds(SEQ + NQ * b, NQ)
                        col = (2 * s + e) * NQ
                        src = ps[r, 6, s * ROWS:(s + 1) * ROWS].rearrange("p (j c) -> p j c", c=QR)[:, :, col:col + NQ]
                        last = nc.scalar.activation(aH[r, 0:HP, to].rearrange("p (j s) q -> p j s q", s=2)[:, :, s, :], src, ACT.Copy)
                last.then_inc(oT_hi, 1)
            sequence(0, True)
            with act.Fori(0, NB - 1) as i:
                sequence(i + 1, False)
            residual(C_WO1, 1, 3)
            norm(3)
            ffn(1)
            residual(C_DN1, 2, 4)

        @block.tensor
        def _(pe):
            tr = [0]

            def transposes(jobs):
                g = tr[0]
                tr[0] += 1
                if g >= 2:
                    pe.wait_ge(tr_free, g - 1)
                col = 0
                for src in jobs:
                    n, m = src.shape[0], 1
                    for x in src.shape[1:]:
                        m *= x
                    last = nc.tensor.transpose(ps[0:m, 6 + g % 2, col:col + n], src, ident[0:n, 0:n])
                    col += n
                last.then_inc(tr_ready, 1)
                return g

            def product(n0, i, slot, H_, L_, k0, ks, first, last):
                s = n0 % 2
                pe.wait_ge(lo_done, n0 + 1 + 2 * i)
                for k in range(ks):
                    w = slice(k * P, (k + 1) * P)
                    for weights, acts in ((wH[s], (H_, L_)), (wL[s], (H_,))):
                        for a in acts:
                            for h in range(2):
                                mm = nc.tensor.matmul(ps[:, 2 * slot + h, 0:HT], weights[:, w], a[:, k0 + k, h * HT:(h + 1) * HT],
                                                      start=(first and k == 0 and weights is wH[s] and a is H_),
                                                      stop=(last and k == ks - 1 and weights is wL[s]))
                mm.then_inc(w_used, 1)

            def sum_squares(r, j0, i=0):
                pe.wait_ge(sq_done, KD * r + j0 + 1 + 2 * i)
                for h in range(2):
                    mm = nc.tensor.matmul(ps[:, 4 + h, 0:HT], ones[:], sq[:, j0 % 2, h * HT:(h + 1) * HT],
                                          start=(j0 == 0), stop=(i is None or j0 == KD - 1), skip_group_check=True)
                mm.then_inc(sq_used, 1)

            def residual(c0, per_tile, r, k0s):
                def tile(j0, i=0):
                    if j0 >= 2:
                        pe.wait_ge(x_new, KD * (r - 1) + j0 - 1 + 2 * i)
                    H_, L_ = (aH, aL) if per_tile == 1 else (gH, gL)
                    for s in range(per_tile):
                        product(c0 + per_tile * j0 + s, i if per_tile == 1 else 2 * i, j0 % 2, H_, L_, k0s[s],
                                KD if per_tile == 1 else KF2, s == 0, s == per_tile - 1)
                tile(0)
                tile(1)
                if r < 4:
                    sum_squares(r, 0)
                with pe.Fori(0, KD // 2 - 1) as i:
                    for j in range(2, 4):
                        tile(j, i)
                        if r < 4:
                            sum_squares(r, j - 1, i)
                if r < 4:
                    sum_squares(r, KD - 1)

            def ffn(l):
                c0, g0 = C_GU[l], l * KF
                pe.wait_ge(a_ready, KD * (2 * l + 2))

                def tile(f0, i=0):
                    if g0 + f0 >= 2:
                        pe.wait_ge(g_done, g0 + f0 - 1 + 2 * i)
                    for s in range(2):
                        product(c0 + 2 * f0 + s, 2 * i, 2 * (f0 % 2) + s, aH, aL, 0, KD, True, True)
                for f in range(2):
                    tile(f)
                with pe.Fori(0, KF2 - 1) as i:
                    for f in range(2, 4):
                        tile(f, i)
                pe.wait_ge(gL_done, KF * (l + 1))

            def head_sums(z0, i=0):
                pe.wait_ge(z_done, z0 + 1 + 2 * i)
                if z0:
                    pe.wait_ge(hn_done, z0 + 2 * i)
                for h in range(2):
                    mm = nc.tensor.matmul(ps[:, 4 + h, 0:HT], blocks[:], sq[:, z0 % 2, h * HT:(h + 1) * HT], start=True, stop=True)
                mm.then_inc(hn_ready, 1)

            def memory(l):
                mb = MBS[l]
                pe.wait_ge(mn_done, l + 1)
                for g in range(KD // 2):
                    transposes([mb["mem"][:, t, k * P:(k + 1) * P] for k in (2 * g, 2 * g + 1) for t in range(MT)])
                for i in range(N_MEM):
                    n = C_MEM[l] + i
                    pe.wait_ge(lo_done, n + 1)
                    pe.wait_ge(mL_done, l * KD // 2 + (KM * i + KM - 1) // 2 + 1)
                    for kk in range(KM):
                        k = KM * i + kk
                        w = slice(kk * 2 * MW, (kk + 1) * 2 * MW)
                        for t in range(MT):
                            for m_, w_ in ((mb["mH"], wH), (mb["mH"], wL), (mb["mL"], wH)):
                                mm = nc.tensor.matmul(ps[:, t, :], m_[:, k, t * P:(t + 1) * P], w_[n % 2][:, w],
                                                      start=(k == 0 and m_ is mb["mH"] and w_ is wH),
                                                      stop=(k == KD - 1 and m_ is mb["mL"]))
                    mm.then_inc(w_used, 1)
                pe.wait_ge(kv_done, l + 1)
                transposes([mb["km"][:, t, hp * P:(hp + 1) * P] for hp in range(MP) for t in range(MT)])

            def scores(u, unit, mb):
                kind, hp, t, keys = unit
                if u >= 2:
                    pe.wait_ge(at_exp, u - 1)
                for e in range(2):
                    r = slice(DH * e, DH * e + DH)
                    q = qkT[r, hp, t * P:(t + 1) * P] if kind == "fox" else mb["qm"][r, hp, t * P:(t + 1) * P]
                    k = qkT[r, HP + hp, 0:keys] if kind == "fox" else mb["kmT"][r, hp, :]
                    out = ps[:, 2 * (u % 2) + e, 0:keys]
                    mm = nc.tensor.matmul(out, q, k, start=True, stop=(kind == "mem"))
                    if kind == "fox":
                        h = DH * e + 2 * hp + e
                        mm = nc.tensor.matmul(out, ident[r, h:h + 1].broadcast_to([DH, P]), ncT[r, 0:keys], start=False, stop=True)
                mm.then_inc(at_s, 1)

            def attend(u0, units, mb):
                scores(u0, units[0], mb)
                for i, (kind, hp, t, keys) in enumerate(units):
                    u = u0 + i
                    if i + 1 < len(units):
                        scores(u + 1, units[i + 1], mb)
                    pe.wait_ge(at_prob, u + 1)
                    if kind == "mem":
                        transposes([mb["prob"][:, u % 2, e, k * P:(k + 1) * P] for e in range(2) for k in range(MT)])
                    else:
                        for e in range(2):
                            transposes([mb["prob"][:, u % 2, e, k * P:(k + 1) * P] for k in range(t + 1)])
                    pe.wait_ge(tr_free, tr[0])
                    if u >= 2:
                        pe.wait_ge(at_lo, u - 1)
                    n = keys // P
                    for e in range(2):
                        head = slice((2 * hp + e) * DH, (2 * hp + e + 1) * DH)
                        for k in range(n):
                            v = vtok[:, k, head] if kind == "fox" else mb["vm"][:, k, head]
                            mm = nc.tensor.matmul(ps[DH * e:DH * e + DH, 4 + u % 2, 0:P], v, mb["pT"][:, e, k, :],
                                                  start=(k == 0), stop=(k == n - 1))
                    mm.then_inc(at_pv, 1)

            def sample_memory(l, u0):
                mb = MBS[l]
                for G in range(GR):
                    u = u0 + G
                    pe.wait_ge(ks_in, 32 * (GR * l + G + 1))
                    for b in range(GS):
                        transposes([mb["ks"][:, b, k, hp * P:(hp + 1) * P] for hp in range(MP) for k in range(MT)])
                    pe.wait_ge(qd_done, GR * l + G + 1)
                    pe.wait_ge(tr_free, tr[0])
                    pe.wait_ge(at_exp, u - 1)
                    for hp in range(MP):
                        for b in range(GS):
                            mm = nc.tensor.matmul(ps[QR * b:QR * b + QR, 2 * (u % 2), 0:NM], mb["qd"][:, b, hp, :], mb["ksT"][:, b, hp, :],
                                                  start=(hp == 0), stop=(hp == MP - 1), skip_group_check=True, tile_position=(0, QR * b))
                    mm.then_inc(at_s, 1)
                    pe.wait_ge(at_prob, u + 1)
                    transposes([mb["prob"][:, u % 2, 0, k * P:(k + 1) * P] for k in range(MT)])
                    pe.wait_ge(tr_free, tr[0])
                    pe.wait_ge(at_lo, u - 1)
                    for k in range(MT):
                        for b in range(GS):
                            mm = nc.tensor.matmul(ps[QR * b:QR * b + QR, 4 + u % 2, 0:MW], mb["pT"][:, 0, k, QR * b:QR * b + QR],
                                                  mb["vs"][:, b, k, :], start=(k == 0), stop=(k == MT - 1), skip_group_check=True,
                                                  tile_position=(0, QR * b))
                    mm.then_inc(at_pv, 1)
                    pe.wait_ge(at_lo, u + 1)
                    transposes([mb["o"][:, s * P:(s + 1) * P] for s in range(MP)])

            pe.wait_ge(consts, CONSTS0)
            pe.wait_ge(x_in, 16 * (TT + 1))
            for t in range(TT + 1):
                rows = P if t < TT else NS
                for q in range(KD // 4):
                    transposes([xin[0:rows, t, k * P:(k + 1) * P] for k in range(4 * q, 4 * q + 4)])
            for j in range(KD):
                sum_squares(0, j)
            pe.wait_ge(vec_in, 16 * VEC_LOADS)
            transposes([vrow[:]])
            transposes([dwrow[:, c * P:(c + 1) * P] for c in range(KC)])
            pe.wait_ge(hist_in, 16 * GR)
            for G in range(GR):
                for first, count in ((0, 4), (4, KC - 4)):
                    transposes([crow[:, G, c * P:(c + 1) * P] for c in range(first, first + count)])

            pe.wait_ge(a_ready, KD)
            pe.wait_ge(tr_free, tr[0])

            def conv_tile(c0, i=0):
                if c0 >= 2:
                    pe.wait_ge(u_done, c0 - 1 + 2 * i)
                for s in range(2):
                    product(C_CONV + 2 * c0 + s, 2 * i, 2 * (c0 % 2) + s, aH, aL, 0, KD, True, True)
            for c in range(2):
                conv_tile(c)
            with pe.Fori(0, KC // 2 - 1) as i:
                for c in range(2, 4):
                    conv_tile(c, i)
            pe.wait_ge(u_done, KC)
            for z in range(MP):
                product(C_CONV + 2 * KC + z, 0, z % 2, aH, aL, 0, KD, True, True)
                if z:
                    head_sums(z - 1)
            head_sums(MP - 1)
            for first, count in ((0, 4), (4, KC - 4)):
                transposes([uP[:, c, SEQ:SEQ + H] for c in range(first, first + count)])
            pe.wait_ge(usc_done, 1)
            for G in range(GR):
                for first, count in ((0, 4), (4, KC - 4)):
                    transposes([usc[:, c, G * GS:(G + 1) * GS, :].rearrange("p b n -> p (b n)") for c in range(first, first + count)])
            pe.wait_ge(z_done, MP)
            memory(0)
            pe.wait_ge(hn_done, MP)
            pe.wait_ge(tr_free, tr[0])
            attend(0, MEM_UNITS, mb0)
            sample_memory(0, len(MEM_UNITS))
            pe.wait_ge(y_done, KC)
            pe.wait_ge(at_exp, len(MEM_UNITS) + GR)
            for source, bank in ((yc, 0), (sq, 2)):
                for c in range(KC):
                    if bank:
                        pe.wait_ge(ysq_done, c + 1)
                    src = yc[:, c] if not bank else sq[:, c % 2]
                    for h in range(2):
                        mm = nc.tensor.matmul(ps[:, bank + h, 0:HT], ones[:], src[:, h * HT:(h + 1) * HT], start=(c == 0), stop=(c == KC - 1))
                    if bank and c < KC - 1:
                        mm.then_inc(ysq_used, 1)
                mm.then_inc(ln_ready, 1)
            pe.wait_ge(stage_done, KC)
            pe.wait_ge(tr_free, tr[0])
            residual(C_WO0, 1, 1, (0,))
            ffn(0)
            residual(C_DN0, 2, 2, (0, KF2))

            Z = MP
            pe.wait_ge(a_ready, KD * 3)

            def tile(z0, i=0):
                pe.wait_ge(z_done, z0 - 1 + 2 * i)
                product(C_FOX - Z + z0, i, z0 % 2, aH, aL, 0, KD, True, True)
            tile(Z)
            tile(Z + 1)
            pe.wait_ge(z_done, Z + 1)
            pe.wait_ge(hn_done, Z)
            for t in range(TT + 1):
                n = P if t < TT else NS
                mm = nc.tensor.transpose(ps[0:n, 4, t * NH:(t + 1) * NH], tmp[0:NH, Z % 2, t * P:t * P + n], ident[0:NH, 0:NH])
            mm.then_inc(hn_ready, 1)
            with pe.Fori(0, HP - 1) as i:
                for n in range(2, 4):
                    tile(Z + n, i)
                    head_sums(Z + n - 1, i)
            tile(Z + 2 * HP)
            head_sums(Z + 2 * HP - 1)
            for n in range(2 * HP + 1, N_FOX + 1):
                if n < N_FOX:
                    tile(Z + n)
                z = Z + n - 1
                if n - 1 in range(2 * HP + 1, 3 * HP + 1):
                    pe.wait_ge(z_done, z + 1)
                    pe.wait_ge(hn_done, z)
                    for t in range(TT + 1):
                        m = P if t < TT else NS
                        mm = nc.tensor.transpose(ps[0:m, 4 + t // TT, (t % TT) * P:(t % TT + 1) * P],
                                                 tmp[:, z % 2, t * P:t * P + m], ident[:])
                    mm.then_inc(hn_ready, 1)
                else:
                    head_sums(z)
            pe.wait_ge(hn_done, Z + N_FOX)
            for t in range(TT + 1):
                n = P if t < TT else NS
                for first, count in ((0, 4), (4, HP - 4)):
                    transposes([qkT[:, HP + hp, t * P:t * P + n] for hp in range(first, first + count)])
            pe.wait_ge(c_ready, 1)
            pe.wait_ge(tr_free, tr[0] - 1)
            out = ps[:, 6 + tr[0] % 2, :]
            tr[0] += 1
            for t in range(TT):
                for s in range(t + 1):
                    mm = nc.tensor.matmul(out[:, t * NH:(t + 1) * NH], win[:, (TT - 1 - s + t) * P:(TT - s + t) * P], lf[:, s, :],
                                          start=(s == 0), stop=(s == t))
            nc.tensor.matmul(out[0:NS, TT * NH:(TT + 1) * NH], sameq[:], lf[0:NS, TT, :], start=True, stop=True).then_inc(tr_ready, 1)
            pe.wait_ge(tr_free, tr[0] - 1)
            out = ps[:, 6 + tr[0] % 2, :]
            tr[0] += 1
            for s in range(TT):
                mm = nc.tensor.matmul(out, lfd[:, s, :], win[:, (TT - 1 - s) * P:(TT - 1 - s) * P + SEQ], start=(s == 0), stop=(s == TT - 1))
            mm.then_inc(tr_ready, 1)
            pe.wait_ge(c_done, 1)
            pe.wait_ge(tr_free, tr[0] - 1)
            out = ps[:, 6 + tr[0] % 2, :]
            tr[0] += 1
            nc.tensor.matmul(out[0:ROWS, 0:NB], cqA[:].rearrange("p h q -> p (h q)"), bm[:], start=True, stop=True)
            nc.tensor.transpose(out[0:ROWS, NB:NB + 2 * NS - NQ], mshT[:], ident[0:2 * NS - NQ, 0:2 * NS - NQ]).then_inc(tr_ready, 1)
            memory(1)
            pe.wait_ge(tr_free, tr[0])
            u = len(MEM_UNITS) + GR
            attend(u, MEM_UNITS, mb1)
            sample_memory(1, u + len(MEM_UNITS))
            u += len(MEM_UNITS) + GR
            attend(u, FOX_UNITS, mb1)
            pe.wait_ge(at_lo, u + len(FOX_UNITS))
            pe.wait_ge(tr_free, tr[0])

            def sequence(b, first):
                pe.wait_ge(lfa_done, b + 1)
                if not first:
                    pe.wait_ge(o_done, b)
                nc.tensor.matmul(ps[:, 5, 0:NP * NH], after[:], lfp[:].rearrange("p g h -> p (g h)"), start=True, stop=False)
                nc.tensor.matmul(ps[:, 5, 0:NP * NH], ones[:], lfa[:].rearrange("p g h -> p (g h)"), start=False,
                                 stop=True).then_inc(r_ready, 1)

                def keys_T(c):
                    pe.wait_ge(k_in[c % 2], 32 * (NCH // 2 * b + c // 2 + 1))
                    if not first or c:
                        pe.wait_ge(kt_ev_v, NCH * b + c)
                        pe.wait_ge(kt_ev_a, 2 * (NCH * b + c))
                    for g in range(3):
                        for n in range(4):
                            hp, pp = (4 * g + n) // 2, n % 2
                            mm = nc.tensor.transpose(ps[:, g, n * P:(n + 1) * P], kring[:, c % 2, pp, hp * P:(hp + 1) * P], ident[:])
                        mm.then_inc(kt_ready, 1)
                keys_T(0)
                pe.wait_ge(qx_done, b + 1)
                for c in range(NCH):
                    if c + 1 < NCH:
                        keys_T(c + 1)
                    pe.wait_ge(kt_ev_v, NCH * b + c + 1)
                    pe.wait_ge(kt_ev_a, 2 * (NCH * b + c + 1))
                    pe.wait_ge(rx_done, NCH * b + c + 1)
                    if c >= 2:
                        pe.wait_ge(sc_free, NCH * b + c - 1)
                    for odd in range(2):
                        for j in range(3):
                            mm = nc.tensor.matmul(ps[QR * j:QR * j + QR, 3 + c % 2, 0:KEYS], qx[:, 2 * j + odd, :], kT[:, c % 2, 2 * j + odd, :],
                                                  start=(odd == 0), stop=False, skip_group_check=True, tile_position=(0, QR * j))
                    for pp in range(CPG):
                        for j in range(3):
                            r = rx[:, c % 2, pp, 4 * j:4 * j + 4, :].rearrange("p h q -> p (h q)")
                            mm = nc.tensor.matmul(ps[QR * j:QR * j + QR, 3 + c % 2, pp * P:(pp + 1) * P], r, ident[:],
                                                  start=False, stop=(pp == CPG - 1), skip_group_check=True, tile_position=(0, QR * j))
                    mm.then_inc(sc_ready, 1)
                for odd in range(2):
                    for j in range(3):
                        nc.tensor.matmul(ps[QR * j:QR * j + QR, 5, 0:NS], qx[:, 2 * j + odd, :], qkT[:, HP + 2 * j + odd, SEQ:T],
                                         start=(odd == 0), stop=False, skip_group_check=True, tile_position=(0, QR * j))
                for j in range(3):
                    c_k = ncx[:, 4 * j:4 * j + 4, :].rearrange("p h q -> p (h q)")
                    mm = nc.tensor.matmul(ps[QR * j:QR * j + QR, 5, 0:NS], c_k, ident[0:NS, 0:NS], start=False, stop=True,
                                          skip_group_check=True, tile_position=(0, QR * j))
                mm.then_inc(sn_ready, 1)
                pe.wait_ge(sexp_done, b + 1)
                for g in range(4):
                    if g >= 2:
                        pe.wait_ge(pt_free, 4 * b + g - 1)
                    elif g == 0:
                        pe.wait_ge(stage_done, KC + b)
                    n = min(5, NP - 5 * g)
                    for x in range(n):
                        k = 5 * g + x
                        mm = nc.tensor.transpose(ps[:, 6 + g % 2, x * ROWS:(x + 1) * ROWS], S[:, k * P:(k + 1) * P], ident[0:ROWS, 0:ROWS])
                    if g == 3:
                        mm = nc.tensor.transpose(ps[0:NS, 6 + g % 2, n * ROWS:(n + 1) * ROWS], S[:, NPAST:NPAST + NS], ident[0:ROWS, 0:ROWS])
                    mm.then_inc(pt_ready, 1)
                for c in range(NCH):
                    pe.wait_ge(v_in[c % 2], 32 * (NCH // 2 * b + c // 2 + 1))
                    pe.wait_ge(pt_free, 4 * b + (CPG * c + CPG - 1) // 5 + 1)
                    for pp in range(CPG):
                        for j in range(3):
                            k = CPG * c + pp
                            mm = nc.tensor.matmul(ps[QR * j:QR * j + QR, 5, 0:4 * DH], pTs[:, k, QR * j:QR * j + QR],
                                                  vring[:, c % 2, pp, 4 * DH * j:4 * DH * (j + 1)], start=(k == 0), stop=False,
                                                  skip_group_check=True, tile_position=(0, QR * j))
                    mm.then_inc(v_used, 1)
                for j in range(3):
                    mm = nc.tensor.matmul(ps[QR * j:QR * j + QR, 5, 0:4 * DH], pTs[0:NS, NP, QR * j:QR * j + QR],
                                          vtok[0:NS, TT, 4 * DH * j:4 * DH * (j + 1)], start=False, stop=True,
                                          skip_group_check=True, tile_position=(0, QR * j))
                mm.then_inc(o_ready, 1)
                pe.wait_ge(o_done, b + 1)
                for s in range(2):
                    mm = nc.tensor.transpose(ps[:, 6, s * ROWS:(s + 1) * ROWS], os_[:, s * P:(s + 1) * P], ident[0:ROWS, 0:ROWS])
                mm.then_inc(oT_ready, 1)
            sequence(0, True)
            with pe.Fori(0, NB - 1) as i:
                sequence(i + 1, False)
            pe.wait_ge(stage_done, KC + NB)
            residual(C_WO1, 1, 3, (0,))
            ffn(1)
            residual(C_DN1, 2, 4, (0, KF2))
            pe.wait_ge(x_new, KD * 4)
            for t in range(TT + 1):
                n = P if t < TT else NS
                for q in range(KD // 4):
                    transposes([xT[:, k, t * P:t * P + n] for k in range(4 * q, 4 * q + 4)])

        @block.sync
        def _(sp):
            def load(n0, src, i=0):
                s = n0 % 2
                if n0 >= 2:
                    sp.wait_ge(lo_done, n0 - 1 + 2 * i)
                size = src.shape[1] * src.shape[2]
                sp.dma_start(raw[:, s, 0:size].rearrange("p (k n) -> p k n", k=src.shape[1]), src).then_inc(raw_in[s], 16)

            def mem_chunks(l):
                for i in range(N_MEM):
                    load(C_MEM[l] + i, w_mem_kv[l].rearrange("(k p) n -> p k n", p=P)[:, KM * i:KM * i + KM, :])

            def out_chunks(l):
                with sp.Fori(0, KD // 2) as i:
                    for j in range(2):
                        load(C_WO[l] + j, columns(w_out[l], j * P + 2 * P * i), i)

            def ffn_chunks(l):
                with sp.Fori(0, KF) as f:
                    load(C_GU[l], columns(w_gate_up[l], P * f), f)
                    load(C_GU[l] + 1, columns(w_gate_up[l], DF + P * f), f)
                with sp.Fori(0, KD) as j:
                    for s in range(2):
                        load(C_DN[l] + s, columns(w_down[l], P * j, s * KF2, KF2), j)

            def conv_pair(c0, i):
                load(C_CONV + 2 * c0, columns(conv_w_in[0], c0 * P + P * i), i)
                load(C_CONV + 2 * c0 + 1, columns(conv_w_in[0], CH + c0 * P + P * i), i)
            conv_pair(0, 0)
            with sp.Fori(0, KC - 1) as i:
                conv_pair(1, i)
            for z in range(MP):
                load(C_CONV + 2 * KC + z, columns(conv_w_in[0], 2 * CH + z * P))
            mem_chunks(0)
            out_chunks(0)
            ffn_chunks(0)
            w = fox_w_in[0]
            load(C_FOX, columns(w, 3 * CH))
            with sp.Fori(0, 3 * HP // 2) as i:
                for j in range(2):
                    load(C_FOX + 1 + j, columns(w, j * P + 2 * P * i), i)
            for z in range(MP):
                load(C_FOX + 1 + 3 * HP + z, columns(w, 3 * CH + NH + z * P))
            mem_chunks(1)
            load(C_WO1, columns(w_out[1], 0))
            load(C_WO1 + 1, columns(w_out[1], P))
            sp.dma_start(pages[:], page_table.rearrange("b n -> (b n)").unsqueeze(0)).then_inc(pages_in, 16)
            sp.wait_ge(pages_in, 16)
            sp.wait_ge(tr_free, marks["far"])

            def page(p):
                return sp.value_load(pages[0:1, bass.ds(p, 1)], min_val=0, max_val=N_PHYS - 1)

            def keys(c, first, read=None):
                which = [page(first + CPG * c + pp) for pp in range(CPG)]
                if read is not None:
                    sp.wait_ge(kt_ready, read)
                for pp in range(CPG):
                    sp.dma_start(kring[:, c % 2, pp, :], cache_fox_k[0, bass.ds(which[pp], 1)].rearrange("o p h d -> (o p) (h d)"))\
                      .then_inc(k_in[c % 2], 16)

            def forgets(first, read=None):
                which = page(first)
                if read is not None:
                    sp.wait_ge(r_ready, read)
                for p in range(NP):
                    sp.dma_start(lfp[:, p, :], cache_fox_logf[0, bass.ds(which, 1)].rearrange("o p h -> (o p) h")).then_inc(lf_in, 16)
                    if p + 1 < NP:
                        which = page(first + p + 1)
            forgets(0)
            keys(0, 0)
            keys(1, 0)
            with sp.Fori(0, NB - 1) as b:
                for c in range(NCH):
                    keys(c + 2, NP * b, 3 * NCH * b + 3 * (c + 1))
                    if c == 1:
                        forgets(NP * b + NP, b + 1)
            for c in range(NCH - 2):
                keys(c + 2, NP * (NB - 1), 3 * NCH * (NB - 1) + 3 * (c + 1))
            with sp.Fori(0, KD // 2 - 1) as i:
                for j in range(2, 4):
                    load(C_WO1 + j, columns(w_out[1], j * P + 2 * P * i), i)
            ffn_chunks(1)

        @block.gpsimd
        def _(pool):
            count = [0, 0]

            def step(instruction, semaphore=None, which=0):
                instruction.then_inc((consts, consts1)[which], 1)
                count[which] += 1
                pool.wait_ge((consts, consts1)[which], count[which])

            for n, value in enumerate((D * EPS, DH * EPS, EPS)):
                step(nc.gpsimd.memset(eps[:, n:n + 1], value))
            step(nc.gpsimd.memset(ones[:], 1.0))
            step(nc.gpsimd.memset(blocks[:], 0.0))
            step(nc.gpsimd.memset(blocks[0:DH, 0:DH], 1.0))
            step(nc.gpsimd.memset(blocks[DH:P, DH:P], 1.0))
            step(nc.gpsimd.affine_select(out=ident[:], in_=ones[:], compare_op=ALU.is_equal, fill=0.0, base=0,
                                         pattern=[[-1, P]], channel_multiplier=1))
            step(nc.gpsimd.affine_select(out=after[:], in_=ones[:], compare_op=ALU.is_gt, fill=0.0, base=0,
                                         pattern=[[-1, P]], channel_multiplier=1))
            assert count[0] == CONSTS0
            stores = [0]

            def store(dst, src, semaphore=stored):
                pool.dma_start(dst, src).then_inc(semaphore, 16)
                stores[0] += semaphore is stored

            def memory(l):
                mb = MBS[l]
                pool.dma_start(mb["mem"][:], mem_prompt[0].rearrange("(t p) n -> p t n", p=P)).then_inc(mem_in, 16)

            def sample_loads(l, G):
                mb = MBS[l]
                for buffer, cache in ((mb["ks"], cache_mem_k), (mb["vs"], cache_mem_v)):
                    pool.dma_start(buffer[:].rearrange("p b t n -> p (b t) n"),
                                   cache[l, G * GS:(G + 1) * GS].rearrange("b (t p) h d -> p (b t) (h d)", p=P)).then_inc(ks_in, 16)

            def memory_stores(l):
                pool.wait_ge(kv_done, l + 1)
                for t, b in ((new_mem_k_p, "km"), (new_mem_v_p, "vm")):
                    store(t[l, 0].rearrange("(t p) h d -> p t (h d)", p=P), MBS[l][b][:])

            pool.wait_ge(tr_free, marks["start"])
            memory(0)
            pool.wait_ge(tr_free, marks["conv states"])
            store(new_conv_p[0, 0], stP[:])
            for G in range(GR):
                store(new_conv_s[0, G * GS:(G + 1) * GS].rearrange("b n c -> (b n) c"), stS[:, G, :])
            pool.wait_ge(stored, 16 * stores[0])
            sample_loads(0, 0)
            memory_stores(0)
            for G in range(1, GR):
                pool.wait_ge(at_pv, len(MEM_UNITS) + G)
                sample_loads(0, G)

            pool.wait_ge(w_used, C_FOX)
            one = lambda instruction: step(instruction, which=1)
            one(nc.gpsimd.memset(win[:], 1.0))
            one(nc.gpsimd.affine_select(out=win[:], in_=win[:], compare_op=ALU.is_ge, fill=0.0, base=-(SEQ - P),
                                        pattern=[[1, 2 * SEQ - P]], channel_multiplier=-1))
            one(nc.gpsimd.memset(maskd[:], 0.0))
            one(nc.gpsimd.affine_select(out=maskd[:], in_=maskd[:], compare_op=ALU.is_ge, fill=NEG, base=0,
                                        pattern=[[-1, P]], channel_multiplier=1))
            one(nc.gpsimd.memset(bm[:], 1.0))
            one(nc.gpsimd.affine_select(out=bm[:], in_=bm[:], compare_op=ALU.is_ge, fill=0.0, base=0,
                                        pattern=[[-NQ, NB]], channel_multiplier=1))
            one(nc.gpsimd.affine_select(out=bm[:], in_=bm[:], compare_op=ALU.is_ge, fill=0.0, base=NQ - 1,
                                        pattern=[[NQ, NB]], channel_multiplier=-1))
            one(nc.gpsimd.affine_select(out=sameq[:], in_=bm[:].unsqueeze(2).broadcast_to([NS, NB, NQ]), compare_op=ALU.is_ge,
                                        fill=0.0, base=0, pattern=[[NQ, NB], [1, NQ]], channel_multiplier=-1))
            one(nc.gpsimd.memset(mshT[:], 0.0))
            m = mshT[:].rearrange("j (h q) -> j h q", h=NH)
            one(nc.gpsimd.affine_select(out=m, in_=m, compare_op=ALU.is_ge, fill=NEG, base=-(NS - NQ),
                                        pattern=[[0, NH], [0, NQ]], channel_multiplier=1))
            one(nc.gpsimd.affine_select(out=m, in_=m, compare_op=ALU.is_ge, fill=NEG, base=NS - NQ,
                                        pattern=[[0, NH], [1, NQ]], channel_multiplier=-1))
            one(nc.gpsimd.memset(dq[:], 0.0))
            for b in range(NB):
                one(nc.gpsimd.affine_select(out=dq[:], in_=dq[:], compare_op=ALU.not_equal, fill=1.0, base=-NQ * b,
                                            pattern=[[-1, NQ]], channel_multiplier=1))
            assert count[1] == CONSTS1
            pool.wait_ge(c_ready, 1)
            store(new_fox_logf_p[0, 0].rearrange("(t p) h -> p t h", p=P), lf[:, 0:TT, :])
            store(new_fox_logf_s[0].rearrange("b q h -> (b q) h"), lf[0:NS, TT, :])
            pool.wait_ge(hn_done, MP + 1 + 3 * HP)
            store(new_fox_v_p[0, 0].rearrange("(t p) h d -> p t (h d)", p=P), vtok[:, 0:TT, :])
            store(new_fox_v_s[0].rearrange("b q h d -> (b q) (h d)"), vtok[0:NS, TT, :])
            for t in range(TT + 1):
                pool.wait_ge(tr_free, marks["k", t])
                if t < TT:
                    store(new_fox_k_p[0, 0].rearrange("(t p) h d -> t p (h d)", p=P)[t], ktok[:, t % 2, :], k_stored[t % 2])
                else:
                    store(new_fox_k_s[0].rearrange("b q h d -> (b q) (h d)"), ktok[0:NS, t % 2, :], k_stored[t % 2])
            for s in range(2):
                pool.wait_ge(k_stored[s], 16 * ((TT + 2 - s) // 2))
            pool.wait_ge(tr_free, marks["forget"])
            memory(1)
            memory_stores(1)
            pool.wait_ge(w_used, C_MEM1 + N_MEM)
            sample_loads(1, 0)
            pool.wait_ge(at_pv, 2 * len(MEM_UNITS) + GR + 1)
            sample_loads(1, 1)
            assert GR == 2

            pool.wait_ge(pages_in, 16)
            pool.wait_ge(tr_free, marks["far"])

            def values(c, first):
                for pp in range(CPG):
                    p = pool.value_load(pages[0:1, bass.ds(first + CPG * c + pp, 1)], min_val=0, max_val=N_PHYS - 1)
                    pool.dma_start(vring[:, c % 2, pp, :], cache_fox_v[0, bass.ds(p, 1)].rearrange("o p h d -> (o p) (h d)"))\
                        .then_inc(v_in[c % 2], 16)
            values(0, 0)
            values(1, 0)
            with pool.Fori(0, NB - 1) as b:
                for c in range(NCH):
                    pool.wait_ge(v_used, NCH * b + c + 1)
                    values(c + 2, NP * b)
            for c in range(NCH - 2):
                pool.wait_ge(v_used, NCH * (NB - 1) + c + 1)
                values(c + 2, NP * (NB - 1))
            for t in range(TT + 1):
                pool.wait_ge(tr_free, marks["y", t])
                if t < TT:
                    store(y_prompt[0].rearrange("(t p) n -> t p n", p=P)[t], ystage[:, t % 2, :], y_stored[t % 2])
                else:
                    store(y_sample.rearrange("b q n -> (b q) n"), ystage[0:NS, t % 2, :], y_stored[t % 2])
            pool.wait_ge(stored, 16 * stores[0])
            for s in range(2):
                pool.wait_ge(y_stored[s], 16 * ((TT + 2 - s) // 2))


_INS = ['x_prompt', 'x_sample', 'cache_conv', 'cache_fox_k', 'cache_fox_v', 'cache_fox_logf', 'cache_mem_k',
        'cache_mem_v', 'page_table', 'mem_prompt', 'norm1', 'conv_w_in', 'conv_dw', 'conv_dw_b', 'conv_ln_g',
        'conv_ln_b', 'fox_w_in', 'fox_b_f', 'fox_q_norm', 'fox_k_norm', 'mem_norm', 'w_mem_kv', 'mem_q_norm',
        'mem_k_norm', 'w_out', 'norm2', 'w_gate_up', 'w_down']


def kernel(**inputs):
    import numpy as _np
    import concourse.bacc as _bacc
    from concourse import mybir as _mybir
    from concourse.bass_utils import run_bass_kernel_spmd as _run

    nc = _bacc.Bacc("TRN2", target_bir_lowering=False, num_devices=1)
    arrays, args = {}, []
    for name in _INS:
        a = _np.ascontiguousarray(inputs[name])
        arrays[f"in_{name}_dram"] = a
        args.append(nc.dram_tensor(f"in_{name}_dram", a.shape, _mybir.dt.from_np(a.dtype), kind="ExternalInput").ap())
    _, S_, D_ = inputs["x_prompt"].shape
    NB_, NQ_ = inputs["x_sample"].shape[:2]
    _, H_, C_ = inputs["cache_conv"].shape[1:]
    NH_, DH_ = inputs["cache_fox_k"].shape[3:]
    L_, _, NM_, MH_, _ = inputs["cache_mem_k"].shape
    outs = [(1, S_, D_), (NB_, NQ_, D_), (1, 1, H_, C_), (1, 1, S_, NH_, DH_), (1, 1, S_, NH_, DH_), (1, 1, S_, NH_),
            (L_, 1, NM_, MH_, DH_), (L_, 1, NM_, MH_, DH_), (1, NB_, H_, C_), (1, NB_, NQ_, NH_, DH_),
            (1, NB_, NQ_, NH_, DH_), (1, NB_, NQ_, NH_)]
    for i, shape in enumerate(outs):
        args.append(nc.dram_tensor(f"out_{i}_dram", shape, _mybir.dt.float32, kind="ExternalOutput").ap())
    build(nc, *args)
    r = _run(nc, [arrays], core_ids=[0])
    return tuple(r.results[0][f"out_{i}_dram"] for i in range(len(outs)))
```

```python
from contextlib import ExitStack

import concourse.bass as bass
from concourse import mybir

ALU = mybir.AluOpType
ACT = mybir.ActivationFunctionType
F32 = mybir.dt.float32
F32R = mybir.dt.float32r
I32 = mybir.dt.int32
AX_X = mybir.AxisListType.X

P = 128
EPS = 1e-6
NEG = -1e30
ATANH_TERMS = 8


class Steps:

    def __init__(self, semaphore):
        self.semaphore, self.n, self.per_pass, self.i = semaphore, 0, 0, None

    def inc(self, instruction):
        instruction.then_inc(self.semaphore, 1)
        self.n += 1

    def value(self):
        return self.n if self.i is None else self.i * self.per_pass + self.n

    def enter(self, i, per_pass):
        self.i, self.per_pass, self.first = i, per_pass, self.n

    def leave(self, passes):
        assert self.n - self.first == self.per_pass, (self.n - self.first, self.per_pass)
        self.i, self.n = None, self.first + passes * self.per_pass


def build(nc, x_prompt, x_sample, cache_conv, cache_fox_k, cache_fox_v, cache_fox_logf,
          cache_mem_k, cache_mem_v, page_table, mem_prompt, norm1, conv_w_in, conv_dw,
          conv_dw_b, conv_ln_g, conv_ln_b, fox_w_in, fox_b_f, fox_q_norm, fox_k_norm,
          mem_norm, w_mem_kv, mem_q_norm, mem_k_norm, w_out, norm2, w_gate_up, w_down,
          y_prompt, y_sample, new_conv_p, new_fox_k_p, new_fox_v_p, new_fox_logf_p,
          new_mem_k_p, new_mem_v_p, new_conv_s, new_fox_k_s, new_fox_v_s, new_fox_logf_s):
    SEQ, D = x_prompt.shape[1:]
    NB, NQ = x_sample.shape[:2]
    NS = NB * NQ
    T = SEQ + NS
    HT = T // 2
    KD = D // P
    TT = SEQ // P
    W = conv_dw.shape[1]
    H = W - 1
    CH = conv_dw.shape[2]
    KC = CH // P
    DF = w_down.shape[1]
    KF = DF // P
    KF2 = KF // 2
    NH, DH = cache_fox_k.shape[3:]
    HP = NH // 2
    NP, PG = page_table.shape[1], cache_fox_k.shape[2]
    N_PHYS = cache_fox_k.shape[1]
    MH = cache_mem_k.shape[3]
    NM = mem_prompt.shape[1]
    MT = NM // P
    MW = MH * DH
    MP = MH // 2
    GS = 4
    GR = NB // GS
    ROWS = NH * NQ
    QR = 4 * NQ
    SCALE = float(DH) ** -0.5
    NPAST = NP * PG
    CPG = 2
    NCH = NP // CPG
    KEYS = CPG * PG
    PE_TAPS = 9
    RING = 4
    assert P == PG == NB * NP and T % 2 == 0 and HT <= 512 and KF % 2 == 0 and NS <= P and MH == 4
    assert QR == 32 and ROWS == 3 * QR and KC == HP and MP == MT == 2 and KD == KC + MP

    C_CONV = 0
    C_MEM0 = C_CONV + 2 * KC + MP
    N_MEM = 4
    C_WO0 = C_MEM0 + N_MEM
    C_GU0 = C_WO0 + KD
    C_DN0 = C_GU0 + 2 * KF
    C_FOX = C_DN0 + 2 * KD
    N_FOX = 1 + 3 * HP + MP
    C_MEM1 = C_FOX + N_FOX
    C_WO1 = C_MEM1 + N_MEM
    C_GU1 = C_WO1 + KD
    C_DN1 = C_GU1 + 2 * KF
    C_END = C_DN1 + 2 * KD
    C_MEM, C_WO, C_GU, C_DN = (C_MEM0, C_MEM1), (C_WO0, C_WO1), (C_GU0, C_GU1), (C_DN0, C_DN1)
    KM = KD // N_MEM
    SMALL, LARGE = KD * P, KF2 * P
    assert KM * 2 * MW == SMALL

    def chunk_size(n):
        return LARGE if C_DN0 <= n < C_FOX or C_DN1 <= n else SMALL

    VEC_LOADS = 6 + 8 + 1 + 2 + 1
    CONSTS0, CONSTS1 = 9, 14 + NB

    MEM_UNITS = [("mem", hp, t, NM) for hp in range(MP) for t in range(TT)]
    FOX_UNITS = [("fox", hp, t, (t + 1) * P) for hp in range(HP) for t in range(TT)]

    with ExitStack() as ctx:
        def sem(name):
            return ctx.enter_context(nc.semaphore(name))

        top = [nc.sbuf_base + (-nc.sbuf_base) % 32]

        def at(name, shape, offset, dt=F32):
            size = 4
            for n in shape[1:]:
                size *= n
            end = offset + size + (-size) % 32
            assert end <= nc.sbuf_usable_end, (name, end)
            return nc.alloc_sbuf_tensor_at(name, shape, dt, offset=offset), end

        def sb(name, shape, dt=F32):
            buffer, top[0] = at(name, shape, top[0], dt)
            return buffer

        xT = sb("xT", [P, KD, T])
        aH = sb("aH", [P, KD, T], F32R)
        aL = sb("aL", [P, KD, T], F32R)
        ring_at = top[0]
        raw = sb("raw", [P, 2, LARGE])
        wH = [sb(f"wH{s}", [P, LARGE], F32R) for s in range(2)]
        wL = [sb(f"wL{s}", [P, LARGE], F32R) for s in range(2)]
        sq = sb("sq", [P, 2, T])
        tmp = sb("tmp", [P, 2, T])
        rb = sb("rb", [P, T])
        ident = sb("ident", [P, P])
        ones = sb("ones", [P, P])
        blocks = sb("blocks", [P, P])
        after = sb("after", [P, P])
        V_N1, V_N2, V_MEM = 0, 2 * KD, 4 * KD
        V_DWB, V_LNG, V_LNB = 6 * KD, 6 * KD + KC, 6 * KD + 2 * KC
        V_MQ = 6 * KD + 3 * KC
        N_VEC = V_MQ + 4
        vec = sb("vec", [P, N_VEC])
        dw_at = top[0]
        dw = sb("dw", [P, KC, W])
        eps = sb("eps", [P, 3])
        dw2 = sb("dw2", [P, 2, W])
        gk_row = sb("gk_row", [P, 2, DH])
        bf = sb("bf", [NH, 1])
        stat = sb("stat", [P, 64])
        pages = sb("pages", [1, NB * NP], I32)
        BASE = top[0]

        def memory_buffers(n, o, far):
            b = {}
            for name, shape in (("prob", [P, 2, 2, 512 if n else NM]), ("pT", [P, 2, 4, P]), ("km", [P, MT, MW]),
                                ("vm", [P, MT, MW]), ("kmT", [P, MP, NM]), ("qm", [P, MP, T]),
                                ("qd", [P, GS, MP, QR]), ("o", [P, MW])):
                b[name], o = at(f"{name}{n}", shape, o)
            end = o
            o = far or o
            b["mem"], o = at(f"mem{n}", [P, MT, D], o)
            b["mH"], o = at(f"mH{n}", [P, KD, NM], o, F32R)
            b["mL"], o = at(f"mL{n}", [P, KD, NM], o, F32R)
            far_end = o
            o = far or (end if not n else o)
            if not n:
                o = far_end
            b["ks"], o = at(f"ks{n}", [P, GS, MT, MW], o)
            b["vs"], o = at(f"vs{n}", [P, GS, MT, MW], o)
            b["ksT"], o = at(f"ksT{n}", [P, GS, MP, NM], o)
            return b, end, o

        uP, o = at("uP", [P, KC, H + SEQ], BASE)
        uS, o = at("uS", [P, KC, NB, H + NQ], o)
        yc_at = o
        yc, o = at("yc", [P, KC, T], o)
        mb0, _, o0 = memory_buffers(0, o, None)
        ks_at = o0 - 3 * 4 * GS * MT * MW
        stP, o = at("stP", [H, CH], ks_at)
        stS, o = at("stS", [GS * H, GR, CH], o)
        usc, o = at("usc", [P, KC, NB, H], o)
        diag, o = at("diag", [P, 2, PE_TAPS, P], o)
        assert o <= o0
        xin, o = at("xin", [P, TT + 1, D], yc_at)
        vrow, o = at("vrow", [N_VEC, P], o)
        dwrow, o = at("dwrow", [W, CH], o)
        crow, o = at("crow", [GS * H, GR, CH], o)
        gH, o = at("gH", [P, KF, T], BASE, F32R)
        gL, o = at("gL", [P, KF, T], o, F32R)
        qkT, o = at("qkT", [P, 2 * HP, T], BASE)
        vtok, o = at("vtok", [P, TT + 1, CH], o)
        lf, o = at("lf", [P, TT + 1, NH], o)
        ctok, o = at("ctok", [P, TT + 1, NH], o)
        work, o = at("work", [P, 4, (TT + 1) * NH], o)
        maskd, o = at("maskd", [P, P], o)
        sameq, o = at("sameq", [NS, NS], o)
        mshift, o = at("mshift", [ROWS, NS - NQ + NS], o)
        maskb, o = at("maskb", [ROWS, NS], o)
        mshT, o = at("mshT", [NS - NQ + NS, ROWS], o)
        bm, o = at("bm", [NS, NB], o)
        dq, o = at("dq", [NS, NQ], o)
        cqA, o = at("cqA", [NS, NH, NQ], o)
        cqr, o = at("cqr", [ROWS, NB], o)
        ncx, o = at("ncx", [NS, NH, NQ], o)
        rx, o = at("rx", [P, 2, CPG, NH, NQ], o)
        qx, o = at("qx", [P, HP, QR], o)
        rtok, _ = at("rtok", [P, NH, NB * NP], o)
        lfrow, o = at("lfrow", [NB * NP, PG * NH], o)
        later, _ = at("later", [NB * NP, NB * NP], dw_at)
        assert NB * NP <= KC * W
        lftot, o = at("lftot", [NB * NP, NH], o)
        ncT, o = at("ncT", [P, SEQ], o)
        mix_at = o
        assert mix_at % 32 == 0
        far1 = mix_at + 4 * (2 * 2 * 512 + 2 * 4 * P + 2 * MT * MW + MP * NM + MP * T + GS * MP * QR + MW)
        mb1, z_end, _ = memory_buffers(1, mix_at, far1)
        assert z_end == far1
        ktok, _ = at("ktok", [P, 2, CH], far1)
        lfd, e_ = at("lfd", [P, TT, P], far1 + 4 * 2 * CH)
        win, _ = at("win", [P, 2 * SEQ - P], e_)
        kT, o = at("kT", [P, 2, HP, KEYS], mix_at)
        S, o = at("S", [ROWS, NPAST + NS], o)
        pTs, o = at("pTs", [P, NP + 1, ROWS], o)
        lfT, _ = at("lfT", [P, NH, NB * NP], mix_at + 4 * 2 * HP * KEYS)
        ncb, e_ = at("ncb", [P, 2, 2, SEQ], mix_at + 4 * 2 * HP * KEYS)
        assert e_ <= far1
        kring, vring = [], []
        ring_end = ring_at
        for c in range(RING):
            buffer, ring_end = at(f"kring{c}", [P, CPG, CH], ring_end)
            kring.append(buffer)
        for c in range(RING):
            if c == RING - 1:
                buffer, ring_end = at(f"vring{c}", [P, CPG, CH], ring_end)
            else:
                buffer, o = at(f"vring{c}", [P, CPG, CH], o)
            vring.append(buffer)
        assert ring_end <= ring_at + 4 * 6 * LARGE
        os_, o = at("os_", [ROWS, 4 * DH], o)
        L1_END = o
        ystage, _ = at("ystage", [P, 2, D], BASE)
        MBS = (mb0, mb1)

        ps = ctx.enter_context(nc.psum_tensor("ps", [P, 8, 512], F32))

        def acc(slot):
            return ps[:, 2 * slot:2 * slot + 2, 0:HT]

        def halves(ap):
            return ap.rearrange("p (a n) -> p a n", a=2)

        x_in, vec_in, hist_in, mem_in, pages_in = (sem(n) for n in ("x_in", "vec_in", "hist_in", "mem_in", "pages_in"))
        raw_in = [sem(f"raw_in{s}") for s in range(2)]
        ks_in = sem("ks_in")
        k_in = [sem(f"k_in{s}") for s in range(RING)]
        v_in = [sem(f"v_in{s}") for s in range(RING)]
        lf_in = sem("lf_in")
        hi_done, lo_done, w_used, acc_ready, acc_free = (sem(n) for n in ("hi_done", "lo_done", "w_used", "acc_ready", "acc_free"))
        consts = sem("consts")
        consts1 = sem("consts1")
        vchain = sem("vchain")
        diag_ready, taps_ready, y_begun = sem("diag_ready"), sem("taps_ready"), sem("y_begun")
        ysq_used, swish_done, usc_done = sem("ysq_used"), sem("swish_done"), sem("usc_done")
        x_new, sq_done, sq_used, ss_ready = (sem(n) for n in ("x_new", "sq_done", "sq_used", "ss_ready"))
        sq_added = sem("sq_added")
        v_done, vH_done, a_ready = (sem(n) for n in ("v_done", "vH_done", "a_ready"))
        tr_ready, tr_free = sem("tr_ready"), sem("tr_free")
        sig_done, sig_used, u_done, y_done, ysq_done, ln_ready = (sem(n) for n in ("sig_done", "sig_used", "u_done", "y_done", "ysq_done", "ln_ready"))
        lny_done, mixf_done = sem("lny_done"), sem("mixf_done")
        norm_root, head_root, ln_root, mem_root, kss_done, k_root = (sem(n) for n in ("norm_root", "head_root", "ln_root", "mem_root", "kss_done", "k_root"))
        z_done, hn_ready, hn_done = (sem(n) for n in ("z_done", "hn_ready", "hn_done"))
        ms_done, mn_done, mt_done, mH_done, mL_done, kvsq_done, kv_done = (sem(n) for n in ("ms_done", "mn_done", "mt_done", "mH_done", "mL_done", "kvsq_done", "kv_done"))
        at_s, at_max, at_exp, at_prob, at_pv, at_hi, at_lo = (sem(n) for n in ("at_s", "at_max", "at_exp", "at_prob", "at_pv", "at_hi", "at_lo"))
        qd_done, oT_ready, oT_hi = sem("qd_done"), sem("oT_ready"), sem("oT_hi")
        silu_done, g_done, gH_done, gL_done = (sem(n) for n in ("silu_done", "g_done", "gH_done", "gL_done"))
        e_done, zab_done, c_ready, c_done, stage_done = (sem(n) for n in ("e_done", "zab_done", "c_ready", "c_done", "stage_done"))
        qx_done, lftot_done, rx_done = (sem(n) for n in ("qx_done", "lftot_done", "rx_done"))
        kt_ready, kt_ev_v, kt_ev_a, kt_used = (sem(n) for n in ("kt_ready", "kt_ev_v", "kt_ev_a", "kt_used"))
        sc_ready, sc_free, sn_ready, sn_free = (sem(n) for n in ("sc_ready", "sc_free", "sn_ready", "sn_free"))
        smax_done, sexp_done, pt_ready, pt_free, o_ready, o_done = (sem(n) for n in ("smax_done", "sexp_done", "pt_ready", "pt_free", "o_ready", "o_done"))
        k_used, v_used = sem("k_used"), sem("v_used")
        stored = sem("stored")
        k_stored = [sem(f"k_stored{s}") for s in range(2)]
        y_stored = [sem(f"y_stored{s}") for s in range(2)]

        block = ctx.enter_context(nc.Block())

        marks = {"km stored": 1 + GR + 2 + 2 + 2 + 2}

        def columns(w, start, k0=0, ks=KD):
            return w.rearrange("(k p) n -> p k n", p=P)[:, k0:k0 + ks, bass.ds(start, P)]

        @block.vector
        def _(dve):
            steps = Steps(vchain)
            tr = [0]

            def link(instruction):
                steps.inc(instruction)
                dve.wait_ge(vchain, steps.value())

            def lo(n0, i=0):
                s, size = n0 % 2, chunk_size(n0)
                dve.wait_ge(hi_done, n0 + 1 + 2 * i)
                nc.vector.tensor_tensor(wL[s][:, 0:size], raw[:, s, 0:size], wH[s][:, 0:size].bitcast(F32),
                                        ALU.subtract).then_inc(lo_done, 1)

            def group():
                g = tr[0]
                tr[0] += 1
                dve.wait_ge(tr_ready, g + 1)
                return ps[:, 6 + g % 2, :]

            def norm(r):
                gain = (V_N1, V_N2)[r % 2] + (r // 2) * KD
                dve.wait_ge(norm_root, r + 1)
                link(nc.vector.reciprocal(rb[:], rb[:]))
                for k in range(KD + 1):
                    if k < KD:
                        if KD * r + k >= 2:
                            dve.wait_ge(a_ready, KD * r + k - 1)
                        nc.vector.scalar_tensor_tensor(out=tmp[:, k % 2], in0=xT[:, k], scalar=vec[:, gain + k:gain + k + 1],
                                                       in1=rb[:], op0=ALU.mult, op1=ALU.mult).then_inc(v_done, 1)
                    if k:
                        dve.wait_ge(vH_done, KD * r + k)
                        nc.vector.tensor_tensor(aL[:, k - 1], tmp[:, (k - 1) % 2], aH[:, k - 1].bitcast(F32),
                                                ALU.subtract).then_inc(a_ready, 1)

            def finish_head(z0, out, gain, h0, i=0):
                dve.wait_ge(head_root, h0 + 1 + 2 * i)
                link(nc.vector.reciprocal(rb[:], rb[:]))
                nc.vector.scalar_tensor_tensor(out=out, in0=tmp[:, z0 % 2], scalar=vec[:, gain:gain + 1], in1=rb[:],
                                               op0=ALU.mult, op1=ALU.mult).then_inc(hn_done, 1)

            def memory(l):
                mb = MBS[l]
                dve.wait_ge(mem_root, l + 1)
                link(nc.vector.reciprocal(stat[:, 34:34 + MT], stat[:, 34:34 + MT]))
                for t in range(MT):
                    last = nc.vector.tensor_scalar(mb["mem"][:, t], mb["mem"][:, t], stat[:, 34 + t:35 + t], None, ALU.mult)
                last.then_inc(mn_done, 1)
                for g in range(KD // 2):
                    bank = group()
                    if g >= 2:
                        dve.wait_ge(mL_done, l * KD // 2 + g - 1)
                    for k in range(2):
                        gain = V_MEM + l * KD + 2 * g + k
                        last = nc.vector.tensor_scalar(tmp[:, g % 2, k * NM:(k + 1) * NM], bank[:, k * NM:(k + 1) * NM],
                                                       vec[:, gain:gain + 1], None, ALU.mult)
                    last.then_inc(tr_free, 1)
                    marks["memory", l, g] = tr[0]
                    dve.wait_ge(mH_done, l * KD // 2 + g + 1)
                    nc.vector.tensor_tensor(mb["mL"][:, 2 * g:2 * g + 2, :].rearrange("p k n -> p (k n)"), tmp[:, g % 2, 0:2 * NM],
                                            mb["mH"][:, 2 * g:2 * g + 2, :].rearrange("p k n -> p (k n)").bitcast(F32),
                                            ALU.subtract).then_inc(mL_done, 1)
                for i in range(N_MEM - l):
                    lo(C_MEM[l] + 1 + i)
                    if not l:
                        share = [PE_TAPS + (W - PE_TAPS) * x // N_MEM for x in (i, i + 1)]
                        taps(KC - 1, 0, *share)
                dve.wait_ge(kvsq_done, l + 1)
                (nc.vector.tensor_reduce(stat[:, 36:36 + MT * MH].rearrange("p (t h) -> p t h", t=MT),
                                             sq[:, :, 0:MW].rearrange("p t (h d) -> p t h d", h=MH), AX_X, ALU.add)).then_inc(kss_done, 1)
                dve.wait_ge(k_root, l + 1)
                link(nc.vector.reciprocal(stat[:, 44:44 + MT * MH], stat[:, 44:44 + MT * MH]))
                for t in range(MT):
                    link(nc.vector.tensor_tensor(mb["km"][:, t].rearrange("p (h d) -> p h d", h=MH),
                                                 ps[:, t, 0:MW].rearrange("p (h d) -> p h d", h=MH),
                                                 stat[:, 44 + MH * t:44 + MH * t + MH].unsqueeze(2).broadcast_to([P, MH, DH]), ALU.mult))
                    last = nc.vector.tensor_tensor(mb["km"][:, t].rearrange("p (h d) -> p h d", h=MH),
                                                   mb["km"][:, t].rearrange("p (h d) -> p h d", h=MH),
                                                   gk_row[:, l:l + 1, :].broadcast_to([P, MH, DH]), ALU.mult)
                last.then_inc(kv_done, 1)
                bank = group()
                nc.vector.tensor_copy(mb["kmT"][:].rearrange("p a n -> p (a n)"), bank).then_inc(tr_free, 1)

            def top_of(u, unit, mb):
                kind, hp, t, keys = unit
                banks = ps[:, 2 * (u % 2):2 * (u % 2) + 2, 0:keys]
                st = stat[:, 8 * (u % 2):8 * (u % 2) + 8]
                dve.wait_ge(at_s, u + 1)
                if kind == "fox":
                    for e in range(2):
                        c_q = ctok[:, t, 2 * hp + e:2 * hp + e + 1]
                        last = nc.vector.scalar_tensor_tensor(out=mb["prob"][:, u % 2, e, 0:keys], in0=banks[:, e, :], scalar=c_q,
                                                              in1=ncb[:, hp % 2, e, 0:keys], op0=ALU.add, op1=ALU.add)
                    link(last)
                    diagonal = mb["prob"][:, u % 2, :, keys - P:keys]
                    link(nc.vector.tensor_tensor(diagonal, diagonal, maskd[:].unsqueeze(1).broadcast_to([P, 2, P]), ALU.add))
                    banks = mb["prob"][:, u % 2, :, 0:keys]
                nc.vector.tensor_reduce(st[:, 0:2], banks, AX_X, ALU.max, negate=True).then_inc(at_max, 1)

            def attend(u0, units, mb, h0):
                def out_lo(i):
                    kind, hp, t, keys = units[i]
                    tile, u = (hp if kind == "fox" else KC + hp), u0 + i
                    dve.wait_ge(at_hi, h0 + i + 1)
                    nc.vector.tensor_tensor(aL[:, tile, t * P:(t + 1) * P], ps[:, 4 + u % 2, 0:P],
                                            aH[:, tile, t * P:(t + 1) * P].bitcast(F32), ALU.subtract).then_inc(at_lo, 1)
                def broadcast_c(hp):
                    for e in range(2):
                        bank = group()
                        nc.vector.tensor_copy(ncb[:, hp % 2, e, :], bank).then_inc(tr_free, 1)
                if units[0][0] == "fox":
                    broadcast_c(0)
                    dve.wait_ge(tr_free, tr[0])
                for i in range(2):
                    top_of(u0 + i, units[i], mb)
                for i, (kind, hp, t, keys) in enumerate(units):
                    u = u0 + i
                    st = stat[:, 8 * (u % 2):8 * (u % 2) + 8]
                    dve.wait_ge(at_exp, u + 1)
                    link(nc.vector.reciprocal(st[:, 4:6], st[:, 2:4]))
                    for e in range(2):
                        last = nc.vector.tensor_scalar(mb["prob"][:, u % 2, e, 0:keys], mb["prob"][:, u % 2, e, 0:keys],
                                                       st[:, 4 + e:5 + e], None, ALU.mult)
                    last.then_inc(at_prob, 1)
                    if i:
                        out_lo(i - 1)
                    if kind == "mem":
                        bank = group()
                        nc.vector.tensor_copy(mb["pT"][:, :, 0:2, :].rearrange("p e k q -> p e (k q)"),
                                              bank.rearrange("p (e n) -> p e n", e=2)).then_inc(tr_free, 1)
                    else:
                        for e in range(2):
                            bank = group()
                            nc.vector.tensor_copy(mb["pT"][:, e, 0:t + 1, :].rearrange("p k q -> p (k q)"),
                                                  bank[:, 0:keys]).then_inc(tr_free, 1)
                    if i + 2 < len(units):
                        top_of(u + 2, units[i + 2], mb)
                    if kind == "fox" and t == 0 and hp + 1 < HP:
                        broadcast_c(hp + 1)
                out_lo(len(units) - 1)

            def sample_memory(l, u0):
                mb = MBS[l]
                link(nc.vector.memset(mb["qd"][:], 0.0))
                for G in range(GR):
                    u = u0 + G
                    st = stat[:, 8 * (u % 2):8 * (u % 2) + 8]
                    if G:
                        dve.wait_ge(at_s, u)
                    for hp in range(MP):
                        for e in range(2):
                            r = slice(DH * e, DH * e + DH)
                            col = (2 * hp + e) * NQ
                            src = mb["qm"][r, hp, SEQ + G * GS * NQ:SEQ + (G + 1) * GS * NQ].rearrange("p (b q) -> p b q", b=GS)
                            last = nc.vector.tensor_copy(mb["qd"][r, :, hp, col:col + NQ], src)
                    last.then_inc(qd_done, 1)
                    for b in range(GS):
                        bank = group()
                        nc.vector.tensor_copy(mb["ksT"][:, b].rearrange("p a n -> p (a n)"), bank).then_inc(tr_free, 1)
                    dve.wait_ge(at_s, u + 1)
                    nc.vector.tensor_reduce(st[:, 0:1], ps[:, 2 * (u % 2), 0:NM], AX_X, ALU.max, negate=True).then_inc(at_max, 1)
                    dve.wait_ge(at_exp, u + 1)
                    link(nc.vector.reciprocal(st[:, 4:5], st[:, 2:3]))
                    nc.vector.tensor_scalar(mb["prob"][:, u % 2, 0, 0:NM], mb["prob"][:, u % 2, 0, 0:NM], st[:, 4:5], None,
                                            ALU.mult).then_inc(at_prob, 1)
                    bank = group()
                    nc.vector.tensor_copy(mb["pT"][:, 0, 0:MT, :].rearrange("p k q -> p (k q)"), bank[:, 0:MT * P]).then_inc(tr_free, 1)
                    dve.wait_ge(at_pv, u + 1)
                    nc.vector.tensor_copy(mb["o"][:], ps[:, 4 + u % 2, 0:MW]).then_inc(at_lo, 1)
                    marks["sample memory", l, G] = tr[0]
                    bank = group()
                    dve.wait_ge(oT_hi, GR * l + G + 1)
                    for s in range(MP):
                        for e in range(2):
                            r = slice(DH * e, DH * e + DH)
                            src = bank[r, s * P:(s + 1) * P].rearrange("p (b h q) -> p b h q", b=GS, h=MH)[:, :, 2 * s + e, :]
                            to = slice(SEQ + G * GS * NQ, SEQ + (G + 1) * GS * NQ)
                            last = nc.vector.tensor_tensor(aL[r, KC + s, to].rearrange("p (b q) -> p b q", b=GS), src,
                                                           aH[r, KC + s, to].rearrange("p (b q) -> p b q", b=GS).bitcast(F32), ALU.subtract)
                    last.then_inc(tr_free, 1)

            def residual(c0, per_tile, r):
                if r < 4:
                    link(nc.vector.memset(rb[:], 0.0))
                added = (KD - 1) * (r - 1)

                def tile(j0, i):
                    for s in range(per_tile):
                        n0 = c0 + per_tile * j0 + s + 1
                        if n0 < C_END:
                            lo(n0, i if per_tile == 1 else 2 * i)
                    dve.wait_ge(w_used, c0 + per_tile * (j0 + 1) + 2 * per_tile * i)
                    x = xT[:, bass.ds(j0 + 2 * i, 1), :].rearrange("p o (a n) -> p (o a) n", a=2)
                    nc.vector.tensor_tensor(x, x, acc(j0 % 2), ALU.add).then_inc(x_new, 1)
                    if r < 4 and j0:
                        dve.wait_ge(sq_done, KD * r + j0 + 2 * i)
                        if j0 > 1:
                            dve.wait_ge(sq_added, added + j0 - 1 + 2 * i)
                        nc.vector.tensor_tensor(rb[:], rb[:], sq[:, (j0 - 1) % 2], ALU.add).then_inc(sq_added, 1)
                for j in range(2):
                    tile(j, 0)
                with dve.Fori(0, KD // 2 - 2) as i:
                    for j in range(2, 4):
                        tile(j, i)
                for j in range(KD - 2, KD):
                    tile(j, 0)

            def ffn(l):
                c0, g0 = C_GU[l], l * KF

                def tile(f0, i):
                    lo(c0 + 2 * f0 + 1, 2 * i)
                    lo(c0 + 2 * f0 + 2, 2 * i)
                    dve.wait_ge(silu_done, g0 + f0 + 1 + 2 * i)
                    dve.wait_ge(w_used, c0 + 2 * f0 + 2 + 4 * i)
                    if g0 + f0 >= 2:
                        dve.wait_ge(gL_done, g0 + f0 - 1 + 2 * i)
                    nc.vector.tensor_tensor(halves(tmp[:, f0 % 2]), acc(2 * (f0 % 2) + 1), halves(sq[:, f0 % 2]),
                                            ALU.mult).then_inc(g_done, 1)
                    dve.wait_ge(gH_done, g0 + f0 + 1 + 2 * i)
                    f = bass.ds(f0 + 2 * i, 1)
                    nc.vector.tensor_tensor(gL[:, f, :].rearrange("p o n -> p (o n)"), tmp[:, f0 % 2],
                                            gH[:, f, :].rearrange("p o n -> p (o n)").bitcast(F32), ALU.subtract).then_inc(gL_done, 1)
                for f in range(2):
                    tile(f, 0)
                with dve.Fori(0, KF2 - 2) as i:
                    for f in range(2, 4):
                        tile(f, i)
                for f in range(KF - 2, KF):
                    tile(f, 0)

            dve.wait_ge(consts, CONSTS0)
            for t in range(TT + 1):
                rows = P if t < TT else NS
                for q in range(KD // 4):
                    bank = group()
                    last = nc.vector.tensor_copy(xT[:, 4 * q:4 * q + 4, t * P:t * P + rows],
                                                 bank[:, 0:4 * rows].rearrange("p (k n) -> p k n", k=4))
                    last.then_inc(tr_free, 1)
            steps.inc(nc.vector.memset(uP[:, :, 0:H], 0.0))
            bank = group()
            nc.vector.tensor_copy(vec[:], bank[:, 0:N_VEC]).then_inc(tr_free, 1)
            dve.wait_ge(tr_free, tr[0])
            link(nc.vector.tensor_scalar(vec[:, 0:6 * KD], vec[:, 0:6 * KD], float(D) ** 0.5, None, ALU.mult))
            link(nc.vector.tensor_scalar(vec[:, V_MQ + 3:V_MQ + 4], vec[:, V_MQ + 3:V_MQ + 4], float(DH) ** 0.5, None, ALU.mult))
            dve.wait_ge(vec_in, VEC_LOADS * 16)
            link(nc.vector.tensor_scalar(gk_row[:], gk_row[:], float(DH) ** 0.5, None, ALU.mult))
            bank = group()
            nc.vector.tensor_copy(dw[:].rearrange("p c w -> p (c w)"), bank[:, 0:KC * W]).then_inc(tr_free, 1)
            for G in range(GR):
                for first, count in ((0, 4), (4, KC - 4)):
                    bank = group()
                    for c in range(count):
                        last = nc.vector.tensor_copy(uS[:, first + c, G * GS:(G + 1) * GS, 0:H],
                                                     bank[:, c * GS * H:(c + 1) * GS * H].rearrange("p (b n) -> p b n", b=GS))
                    last.then_inc(tr_free, 1)
            marks["start"] = tr[0]
            lo(0)
            norm(0)

            def glu(c0, i):
                c = bass.ds(c0 + 2 * i, 1)
                dve.wait_ge(sig_done, c0 + 1 + 2 * i)
                a = acc(2 * (c0 % 2))
                sg = halves(sq[:, c0 % 2])
                nc.vector.tensor_tensor(uP[:, c, H:H + HT].rearrange("p o n -> p (o n)"), a[:, 0, :], sg[:, 0, :], ALU.mult)
                nc.vector.tensor_tensor(uP[:, c, H + HT:H + SEQ].rearrange("p o n -> p (o n)"), a[:, 1, 0:SEQ - HT],
                                        sg[:, 1, 0:SEQ - HT], ALU.mult)
                nc.vector.tensor_tensor(uS[:, c, :, H:H + NQ].rearrange("p o b n -> p (o b) n"),
                                        a[:, 1, SEQ - HT:HT].rearrange("p (b n) -> p b n", b=NB),
                                        sg[:, 1, SEQ - HT:HT].rearrange("p (b n) -> p b n", b=NB), ALU.mult).then_inc(u_done, 1)
                dve.wait_ge(u_done, c0 + 1 + 2 * i)

            def taps(c0, i, first, end):
                c = bass.ds(c0 + 2 * i, 1)
                y = yc[:, c, :].rearrange("p o n -> p (o n)")
                if first == PE_TAPS:
                    link(nc.vector.tensor_copy(dw2[:, c0 % 2, :], dw[:, c, :].rearrange("p o w -> p (o w)")))
                    dve.wait_ge(y_begun, c0 + 1 + 2 * i)
                for j in range(first, end):
                    w = dw2[:, c0 % 2, j:j + 1]
                    uj = uP[:, c, j:j + SEQ].rearrange("p o n -> p (o n)")
                    sj = uS[:, c, :, j:j + NQ].rearrange("p o b n -> p (o b) n")
                    yp, ysm = y[:, 0:SEQ], y[:, SEQ:T].rearrange("p (b n) -> p b n", b=NB)
                    if j > PE_TAPS:
                        dve.wait_ge(vchain, steps.value() - 1)
                    steps.inc(nc.vector.scalar_tensor_tensor(out=yp, in0=uj, scalar=w, in1=yp, op0=ALU.mult, op1=ALU.add))
                    if j > PE_TAPS:
                        dve.wait_ge(vchain, steps.value() - 1)
                    last = nc.vector.scalar_tensor_tensor(out=ysm, in0=sj, scalar=w, in1=ysm, op0=ALU.mult, op1=ALU.add)
                    if j < W - 1:
                        steps.inc(last)
                    else:
                        last.then_inc(y_done, 1)

            MIDDLE = (PE_TAPS + W) // 2

            def conv_tile(c0, i=0):
                glu(c0, i)
                lo(C_CONV + 2 * c0 + 3, 2 * i)
                if c0 >= 2:
                    taps(c0 - 2, i, PE_TAPS, MIDDLE)
                lo(C_CONV + 2 * c0 + 4, 2 * i)
                if c0 >= 2:
                    taps(c0 - 2, i, MIDDLE, W)
            for n in range(1, 3):
                lo(C_CONV + n)
            for c in range(2):
                conv_tile(c)
            with dve.Fori(0, KC // 2 - 1) as i:
                steps.enter(i, 4 * (W - PE_TAPS))
                for c in range(2, 4):
                    conv_tile(c, i)
            steps.leave(KC // 2 - 1)
            taps(KC - 2, 0, PE_TAPS, MIDDLE)
            for z in range(MP):
                finish_head(z, mb0["qm"][:, z], V_MQ, z)
            taps(KC - 2, 0, MIDDLE, W)

            for first, count in ((0, 4), (4, KC - 4)):
                bank = group()
                nc.vector.tensor_copy(stP[:, first * P:(first + count) * P], bank[0:H, 0:count * P]).then_inc(tr_free, 1)
            for G in range(GR):
                for first, count in ((0, 4), (4, KC - 4)):
                    bank = group()
                    nc.vector.tensor_copy(stS[:, G, first * P:(first + count) * P], bank[0:GS * H, 0:count * P]).then_inc(tr_free, 1)
            marks["conv states"] = tr[0]
            memory(0)
            attend(0, MEM_UNITS, mb0, 0)
            sample_memory(0, len(MEM_UNITS))
            u = len(MEM_UNITS) + GR

            dve.wait_ge(ln_ready, 1)
            link(nc.vector.tensor_scalar(halves(rb[:]), ps[:, 0:2, 0:HT], 1.0 / CH, None, ALU.mult))
            for c in range(KC):
                nc.vector.tensor_tensor(yc[:, c], yc[:, c], rb[:], ALU.subtract).then_inc(lny_done, 1)
            dve.wait_ge(ln_root, 1)
            link(nc.vector.reciprocal(rb[:], rb[:]))
            for c in range(KC + 1):
                if c < KC:
                    nc.vector.scalar_tensor_tensor(out=yc[:, c], in0=yc[:, c], scalar=vec[:, V_LNG + c:V_LNG + c + 1], in1=rb[:],
                                                   op0=ALU.mult, op1=ALU.mult).then_inc(lny_done, 1)
                if c:
                    dve.wait_ge(mixf_done, c)
                    nc.vector.tensor_tensor(aL[:, c - 1], yc[:, c - 1], aH[:, c - 1].bitcast(F32), ALU.subtract).then_inc(stage_done, 1)
            residual(C_WO0, 1, 1)
            norm(1)
            ffn(0)
            residual(C_DN0, 2, 2)
            norm(2)

            dve.wait_ge(consts1, CONSTS1)
            link(nc.vector.memset(work[:, 0], 0.0))
            link(nc.vector.memset(lfd[:], 0.0))
            link(nc.vector.memset(qx[:], 0.0))
            Z = MP
            lo(C_FOX + 1)
            lo(C_FOX + 2)
            dve.wait_ge(hn_ready, Z + 1)
            nc.vector.tensor_copy(work[:, 0, 0:TT * NH], ps[:, 4, 0:TT * NH])
            nc.vector.tensor_copy(work[0:NS, 0, TT * NH:], ps[0:NS, 4, TT * NH:(TT + 1) * NH]).then_inc(hn_done, 1)
            dve.wait_ge(hn_done, Z + 1)
            nc.vector.scalar_tensor_tensor(out=work[:, 1], in0=work[:, 0], scalar=-1.0, in1=work[:, 0],
                                           op0=ALU.mult, op1=ALU.max).then_inc(zab_done, 1)
            z_, e_, s_, s2 = (work[:, n] for n in range(4))
            dve.wait_ge(e_done, 1)
            link(nc.vector.tensor_scalar(s2, e_, 2.0, None, ALU.add))
            link(nc.vector.reciprocal(s2, s2))
            link(nc.vector.tensor_tensor(s_, e_, s2, ALU.mult))
            link(nc.vector.tensor_tensor(s2, s_, s_, ALU.mult))
            link(nc.vector.tensor_scalar(e_, s2, 1.0 / (2 * ATANH_TERMS - 1), None, ALU.mult))
            for n in range(ATANH_TERMS - 2, 0, -1):
                link(nc.vector.scalar_tensor_tensor(out=e_, in0=e_, scalar=1.0 / (2 * n + 1), in1=s2, op0=ALU.add, op1=ALU.mult))
            link(nc.vector.scalar_tensor_tensor(out=s_, in0=e_, scalar=1.0, in1=s_, op0=ALU.add, op1=ALU.mult))
            link(nc.vector.tensor_scalar(z_, z_, 0.0, None, ALU.min))
            link(nc.vector.scalar_tensor_tensor(out=lf[:].rearrange("p t h -> p (t h)"), in0=s_, scalar=-2.0, in1=z_,
                                                op0=ALU.mult, op1=ALU.add))
            for e in range(2):
                last = nc.vector.tensor_copy(lfd[:, :, DH * e:DH * e + NH], lf[:, 0:TT, :])
            last.then_inc(c_ready, 1)

            def head_pass(z0, first, gain, i):
                lo(C_FOX - Z + z0 + 2, i)
                finish_head(z0, qkT[:, bass.ds(first + 2 * i, 1), :].rearrange("p o n -> p (o n)"), gain, z0 - 1, i)
            for first, gain in ((0, V_MQ + 2), (HP, V_MQ + 3)):
                with dve.Fori(0, HP // 2) as i:
                    steps.enter(i, 2)
                    for s in range(2):
                        head_pass(Z + 1 + first + s, first + s, gain, i)
                steps.leave(HP // 2)
            for hp in range(HP):
                z = Z + 1 + 2 * HP + hp
                lo(C_FOX - Z + z + 2)
                dve.wait_ge(hn_ready, z + 1)
                nc.vector.tensor_copy(vtok[:, 0:TT, hp * P:(hp + 1) * P], ps[:, 4, 0:TT * P].rearrange("p (t n) -> p t n", t=TT))
                nc.vector.tensor_copy(vtok[0:NS, TT, hp * P:(hp + 1) * P], ps[0:NS, 5, 0:P]).then_inc(hn_done, 1)
            for hp in range(MP):
                z = Z + 1 + 3 * HP + hp
                if z - Z + C_FOX + 2 <= C_MEM1:
                    lo(C_FOX - Z + z + 2)
                finish_head(z, mb1["qm"][:, hp], V_MQ + 1, MP + 2 * HP + hp)

            for t in range(TT + 1):
                rows = P if t < TT else NS
                if t >= 2:
                    dve.wait_ge(k_stored[t % 2], 16 * (t // 2))
                for first, count in ((0, 4), (4, HP - 4)):
                    bank = group()
                    nc.vector.tensor_copy(ktok[0:rows, t % 2, first * P:(first + count) * P], bank[0:rows, 0:count * P]).then_inc(tr_free, 1)
                marks["k", t] = tr[0]
            bank = group()
            nc.vector.tensor_copy(ctok[:, 0:TT, :].rearrange("p t h -> p (t h)"), bank[:, 0:TT * NH])
            nc.vector.tensor_copy(ctok[0:NS, TT, :], bank[0:NS, TT * NH:(TT + 1) * NH]).then_inc(tr_free, 1)
            dve.wait_ge(tr_free, tr[0])
            nc.vector.tensor_scalar(ncx[:], ctok[0:NS, TT, :].unsqueeze(2).broadcast_to([NS, NH, NQ]), -1.0, None, ALU.mult)
            nc.vector.tensor_tensor(cqA[:], ctok[0:NS, TT, :].unsqueeze(2).broadcast_to([NS, NH, NQ]),
                                    dq[:].unsqueeze(1).broadcast_to([NS, NH, NQ]), ALU.mult).then_inc(c_done, 1)
            bank = group()
            nc.vector.tensor_scalar(ncT[:], bank, -1.0, None, ALU.mult).then_inc(tr_free, 1)
            bank = group()
            nc.vector.tensor_copy(cqr[:], bank[0:ROWS, 0:NB])
            nc.vector.tensor_copy(mshift[:], bank[0:ROWS, NB:NB + NS - NQ + NS]).then_inc(tr_free, 1)
            marks["forget"] = tr[0]
            for s in range(2):
                dve.wait_ge(k_stored[s], 16 * ((TT + 2 - s) // 2))
            memory(1)
            attend(u, MEM_UNITS, mb1, len(MEM_UNITS))
            sample_memory(1, u + len(MEM_UNITS))
            marks["far"] = tr[0]
            u += len(MEM_UNITS) + GR

            dve.wait_ge(lf_in, 16 * NB * NP)
            nc.vector.tensor_reduce(lftot[:], lfrow[:].rearrange("n (k h) -> n h k", h=NH), AX_X, ALU.add).then_inc(lftot_done, 1)
            dve.wait_ge(stored, 16 * marks["km stored"])
            for g in range(NH // 4):
                bank = group()
                nc.vector.tensor_copy(lfT[:, 4 * g:4 * g + 4, :].rearrange("p h n -> p (h n)"), bank).then_inc(tr_free, 1)
            dve.wait_ge(tr_free, tr[0])
            for g in range(NH // 4):
                bank = group()
                nc.vector.tensor_copy(rtok[:, 4 * g:4 * g + 4, :].rearrange("p h n -> p (h n)"), bank).then_inc(tr_free, 1)
            attend(u, FOX_UNITS, mb1, 2 * len(MEM_UNITS))

            def keys_T(b, c):
                dve.wait_ge(kt_ready, 3 * (NCH * b + c) + 1)
                if c >= 2 or not (isinstance(b, int) and b == 0):
                    dve.wait_ge(sc_ready, NCH * b + c - 1)
                nc.vector.tensor_copy(kT[:, c % 2, 0:2, :].rearrange("p a n -> p (a n)"), ps[:, 0, :]).then_inc(kt_ev_v, 1)
                r = rtok[:, :, bass.ds(NP * b + CPG * c, CPG)].rearrange("p h n -> p n h")
                for pp in range(CPG):
                    last = nc.vector.tensor_copy(rx[:, c % 2, pp], r[:, pp].unsqueeze(2).broadcast_to([P, NH, NQ]))
                last.then_inc(rx_done, 1)

            def begin(b):
                for e in range(2):
                    for odd in range(2):
                        r = slice(DH * e, DH * e + DH)
                        col = (2 * odd + e) * NQ
                        nc.vector.tensor_copy(qx[r, :, col:col + NQ].rearrange("p (a o) q -> p a o q", o=2)[:, :, odd, :],
                                              qkT[r, 0:HP, bass.ds(SEQ + NQ * b, NQ)].rearrange("p (a o) q -> p a o q", o=2)[:, :, odd, :])
                nc.vector.tensor_copy(stat[0:ROWS, 56:57], cqr[:, bass.ds(b, 1)]).then_inc(qx_done, 1)
                for c in range(2):
                    keys_T(b, c)

            def output(b):
                dve.wait_ge(oT_hi, GR * 2 + 1 + b)
                for s in range(2):
                    for e in range(2):
                        r = slice(DH * e, DH * e + DH)
                        to = bass.ds(SEQ + NQ * b, NQ)
                        col = (2 * s + e) * NQ
                        src = ps[r, 6, s * ROWS:(s + 1) * ROWS].rearrange("p (j c) -> p j c", c=QR)[:, :, col:col + NQ]
                        last = nc.vector.tensor_tensor(aL[r, 0:HP, to].rearrange("p (j s) q -> p j s q", s=2)[:, :, s, :], src,
                                                       aH[r, 0:HP, to].rearrange("p (j s) q -> p j s q", s=2)[:, :, s, :].bitcast(F32), ALU.subtract)
                last.then_inc(stage_done, 1)

            def sequence(b, first, last_one):
                link(nc.vector.tensor_copy(maskb[:], mshift[:, bass.ds(NS - NQ - NQ * b, NS)]))
                keys_T(b, 2)
                for c in range(NCH):
                    if 2 < c + 1 < NCH:
                        keys_T(b, c + 1)
                    dve.wait_ge(sc_ready, NCH * b + c + 1)
                    nc.vector.tensor_scalar(S[:, c * KEYS:(c + 1) * KEYS], ps[0:ROWS, 3 + c % 2, 0:KEYS], stat[0:ROWS, 56:57], None,
                                            ALU.add).then_inc(sc_free, 1)
                    if c == 3 and not first:
                        output(b - 1)
                dve.wait_ge(sn_ready, b + 1)
                link(nc.vector.scalar_tensor_tensor(out=S[:, NPAST:NPAST + NS], in0=ps[0:ROWS, 5, 0:NS], scalar=stat[0:ROWS, 56:57],
                                                    in1=maskb[:], op0=ALU.add, op1=ALU.add))
                nc.vector.tensor_reduce(stat[0:ROWS, 60:61], S[:], AX_X, ALU.max, negate=True).then_inc(smax_done, 1)
                if not last_one:
                    begin(b + 1)
                dve.wait_ge(sexp_done, b + 1)
                link(nc.vector.reciprocal(stat[0:ROWS, 62:63], stat[0:ROWS, 61:62]))
                for g in range(4):
                    dve.wait_ge(pt_ready, 4 * b + g + 1)
                    n = min(5, NP - 5 * g)
                    last = nc.vector.tensor_copy(pTs[:, 5 * g:5 * g + n, :].rearrange("p k r -> p (k r)"), ps[:, 6 + g % 2, 0:n * ROWS])
                    if g == 3:
                        last = nc.vector.tensor_copy(pTs[0:NS, NP, :], ps[0:NS, 6 + g % 2, n * ROWS:(n + 1) * ROWS])
                    last.then_inc(pt_free, 1)
                dve.wait_ge(o_ready, b + 1)
                nc.vector.tensor_scalar(os_[:], ps[0:ROWS, 5, 0:4 * DH], stat[0:ROWS, 62:63], None, ALU.mult).then_inc(o_done, 1)
            begin(0)
            sequence(0, True, False)
            with dve.Fori(0, NB - 2) as i:
                steps.enter(i, 3)
                sequence(i + 1, False, False)
            steps.leave(NB - 2)
            sequence(NB - 1, False, True)
            output(NB - 1)
            lo(C_WO1)
            residual(C_WO1, 1, 3)
            norm(3)
            ffn(1)
            residual(C_DN1, 2, 4)
            for t in range(TT + 1):
                rows = P if t < TT else NS
                if t >= 2:
                    dve.wait_ge(y_stored[t % 2], 16 * (t // 2))
                for q in range(KD // 4):
                    bank = group()
                    nc.vector.tensor_copy(ystage[0:rows, t % 2, 4 * q * P:4 * (q + 1) * P], bank[0:rows, :]).then_inc(tr_free, 1)
                marks["y", t] = tr[0]

        @block.scalar
        def _(act):
            def hi(n0, i=0):
                s, size = n0 % 2, chunk_size(n0)
                act.wait_ge(raw_in[s], 16 * (n0 // 2 + 1) + 16 * i)
                if n0 >= 2:
                    act.wait_ge(w_used, n0 - 1 + 2 * i)
                nc.scalar.activation(wH[s][:, 0:size], raw[:, s, 0:size], ACT.Copy).then_inc(hi_done, 1)

            def square(r, j0, i=0):
                act.wait_ge(x_new, KD * (r - 1) + j0 + 1 + 2 * i)
                if j0 >= 2:
                    act.wait_ge(sq_added, (KD - 1) * (r - 1) + j0 - 1 + 2 * i)
                x = xT[:, bass.ds(j0 + 2 * i, 1), :].rearrange("p o n -> p (o n)")
                nc.scalar.activation(sq[:, j0 % 2], x, ACT.Square).then_inc(sq_done, 1)

            def norm(r):
                act.wait_ge(ss_ready, r + 1)
                nc.scalar.activation(halves(rb[:]), ps[:, 4:6, 0:HT], ACT.Sqrt, bias=eps[:, 0:1]).then_inc(norm_root, 1)
                for k in range(KD):
                    act.wait_ge(v_done, KD * r + k + 1)
                    nc.scalar.activation(aH[:, k], tmp[:, k % 2], ACT.Copy).then_inc(vH_done, 1)

            def head_tile(z0, i=0):
                chunk = z0 + (2 * KC if z0 < MP else C_FOX - MP)
                act.wait_ge(w_used, chunk + 1 + 2 * i)
                if z0 >= 2:
                    act.wait_ge(hn_done, z0 - 1 + 2 * i)
                nc.scalar.activation(halves(tmp[:, z0 % 2]), acc(z0 % 2), ACT.Copy)
                nc.scalar.activation(halves(sq[:, z0 % 2]), acc(z0 % 2), ACT.Square).then_inc(z_done, 1)

            def head_norm(z0, i=0):
                act.wait_ge(hn_ready, z0 + 1 + 2 * i)
                if z0:
                    act.wait_ge(hn_done, z0 + 2 * i)
                nc.scalar.activation(halves(rb[:]), ps[:, 4:6, 0:HT], ACT.Sqrt, bias=eps[:, 1:2]).then_inc(head_root, 1)

            def memory(l):
                mb = MBS[l]
                act.wait_ge(mem_in, 16 * (l + 1))
                for t in range(MT):
                    nc.scalar.activation(mb["prob"][:].rearrange("p a b n -> p (a b n)")[:, 0:D], mb["mem"][:, t],
                                         ACT.Square, accum_out=stat[:, 32 + t:33 + t]).then_inc(ms_done, 1)
                    act.wait_ge(ms_done, MT * l + t + 1)
                nc.scalar.activation(stat[:, 34:34 + MT], stat[:, 32:32 + MT], ACT.Sqrt, bias=eps[:, 0:1]).then_inc(mem_root, 1)
                for g in range(KD // 2):
                    act.wait_ge(tr_free, marks["memory", l, g])
                    nc.scalar.activation(mb["mH"][:, 2 * g:2 * g + 2, :].rearrange("p k n -> p (k n)"), tmp[:, g % 2, 0:2 * NM],
                                         ACT.Copy).then_inc(mH_done, 1)
                for i in range(N_MEM - l):
                    hi(C_MEM[l] + 1 + i)
                act.wait_ge(w_used, C_MEM[l] + N_MEM)
                nc.scalar.activation(mb["vm"][:], ps[:, 0:MT, MW:2 * MW], ACT.Copy)
                nc.scalar.activation(sq[:, :, 0:MW], ps[:, 0:MT, 0:MW], ACT.Square).then_inc(kvsq_done, 1)
                act.wait_ge(kss_done, l + 1)
                nc.scalar.activation(stat[:, 44:44 + MT * MH], stat[:, 36:36 + MT * MH], ACT.Sqrt, bias=eps[:, 1:2]).then_inc(k_root, 1)

            def exps(u, unit, mb):
                kind, hp, t, keys = unit
                st = stat[:, 8 * (u % 2):8 * (u % 2) + 8]
                act.wait_ge(at_max, u + 1)
                for e in range(2):
                    src = mb["prob"][:, u % 2, e, 0:keys] if kind == "fox" else ps[:, 2 * (u % 2) + e, 0:keys]
                    last = nc.scalar.activation(mb["prob"][:, u % 2, e, 0:keys], src, ACT.Exp, bias=st[:, e:e + 1],
                                                accum_out=st[:, 2 + e:3 + e])
                last.then_inc(at_exp, 1)

            def attend(u0, units, mb):
                for i in range(2):
                    exps(u0 + i, units[i], mb)
                for i, (kind, hp, t, keys) in enumerate(units):
                    u = u0 + i
                    if i + 2 < len(units):
                        exps(u + 2, units[i + 2], mb)
                    tile = hp if kind == "fox" else KC + hp
                    act.wait_ge(at_pv, u + 1)
                    nc.scalar.activation(aH[:, tile, t * P:(t + 1) * P], ps[:, 4 + u % 2, 0:P], ACT.Copy).then_inc(at_hi, 1)

            def sample_memory(l, u0):
                mb = MBS[l]
                for G in range(GR):
                    u = u0 + G
                    st = stat[:, 8 * (u % 2):8 * (u % 2) + 8]
                    act.wait_ge(at_max, u + 1)
                    nc.scalar.activation(mb["prob"][:, u % 2, 0, 0:NM], ps[:, 2 * (u % 2), 0:NM], ACT.Exp, bias=st[:, 0:1],
                                         accum_out=st[:, 2:3]).then_inc(at_exp, 1)
                    g = marks["sample memory", l, G]
                    act.wait_ge(tr_ready, g + 1)
                    bank = ps[:, 6 + g % 2, :]
                    for s in range(MP):
                        for e in range(2):
                            r = slice(DH * e, DH * e + DH)
                            src = bank[r, s * P:(s + 1) * P].rearrange("p (b h q) -> p b h q", b=GS, h=MH)[:, :, 2 * s + e, :]
                            to = slice(SEQ + G * GS * NQ, SEQ + (G + 1) * GS * NQ)
                            last = nc.scalar.activation(aH[r, KC + s, to].rearrange("p (b q) -> p b q", b=GS), src, ACT.Copy)
                    last.then_inc(oT_hi, 1)

            def residual(c0, per_tile, r):
                def tile(j0, i):
                    for s in range(per_tile):
                        n0 = c0 + per_tile * j0 + s + 1
                        if n0 < C_END:
                            hi(n0, i if per_tile == 1 else 2 * i)
                    if r < 4:
                        square(r, j0, i)
                for j in range(2):
                    tile(j, 0)
                with act.Fori(0, KD // 2 - 2) as i:
                    for j in range(2, 4):
                        tile(j, i)
                for j in range(KD - 2, KD):
                    tile(j, 0)

            def ffn(l):
                c0, g0 = C_GU[l], l * KF

                def tile(f0, i):
                    hi(c0 + 2 * f0 + 1, 2 * i)
                    hi(c0 + 2 * f0 + 2, 2 * i)
                    if g0 + f0 >= 2:
                        act.wait_ge(g_done, g0 + f0 - 1 + 2 * i)
                    nc.scalar.activation(halves(sq[:, f0 % 2]), acc(2 * (f0 % 2)), ACT.Silu).then_inc(silu_done, 1)
                    act.wait_ge(g_done, g0 + f0 + 1 + 2 * i)
                    f = bass.ds(f0 + 2 * i, 1)
                    nc.scalar.activation(gH[:, f, :].rearrange("p o n -> p (o n)"), tmp[:, f0 % 2], ACT.Copy).then_inc(gH_done, 1)
                for f in range(2):
                    tile(f, 0)
                with act.Fori(0, KF2 - 2) as i:
                    for f in range(2, 4):
                        tile(f, i)
                for f in range(KF - 2, KF):
                    tile(f, 0)

            xp = x_prompt[0].rearrange("(t p) n -> p t n", p=P)
            for t in range(TT):
                act.dma_start(xin[:, t], xp[:, t]).then_inc(x_in, 16)
            act.dma_start(xin[0:NS, TT], x_sample.rearrange("b q n -> (b q) n")).then_inc(x_in, 16)
            loads = 0
            for at_row, v in ((V_N1, norm1), (V_N2, norm2), (V_MEM, mem_norm), (V_DWB, conv_dw_b), (V_LNG, conv_ln_g), (V_LNB, conv_ln_b)):
                rows = v.rearrange("l (k n) -> (l k) n", n=P)
                act.dma_start(vrow[at_row:at_row + rows.shape[0], :], rows).then_inc(vec_in, 16)
                loads += 1
            for row, v in ((V_MQ, mem_q_norm[0:1]), (V_MQ + 1, mem_q_norm[1:2]), (V_MQ + 2, fox_q_norm), (V_MQ + 3, fox_k_norm)):
                for e in range(2):
                    act.dma_start(vrow[row:row + 1, DH * e:DH * e + DH], v).then_inc(vec_in, 16)
                    loads += 1
            act.dma_start(dwrow[:], conv_dw[0]).then_inc(vec_in, 16)
            for l in range(2):
                act.dma_start(gk_row[:, l, :], mem_k_norm[l:l + 1, :].broadcast_to([P, DH])).then_inc(vec_in, 16)
            act.dma_start(bf[:], fox_b_f.rearrange("o h -> h o")).then_inc(vec_in, 16)
            assert loads + 4 == VEC_LOADS
            for G in range(GR):
                act.dma_start(crow[:, G, :], cache_conv[0, G * GS:(G + 1) * GS].rearrange("b n c -> (b n) c")).then_inc(hist_in, 16)

            act.wait_ge(consts, CONSTS0)
            hi(0)
            for j in range(KD):
                act.wait_ge(tr_free, 2 * (TT + 1))
                if j >= 2:
                    act.wait_ge(sq_used, j - 1)
                nc.scalar.activation(sq[:, j % 2], xT[:, j], ACT.Square).then_inc(sq_done, 1)
            norm(0)

            def y_begin(c0, i=0):
                c = c0 + 2 * i
                act.wait_ge(taps_ready, c0 + 1 + 2 * i)
                bias = vec[:, bass.ds(V_DWB + c0 + 2 * i, 1)]
                y = yc[:, bass.ds(c, 1), :].rearrange("p o n -> p (o n)")
                nc.scalar.activation(y[:, 0:SEQ], ps[:, 4 * (c0 % 2), 0:SEQ], ACT.Identity, bias=bias)
                nc.scalar.activation(y[:, SEQ:T], ps[:, 4 * (c0 % 2) + 1, 0:NS], ACT.Identity, bias=bias).then_inc(y_begun, 1)

            def gate(c0, i=0):
                act.wait_ge(w_used, 2 * c0 + 2 + 4 * i)
                if c0 >= 2:
                    act.wait_ge(u_done, c0 - 1 + 2 * i)
                nc.scalar.activation(halves(sq[:, c0 % 2]), acc(2 * (c0 % 2) + 1), ACT.Sigmoid).then_inc(sig_done, 1)
                hi(C_CONV + 2 * c0 + 3, 2 * i)
                if c0:
                    y_begin(c0 - 1, i)
                if c0 < KC - 1:
                    hi(C_CONV + 2 * c0 + 4, 2 * i)
            for n in range(1, 3):
                hi(C_CONV + n)
            for c in range(2):
                gate(c)
            with act.Fori(0, KC // 2 - 2) as i:
                for c in range(2, 4):
                    gate(c, i)
            gate(KC - 2)
            gate(KC - 1)
            y_begin(KC - 1)
            hi(C_CONV + 2 * KC + 2)
            for z in range(MP):
                if z == 0:
                    act.wait_ge(u_done, KC)
                head_tile(z)
                if z:
                    head_norm(z - 1)
            head_norm(MP - 1)
            for c in range(KC):
                last = nc.scalar.activation(usc[:, c], uS[:, c, :, NQ:NQ + H], ACT.Copy)
            last.then_inc(usc_done, 1)
            memory(0)
            attend(0, MEM_UNITS, mb0)
            sample_memory(0, len(MEM_UNITS))
            for c in range(KC):
                act.wait_ge(lny_done, c + 1)
                if c >= 2:
                    act.wait_ge(ysq_used, c - 1)
                nc.scalar.activation(sq[:, c % 2], yc[:, c], ACT.Square).then_inc(ysq_done, 1)
            act.wait_ge(ln_ready, 2)
            nc.scalar.activation(halves(rb[:]), ps[:, 2:4, 0:HT], ACT.Sqrt, bias=eps[:, 2:3], scale=1.0 / CH).then_inc(ln_root, 1)
            for c in range(KC):
                act.wait_ge(lny_done, KC + c + 1)
                nc.scalar.activation(yc[:, c], yc[:, c], ACT.Silu, bias=vec[:, V_LNB + c:V_LNB + c + 1]).then_inc(swish_done, 1)
                act.wait_ge(swish_done, c + 1)
                nc.scalar.activation(aH[:, c], yc[:, c], ACT.Copy).then_inc(mixf_done, 1)
            residual(C_WO0, 1, 1)
            norm(1)
            ffn(0)
            residual(C_DN0, 2, 2)
            norm(2)

            Z = MP
            hi(C_FOX + 1)
            act.wait_ge(w_used, C_FOX + 1)
            nc.scalar.activation(tmp[0:NH, Z % 2, :].rearrange("p (a n) -> p a n", a=2), acc(Z % 2)[0:NH], ACT.Identity,
                                 bias=bf[:, 0:1]).then_inc(z_done, 1)
            hi(C_FOX + 2)
            head_tile(Z + 1)
            act.wait_ge(zab_done, 1)
            nc.scalar.activation(work[:, 1], work[:, 1], ACT.Exp, scale=-1.0).then_inc(e_done, 1)

            def head_pass(z0, i=0):
                hi(z0 - Z + C_FOX + 1, i)
                head_tile(z0, i)
                head_norm(z0 - 1, i)
            with act.Fori(0, HP) as i:
                for z in range(2):
                    head_pass(Z + 2 + z, i)
            for n in range(2 * HP + 2, N_FOX):
                if n - 1 <= 3 * HP:
                    hi(C_FOX + n + 1)
                    head_tile(Z + n)
                else:
                    head_pass(Z + n)
            head_norm(Z + N_FOX - 1)
            memory(1)
            u = len(MEM_UNITS) + GR
            attend(u, MEM_UNITS, mb1)
            sample_memory(1, u + len(MEM_UNITS))
            u += len(MEM_UNITS) + GR
            attend(u, FOX_UNITS, mb1)

            def keys_T(b, c):
                for g in (1, 2):
                    act.wait_ge(kt_ready, 3 * (NCH * b + c) + g + 1)
                    if g == 1 and (c >= 2 or not (isinstance(b, int) and b == 0)):
                        act.wait_ge(sc_ready, NCH * b + c - 1)
                    nc.scalar.activation(kT[:, c % 2, 2 * g:2 * g + 2, :].rearrange("p a n -> p (a n)"), ps[:, g, :],
                                         ACT.Copy).then_inc(kt_ev_a, 1)

            def output(b):
                act.wait_ge(oT_ready, b + 1)
                for s in range(2):
                    for e in range(2):
                        r = slice(DH * e, DH * e + DH)
                        to = bass.ds(SEQ + NQ * b, NQ)
                        col = (2 * s + e) * NQ
                        src = ps[r, 6, s * ROWS:(s + 1) * ROWS].rearrange("p (j c) -> p j c", c=QR)[:, :, col:col + NQ]
                        last = nc.scalar.activation(aH[r, 0:HP, to].rearrange("p (j s) q -> p j s q", s=2)[:, :, s, :], src, ACT.Copy)
                last.then_inc(oT_hi, 1)

            def sequence(b, first, last_one):
                for c in range(2, NCH):
                    keys_T(b, c)
                    if c == 4 and not first:
                        output(b - 1)
                if not last_one:
                    keys_T(b + 1, 0)
                act.wait_ge(smax_done, b + 1)
                nc.scalar.activation(S[:], S[:], ACT.Exp, bias=stat[0:ROWS, 60:61],
                                     accum_out=stat[0:ROWS, 61:62]).then_inc(sexp_done, 1)
                if not last_one:
                    keys_T(b + 1, 1)
            for c in range(2):
                keys_T(0, c)
            sequence(0, True, False)
            with act.Fori(0, NB - 2) as i:
                sequence(i + 1, False, False)
            sequence(NB - 1, False, True)
            output(NB - 1)
            hi(C_WO1)
            residual(C_WO1, 1, 3)
            norm(3)
            ffn(1)
            residual(C_DN1, 2, 4)

        @block.tensor
        def _(pe):
            tr = [0]

            def transposes(jobs):
                g = tr[0]
                tr[0] += 1
                if g >= 2:
                    pe.wait_ge(tr_free, g - 1)
                col = 0
                for src in jobs:
                    n, m = src.shape[0], 1
                    for x in src.shape[1:]:
                        m *= x
                    last = nc.tensor.transpose(ps[0:m, 6 + g % 2, col:col + n], src, ident[0:n, 0:n])
                    col += n
                last.then_inc(tr_ready, 1)
                return g

            def product(n0, i, slot, H_, L_, k0, ks, first, last, ready=None):
                s = n0 % 2
                pe.wait_ge(lo_done, n0 + 1 + 2 * i)
                for k in range(ks):
                    if ready is not None:
                        pe.wait_ge(a_ready, ready + k + 1)
                    w = slice(k * P, (k + 1) * P)
                    for weights, acts in ((wH[s], (H_, L_)), (wL[s], (H_,))):
                        for a in acts:
                            for h in range(2):
                                mm = nc.tensor.matmul(ps[:, 2 * slot + h, 0:HT], weights[:, w], a[:, k0 + k, h * HT:(h + 1) * HT],
                                                      start=(first and k == 0 and weights is wH[s] and a is H_),
                                                      stop=(last and k == ks - 1 and weights is wL[s]))
                mm.then_inc(w_used, 1)

            def sum_squares(r):
                pe.wait_ge(sq_added, (KD - 1) * r)
                pe.wait_ge(sq_done, KD * (r + 1))
                for n, src in enumerate((rb[:], sq[:, (KD - 1) % 2])):
                    for h in range(2):
                        mm = nc.tensor.matmul(ps[:, 4 + h, 0:HT], ones[:], src[:, h * HT:(h + 1) * HT], start=(n == 0), stop=(n == 1))
                mm.then_inc(ss_ready, 1)

            def residual(c0, per_tile, r, k0s):
                def tile(j0, i=0):
                    if j0 >= 2:
                        pe.wait_ge(x_new, KD * (r - 1) + j0 - 1 + 2 * i)
                    H_, L_ = (aH, aL) if per_tile == 1 else (gH, gL)
                    for s in range(per_tile):
                        product(c0 + per_tile * j0 + s, i if per_tile == 1 else 2 * i, j0 % 2, H_, L_, k0s[s],
                                KD if per_tile == 1 else KF2, s == 0, s == per_tile - 1)
                tile(0)
                tile(1)
                with pe.Fori(0, KD // 2 - 1) as i:
                    for j in range(2, 4):
                        tile(j, i)
                if r < 4:
                    sum_squares(r)

            def ffn(l):
                c0, g0 = C_GU[l], l * KF

                def tile(f0, i=0, ready=None):
                    if g0 + f0 >= 2:
                        pe.wait_ge(g_done, g0 + f0 - 1 + 2 * i)
                    for s in range(2):
                        product(c0 + 2 * f0 + s, 2 * i, 2 * (f0 % 2) + s, aH, aL, 0, KD, True, True, None if s else ready)
                tile(0, ready=KD * (2 * l + 1))
                tile(1)
                with pe.Fori(0, KF2 - 1) as i:
                    for f in range(2, 4):
                        tile(f, i)
                pe.wait_ge(gL_done, KF * (l + 1))

            def head_sums(z0, i=0):
                pe.wait_ge(z_done, z0 + 1 + 2 * i)
                if z0:
                    pe.wait_ge(hn_done, z0 + 2 * i)
                for h in range(2):
                    mm = nc.tensor.matmul(ps[:, 4 + h, 0:HT], blocks[:], sq[:, z0 % 2, h * HT:(h + 1) * HT], start=True, stop=True)
                mm.then_inc(hn_ready, 1)

            def memory(l):
                mb = MBS[l]
                pe.wait_ge(mn_done, l + 1)
                for g in range(KD // 2):
                    transposes([mb["mem"][:, t, k * P:(k + 1) * P] for k in (2 * g, 2 * g + 1) for t in range(MT)])
                for i in range(N_MEM):
                    n = C_MEM[l] + i
                    pe.wait_ge(lo_done, n + 1)
                    pe.wait_ge(mL_done, l * KD // 2 + (KM * i + KM - 1) // 2 + 1)
                    for kk in range(KM):
                        k = KM * i + kk
                        w = slice(kk * 2 * MW, (kk + 1) * 2 * MW)
                        for t in range(MT):
                            for m_, w_ in ((mb["mH"], wH), (mb["mH"], wL), (mb["mL"], wH)):
                                mm = nc.tensor.matmul(ps[:, t, :], m_[:, k, t * P:(t + 1) * P], w_[n % 2][:, w],
                                                      start=(k == 0 and m_ is mb["mH"] and w_ is wH),
                                                      stop=(k == KD - 1 and m_ is mb["mL"]))
                    mm.then_inc(w_used, 1)
                pe.wait_ge(kv_done, l + 1)
                transposes([mb["km"][:, t, hp * P:(hp + 1) * P] for hp in range(MP) for t in range(MT)])

            def scores(u, unit, mb):
                kind, hp, t, keys = unit
                if u >= 2:
                    pe.wait_ge(at_exp, u - 1)
                for e in range(2):
                    r = slice(DH * e, DH * e + DH)
                    q = qkT[r, hp, t * P:(t + 1) * P] if kind == "fox" else mb["qm"][r, hp, t * P:(t + 1) * P]
                    k = qkT[r, HP + hp, 0:keys] if kind == "fox" else mb["kmT"][r, hp, :]
                    out = ps[:, 2 * (u % 2) + e, 0:keys]
                    mm = nc.tensor.matmul(out, q, k, start=True, stop=True)
                mm.then_inc(at_s, 1)

            def broadcast_c(hp):
                for e in range(2):
                    pe.wait_ge(tr_free, tr[0] - 1)
                    h = 2 * hp + e
                    nc.tensor.matmul(ps[:, 6 + tr[0] % 2, :], ident[0:DH, h:h + 1].broadcast_to([DH, P]), ncT[0:DH, :],
                                     start=True, stop=True).then_inc(tr_ready, 1)
                    tr[0] += 1

            def attend(u0, units, mb):
                if units[0][0] == "fox":
                    broadcast_c(0)
                for i in range(2):
                    scores(u0 + i, units[i], mb)
                for i, (kind, hp, t, keys) in enumerate(units):
                    u = u0 + i
                    pe.wait_ge(at_prob, u + 1)
                    if kind == "mem":
                        transposes([mb["prob"][:, u % 2, e, k * P:(k + 1) * P] for e in range(2) for k in range(MT)])
                    else:
                        for e in range(2):
                            transposes([mb["prob"][:, u % 2, e, k * P:(k + 1) * P] for k in range(t + 1)])
                    if i + 2 < len(units):
                        scores(u + 2, units[i + 2], mb)
                    pe.wait_ge(tr_free, tr[0])
                    if u >= 2:
                        pe.wait_ge(at_lo, u - 1)
                    n = keys // P
                    for k in range(n):
                        for e in range(2):
                            head = slice((2 * hp + e) * DH, (2 * hp + e + 1) * DH)
                            v = vtok[:, k, head] if kind == "fox" else mb["vm"][:, k, head]
                            mm = nc.tensor.matmul(ps[DH * e:DH * e + DH, 4 + u % 2, 0:P], v, mb["pT"][:, e, k, :],
                                                  start=(k == 0), stop=(k == n - 1))
                    mm.then_inc(at_pv, 1)
                    if kind == "fox" and t == 0 and hp + 1 < HP:
                        broadcast_c(hp + 1)

            def sample_memory(l, u0):
                mb = MBS[l]
                for G in range(GR):
                    u = u0 + G
                    pe.wait_ge(ks_in, 32 * (GR * l + G + 1))
                    for b in range(GS):
                        transposes([mb["ks"][:, b, k, hp * P:(hp + 1) * P] for hp in range(MP) for k in range(MT)])
                    pe.wait_ge(qd_done, GR * l + G + 1)
                    pe.wait_ge(tr_free, tr[0])
                    pe.wait_ge(at_exp, u - 1)
                    for hp in range(MP):
                        for b in range(GS):
                            mm = nc.tensor.matmul(ps[QR * b:QR * b + QR, 2 * (u % 2), 0:NM], mb["qd"][:, b, hp, :], mb["ksT"][:, b, hp, :],
                                                  start=(hp == 0), stop=(hp == MP - 1), skip_group_check=True, tile_position=(0, QR * b))
                    mm.then_inc(at_s, 1)
                    pe.wait_ge(at_prob, u + 1)
                    transposes([mb["prob"][:, u % 2, 0, k * P:(k + 1) * P] for k in range(MT)])
                    pe.wait_ge(tr_free, tr[0])
                    pe.wait_ge(at_lo, u - 1)
                    for k in range(MT):
                        for b in range(GS):
                            mm = nc.tensor.matmul(ps[QR * b:QR * b + QR, 4 + u % 2, 0:MW], mb["pT"][:, 0, k, QR * b:QR * b + QR],
                                                  mb["vs"][:, b, k, :], start=(k == 0), stop=(k == MT - 1), skip_group_check=True,
                                                  tile_position=(0, QR * b))
                    mm.then_inc(at_pv, 1)
                    pe.wait_ge(at_lo, u + 1)
                    transposes([mb["o"][:, s * P:(s + 1) * P] for s in range(MP)])

            pe.wait_ge(consts, CONSTS0)
            pe.wait_ge(x_in, 16 * (TT + 1))
            for t in range(TT + 1):
                rows = P if t < TT else NS
                for q in range(KD // 4):
                    transposes([xin[0:rows, t, k * P:(k + 1) * P] for k in range(4 * q, 4 * q + 4)])
            for j in range(KD):
                pe.wait_ge(sq_done, j + 1)
                for h in range(2):
                    mm = nc.tensor.matmul(ps[:, 4 + h, 0:HT], ones[:], sq[:, j % 2, h * HT:(h + 1) * HT], start=(j == 0), stop=(j == KD - 1))
                mm.then_inc(sq_used if j < KD - 1 else ss_ready, 1)
            pe.wait_ge(vec_in, 16 * VEC_LOADS)
            transposes([vrow[:]])
            transposes([dwrow[:, c * P:(c + 1) * P] for c in range(KC)])
            pe.wait_ge(hist_in, 16 * GR)
            for G in range(GR):
                for first, count in ((0, 4), (4, KC - 4)):
                    transposes([crow[:, G, c * P:(c + 1) * P] for c in range(first, first + count)])


            def conv_tile(c0, i=0, ready=None):
                if c0 >= 2:
                    pe.wait_ge(y_begun, c0 - 1 + 2 * i)
                for s in range(2):
                    product(C_CONV + 2 * c0 + s, 2 * i, 2 * (c0 % 2) + s, aH, aL, 0, KD, True, True, None if s else ready)

            def taps(c0, i=0):
                pe.wait_ge(u_done, c0 + 1 + 2 * i)
                pe.wait_ge(diag_ready, c0 + 1 + 2 * i)
                c = bass.ds(c0 + 2 * i, 1)
                for j in range(PE_TAPS):
                    uj = uP[:, c, j:j + SEQ].rearrange("p o n -> p (o n)")
                    sj = uS[:, c, :, j:j + NQ].rearrange("p o b n -> p (o b) n")
                    nc.tensor.matmul(ps[:, 4 * (c0 % 2), 0:SEQ], diag[:, c0 % 2, j], uj, start=(j == 0), stop=(j == PE_TAPS - 1))
                    mm = nc.tensor.matmul(ps[:, 4 * (c0 % 2) + 1, 0:NS].rearrange("p (b n) -> p b n", b=NB), diag[:, c0 % 2, j], sj,
                                          start=(j == 0), stop=(j == PE_TAPS - 1))
                mm.then_inc(taps_ready, 1)
            conv_tile(0, ready=0)
            pe.wait_ge(tr_free, tr[0])
            conv_tile(1)
            taps(0)
            with pe.Fori(0, KC // 2 - 1) as i:
                for c in range(2, 4):
                    conv_tile(c, i)
                    taps(c - 1, i)
            taps(KC - 1)
            pe.wait_ge(y_begun, KC)
            for z in range(MP):
                product(C_CONV + 2 * KC + z, 0, z % 2, aH, aL, 0, KD, True, True)
                if z:
                    head_sums(z - 1)
            head_sums(MP - 1)
            for first, count in ((0, 4), (4, KC - 4)):
                transposes([uP[:, c, SEQ:SEQ + H] for c in range(first, first + count)])
            pe.wait_ge(usc_done, 1)
            for G in range(GR):
                for first, count in ((0, 4), (4, KC - 4)):
                    transposes([usc[:, c, G * GS:(G + 1) * GS, :].rearrange("p b n -> p (b n)") for c in range(first, first + count)])
            pe.wait_ge(z_done, MP)
            memory(0)
            pe.wait_ge(hn_done, MP)
            pe.wait_ge(tr_free, tr[0])
            attend(0, MEM_UNITS, mb0)
            sample_memory(0, len(MEM_UNITS))
            pe.wait_ge(y_done, KC)
            pe.wait_ge(at_exp, len(MEM_UNITS) + GR)
            for source, bank in ((yc, 0), (sq, 2)):
                for c in range(KC):
                    if bank:
                        pe.wait_ge(ysq_done, c + 1)
                    src = yc[:, c] if not bank else sq[:, c % 2]
                    for h in range(2):
                        mm = nc.tensor.matmul(ps[:, bank + h, 0:HT], ones[:], src[:, h * HT:(h + 1) * HT], start=(c == 0), stop=(c == KC - 1))
                    if bank and c < KC - 1:
                        mm.then_inc(ysq_used, 1)
                mm.then_inc(ln_ready, 1)
            pe.wait_ge(stage_done, KC)
            pe.wait_ge(tr_free, tr[0])
            residual(C_WO0, 1, 1, (0,))
            ffn(0)
            residual(C_DN0, 2, 2, (0, KF2))

            Z = MP

            def tile(z0, i=0, ready=None):
                pe.wait_ge(z_done, z0 - 1 + 2 * i)
                product(C_FOX - Z + z0, i, z0 % 2, aH, aL, 0, KD, True, True, ready)
            tile(Z, ready=KD * 2)
            tile(Z + 1)
            pe.wait_ge(z_done, Z + 1)
            pe.wait_ge(hn_done, Z)
            for t in range(TT + 1):
                n = P if t < TT else NS
                mm = nc.tensor.transpose(ps[0:n, 4, t * NH:(t + 1) * NH], tmp[0:NH, Z % 2, t * P:t * P + n], ident[0:NH, 0:NH])
            mm.then_inc(hn_ready, 1)
            with pe.Fori(0, HP - 1) as i:
                for n in range(2, 4):
                    tile(Z + n, i)
                    head_sums(Z + n - 1, i)
            tile(Z + 2 * HP)
            head_sums(Z + 2 * HP - 1)
            for n in range(2 * HP + 1, N_FOX + 1):
                if n < N_FOX:
                    tile(Z + n)
                z = Z + n - 1
                if n - 1 in range(2 * HP + 1, 3 * HP + 1):
                    pe.wait_ge(z_done, z + 1)
                    pe.wait_ge(hn_done, z)
                    for t in range(TT + 1):
                        m = P if t < TT else NS
                        mm = nc.tensor.transpose(ps[0:m, 4 + t // TT, (t % TT) * P:(t % TT + 1) * P],
                                                 tmp[:, z % 2, t * P:t * P + m], ident[:])
                    mm.then_inc(hn_ready, 1)
                else:
                    head_sums(z)
            pe.wait_ge(hn_done, Z + N_FOX)
            for t in range(TT + 1):
                n = P if t < TT else NS
                for first, count in ((0, 4), (4, HP - 4)):
                    transposes([qkT[:, HP + hp, t * P:t * P + n] for hp in range(first, first + count)])
            pe.wait_ge(c_ready, 1)
            pe.wait_ge(tr_free, tr[0] - 1)
            out = ps[:, 6 + tr[0] % 2, :]
            tr[0] += 1
            for t in range(TT):
                for s in range(t + 1):
                    mm = nc.tensor.matmul(out[:, t * NH:(t + 1) * NH], win[:, (TT - 1 - s + t) * P:(TT - s + t) * P], lf[:, s, :],
                                          start=(s == 0), stop=(s == t))
            nc.tensor.matmul(out[0:NS, TT * NH:(TT + 1) * NH], sameq[:], lf[0:NS, TT, :], start=True, stop=True).then_inc(tr_ready, 1)
            pe.wait_ge(tr_free, tr[0] - 1)
            out = ps[:, 6 + tr[0] % 2, :]
            tr[0] += 1
            for s in range(TT):
                mm = nc.tensor.matmul(out, lfd[:, s, :], win[:, (TT - 1 - s) * P:(TT - 1 - s) * P + SEQ], start=(s == 0), stop=(s == TT - 1))
            mm.then_inc(tr_ready, 1)
            pe.wait_ge(c_done, 1)
            pe.wait_ge(tr_free, tr[0] - 1)
            out = ps[:, 6 + tr[0] % 2, :]
            tr[0] += 1
            nc.tensor.matmul(out[0:ROWS, 0:NB], cqA[:].rearrange("p h q -> p (h q)"), bm[:], start=True, stop=True)
            nc.tensor.transpose(out[0:ROWS, NB:NB + 2 * NS - NQ], mshT[:], ident[0:2 * NS - NQ, 0:2 * NS - NQ]).then_inc(tr_ready, 1)
            memory(1)
            pe.wait_ge(tr_free, tr[0])
            u = len(MEM_UNITS) + GR
            attend(u, MEM_UNITS, mb1)
            sample_memory(1, u + len(MEM_UNITS))
            u += len(MEM_UNITS) + GR
            pe.wait_ge(lf_in, 16 * NB * NP)
            for g in range(NH // 4):
                transposes([lfrow[:].rearrange("n (k h) -> n h k", h=NH)[:, h, :] for h in range(4 * g, 4 * g + 4)])
            pe.wait_ge(tr_free, tr[0])
            pe.wait_ge(lftot_done, 1)
            for g in range(NH // 4):
                pe.wait_ge(tr_free, tr[0] - 1)
                out = ps[:, 6 + tr[0] % 2, :]
                tr[0] += 1
                for h in range(4):
                    nc.tensor.matmul(out[:, h * P:(h + 1) * P], after[:], lfT[:, 4 * g + h, :], start=True, stop=False)
                    mm = nc.tensor.matmul(out[:, h * P:(h + 1) * P], lftot[:, 4 * g + h:4 * g + h + 1].broadcast_to([P, P]), later[:],
                                          start=False, stop=True)
                mm.then_inc(tr_ready, 1)
            attend(u, FOX_UNITS, mb1)
            pe.wait_ge(at_lo, u + len(FOX_UNITS))
            pe.wait_ge(tr_free, tr[0])

            def keys_T(b, c):
                pe.wait_ge(k_in[c % RING], 32 * (NCH // RING * b + c // RING + 1))
                if c or not (isinstance(b, int) and b == 0):
                    pe.wait_ge(kt_ev_v, NCH * b + c)
                    pe.wait_ge(kt_ev_a, 2 * (NCH * b + c))
                for g in range(3):
                    for n in range(4):
                        hp, pp = (4 * g + n) // 2, n % 2
                        mm = nc.tensor.transpose(ps[:, g, n * P:(n + 1) * P], kring[c % RING][:, pp, hp * P:(hp + 1) * P], ident[:])
                    mm.then_inc(kt_ready, 1)

            def step_scores(b, c):
                pe.wait_ge(kt_ev_v, NCH * b + c + 1)
                pe.wait_ge(kt_ev_a, 2 * (NCH * b + c + 1))
                pe.wait_ge(rx_done, NCH * b + c + 1)
                if c >= 2 or not (isinstance(b, int) and b == 0):
                    pe.wait_ge(sc_free, NCH * b + c - 1)
                for odd in range(2):
                    for j in range(3):
                        mm = nc.tensor.matmul(ps[QR * j:QR * j + QR, 3 + c % 2, 0:KEYS], qx[:, 2 * j + odd, :], kT[:, c % 2, 2 * j + odd, :],
                                              start=(odd == 0), stop=False, skip_group_check=True, tile_position=(0, QR * j))
                for pp in range(CPG):
                    for j in range(3):
                        r = rx[:, c % 2, pp, 4 * j:4 * j + 4, :].rearrange("p h q -> p (h q)")
                        mm = nc.tensor.matmul(ps[QR * j:QR * j + QR, 3 + c % 2, pp * P:(pp + 1) * P], r, ident[:],
                                              start=False, stop=(pp == CPG - 1), skip_group_check=True, tile_position=(0, QR * j))
                mm.then_inc(sc_ready, 1)

            def begin(b):
                keys_T(b, 0)
                keys_T(b, 1)
                pe.wait_ge(qx_done, b + 1)
                step_scores(b, 0)
                step_scores(b, 1)

            def output(b):
                pe.wait_ge(o_done, b + 1)
                for s in range(2):
                    mm = nc.tensor.transpose(ps[:, 6, s * ROWS:(s + 1) * ROWS], os_[:, s * P:(s + 1) * P], ident[0:ROWS, 0:ROWS])
                mm.then_inc(oT_ready, 1)

            def sequence(b, first, last_one):
                keys_T(b, 2)
                for c in range(2, NCH):
                    if c + 1 < NCH:
                        keys_T(b, c + 1)
                    if c == 3 and not first:
                        output(b - 1)
                    step_scores(b, c)
                for odd in range(2):
                    for j in range(3):
                        nc.tensor.matmul(ps[QR * j:QR * j + QR, 5, 0:NS], qx[:, 2 * j + odd, :], qkT[:, HP + 2 * j + odd, SEQ:T],
                                         start=(odd == 0), stop=False, skip_group_check=True, tile_position=(0, QR * j))
                for j in range(3):
                    c_k = ncx[:, 4 * j:4 * j + 4, :].rearrange("p h q -> p (h q)")
                    mm = nc.tensor.matmul(ps[QR * j:QR * j + QR, 5, 0:NS], c_k, ident[0:NS, 0:NS], start=False, stop=True,
                                          skip_group_check=True, tile_position=(0, QR * j))
                mm.then_inc(sn_ready, 1)
                if not last_one:
                    begin(b + 1)
                pe.wait_ge(sexp_done, b + 1)
                for g in range(4):
                    if g >= 2:
                        pe.wait_ge(pt_free, 4 * b + g - 1)
                    elif g == 0:
                        pe.wait_ge(stage_done, KC + b)
                    n = min(5, NP - 5 * g)
                    for x in range(n):
                        k = 5 * g + x
                        mm = nc.tensor.transpose(ps[:, 6 + g % 2, x * ROWS:(x + 1) * ROWS], S[:, k * P:(k + 1) * P], ident[0:ROWS, 0:ROWS])
                    if g == 3:
                        mm = nc.tensor.transpose(ps[0:NS, 6 + g % 2, n * ROWS:(n + 1) * ROWS], S[:, NPAST:NPAST + NS], ident[0:ROWS, 0:ROWS])
                    mm.then_inc(pt_ready, 1)
                for c in range(NCH):
                    pe.wait_ge(v_in[c % RING], 32 * (NCH // RING * b + c // RING + 1))
                    pe.wait_ge(pt_free, 4 * b + (CPG * c + CPG - 1) // 5 + 1)
                    for pp in range(CPG):
                        for j in range(3):
                            k = CPG * c + pp
                            mm = nc.tensor.matmul(ps[QR * j:QR * j + QR, 5, 0:4 * DH], pTs[:, k, QR * j:QR * j + QR],
                                                  vring[c % RING][:, pp, 4 * DH * j:4 * DH * (j + 1)], start=(k == 0), stop=False,
                                                  skip_group_check=True, tile_position=(0, QR * j))
                    mm.then_inc(v_used, 1)
                for j in range(3):
                    mm = nc.tensor.matmul(ps[QR * j:QR * j + QR, 5, 0:4 * DH], pTs[0:NS, NP, QR * j:QR * j + QR],
                                          vtok[0:NS, TT, 4 * DH * j:4 * DH * (j + 1)], start=False, stop=True,
                                          skip_group_check=True, tile_position=(0, QR * j))
                mm.then_inc(o_ready, 1)
            begin(0)
            sequence(0, True, False)
            with pe.Fori(0, NB - 2) as i:
                sequence(i + 1, False, False)
            sequence(NB - 1, False, True)
            output(NB - 1)
            pe.wait_ge(stage_done, KC + NB)
            residual(C_WO1, 1, 3, (0,))
            ffn(1)
            residual(C_DN1, 2, 4, (0, KF2))
            pe.wait_ge(x_new, KD * 4)
            for t in range(TT + 1):
                n = P if t < TT else NS
                for q in range(KD // 4):
                    transposes([xT[:, k, t * P:t * P + n] for k in range(4 * q, 4 * q + 4)])

        @block.sync
        def _(sp):
            def load(n0, src, i=0):
                s = n0 % 2
                if n0 >= 2:
                    sp.wait_ge(lo_done, n0 - 1 + 2 * i)
                size = src.shape[1] * src.shape[2]
                sp.dma_start(raw[:, s, 0:size].rearrange("p (k n) -> p k n", k=src.shape[1]), src).then_inc(raw_in[s], 16)

            def mem_chunks(l):
                for i in range(N_MEM):
                    load(C_MEM[l] + i, w_mem_kv[l].rearrange("(k p) n -> p k n", p=P)[:, KM * i:KM * i + KM, :])

            def out_chunks(l):
                with sp.Fori(0, KD // 2) as i:
                    for j in range(2):
                        load(C_WO[l] + j, columns(w_out[l], j * P + 2 * P * i), i)

            def ffn_chunks(l):
                with sp.Fori(0, KF) as f:
                    load(C_GU[l], columns(w_gate_up[l], P * f), f)
                    load(C_GU[l] + 1, columns(w_gate_up[l], DF + P * f), f)
                with sp.Fori(0, KD) as j:
                    for s in range(2):
                        load(C_DN[l] + s, columns(w_down[l], P * j, s * KF2, KF2), j)

            def conv_pair(c0, i):
                load(C_CONV + 2 * c0, columns(conv_w_in[0], c0 * P + P * i), i)
                load(C_CONV + 2 * c0 + 1, columns(conv_w_in[0], CH + c0 * P + P * i), i)
            conv_pair(0, 0)
            with sp.Fori(0, KC - 1) as i:
                conv_pair(1, i)
            for z in range(MP):
                load(C_CONV + 2 * KC + z, columns(conv_w_in[0], 2 * CH + z * P))
            mem_chunks(0)
            out_chunks(0)
            ffn_chunks(0)
            w = fox_w_in[0]
            load(C_FOX, columns(w, 3 * CH))
            with sp.Fori(0, 3 * HP // 2) as i:
                for j in range(2):
                    load(C_FOX + 1 + j, columns(w, j * P + 2 * P * i), i)
            for z in range(MP):
                load(C_FOX + 1 + 3 * HP + z, columns(w, 3 * CH + NH + z * P))
            mem_chunks(1)
            sp.wait_ge(pages_in, 16)
            sp.wait_ge(w_used, C_WO1)

            def keys(c, first, read=None):
                which = [sp.value_load(pages[0:1, bass.ds(first + CPG * c + pp, 1)], min_val=0, max_val=N_PHYS - 1) for pp in range(CPG)]
                if read is not None:
                    sp.wait_ge(kt_ready, read)
                for pp in range(CPG):
                    sp.dma_start(kring[c % RING][:, pp, :], cache_fox_k[0, bass.ds(which[pp], 1)].rearrange("o p h d -> (o p) (h d)"))\
                      .then_inc(k_in[c % RING], 16)
            for c in range(RING):
                keys(c, 0)
            with sp.Fori(0, NB - 1) as b:
                for c in range(NCH):
                    keys(c + RING, NP * b, 3 * NCH * b + 3 * (c + 1))
            for c in range(NCH - RING):
                keys(c + RING, NP * (NB - 1), 3 * NCH * (NB - 1) + 3 * (c + 1))
            sp.wait_ge(kt_ready, 3 * NCH * NB)
            load(C_WO1, columns(w_out[1], 0))
            load(C_WO1 + 1, columns(w_out[1], P))
            with sp.Fori(0, KD // 2 - 1) as i:
                for j in range(2, 4):
                    load(C_WO1 + j, columns(w_out[1], j * P + 2 * P * i), i)
            ffn_chunks(1)

        @block.gpsimd
        def _(pool):
            count = [0, 0]

            def step(instruction, semaphore=None, which=0):
                instruction.then_inc((consts, consts1)[which], 1)
                count[which] += 1
                pool.wait_ge((consts, consts1)[which], count[which])

            for n, value in enumerate((D * EPS, DH * EPS, EPS)):
                step(nc.gpsimd.memset(eps[:, n:n + 1], value))
            step(nc.gpsimd.memset(ones[:], 1.0))
            step(nc.gpsimd.memset(blocks[:], 0.0))
            step(nc.gpsimd.memset(blocks[0:DH, 0:DH], 1.0))
            step(nc.gpsimd.memset(blocks[DH:P, DH:P], 1.0))
            step(nc.gpsimd.affine_select(out=ident[:], in_=ones[:], compare_op=ALU.is_equal, fill=0.0, base=0,
                                         pattern=[[-1, P]], channel_multiplier=1))
            step(nc.gpsimd.affine_select(out=after[:], in_=ones[:], compare_op=ALU.is_gt, fill=0.0, base=0,
                                         pattern=[[-1, P]], channel_multiplier=1))
            assert count[0] == CONSTS0
            stores = [0]

            def store(dst, src, semaphore=stored):
                pool.dma_start(dst, src).then_inc(semaphore, 16)
                stores[0] += semaphore is stored

            def memory(l):
                mb = MBS[l]
                pool.dma_start(mb["mem"][:], mem_prompt[0].rearrange("(t p) n -> p t n", p=P)).then_inc(mem_in, 16)

            def sample_loads(l, G):
                mb = MBS[l]
                for buffer, cache in ((mb["ks"], cache_mem_k), (mb["vs"], cache_mem_v)):
                    pool.dma_start(buffer[:].rearrange("p b t n -> p (b t) n"),
                                   cache[l, G * GS:(G + 1) * GS].rearrange("b (t p) h d -> p (b t) (h d)", p=P)).then_inc(ks_in, 16)

            def memory_stores(l):
                pool.wait_ge(kv_done, l + 1)
                for t, b in ((new_mem_k_p, "km"), (new_mem_v_p, "vm")):
                    store(t[l, 0].rearrange("(t p) h d -> p t (h d)", p=P), MBS[l][b][:])

            def diagonals(c):
                if c >= 2:
                    pool.wait_ge(taps_ready, c - 1)
                nc.gpsimd.affine_select(out=diag[:, c % 2], in_=dw[:, c, 0:PE_TAPS].unsqueeze(2).broadcast_to([P, PE_TAPS, P]),
                                        compare_op=ALU.is_equal, fill=0.0, base=0, pattern=[[0, PE_TAPS], [-1, P]],
                                        channel_multiplier=1).then_inc(diag_ready, 1)
            pool.wait_ge(tr_free, marks["start"])
            memory(0)
            for c in range(KC):
                diagonals(c)
            pool.wait_ge(tr_free, marks["conv states"])
            store(new_conv_p[0, 0], stP[:])
            for G in range(GR):
                store(new_conv_s[0, G * GS:(G + 1) * GS].rearrange("b n c -> (b n) c"), stS[:, G, :])
            pool.wait_ge(stored, 16 * stores[0])
            sample_loads(0, 0)
            memory_stores(0)
            for G in range(1, GR):
                pool.wait_ge(at_pv, len(MEM_UNITS) + G)
                sample_loads(0, G)

            pool.wait_ge(w_used, C_FOX)
            one = lambda instruction: step(instruction, which=1)
            one(nc.gpsimd.memset(win[:], 1.0))
            one(nc.gpsimd.affine_select(out=win[:], in_=win[:], compare_op=ALU.is_ge, fill=0.0, base=-(SEQ - P),
                                        pattern=[[1, 2 * SEQ - P]], channel_multiplier=-1))
            one(nc.gpsimd.memset(maskd[:], 0.0))
            one(nc.gpsimd.affine_select(out=maskd[:], in_=maskd[:], compare_op=ALU.is_ge, fill=NEG, base=0,
                                        pattern=[[-1, P]], channel_multiplier=1))
            one(nc.gpsimd.memset(bm[:], 1.0))
            one(nc.gpsimd.affine_select(out=bm[:], in_=bm[:], compare_op=ALU.is_ge, fill=0.0, base=0,
                                        pattern=[[-NQ, NB]], channel_multiplier=1))
            one(nc.gpsimd.affine_select(out=bm[:], in_=bm[:], compare_op=ALU.is_ge, fill=0.0, base=NQ - 1,
                                        pattern=[[NQ, NB]], channel_multiplier=-1))
            one(nc.gpsimd.affine_select(out=sameq[:], in_=bm[:].unsqueeze(2).broadcast_to([NS, NB, NQ]), compare_op=ALU.is_ge,
                                        fill=0.0, base=0, pattern=[[NQ, NB], [1, NQ]], channel_multiplier=-1))
            one(nc.gpsimd.memset(mshT[:], 0.0))
            m = mshT[:].rearrange("j (h q) -> j h q", h=NH)
            one(nc.gpsimd.affine_select(out=m, in_=m, compare_op=ALU.is_ge, fill=NEG, base=-(NS - NQ),
                                        pattern=[[0, NH], [0, NQ]], channel_multiplier=1))
            one(nc.gpsimd.affine_select(out=m, in_=m, compare_op=ALU.is_ge, fill=NEG, base=NS - NQ,
                                        pattern=[[0, NH], [1, NQ]], channel_multiplier=-1))
            one(nc.gpsimd.memset(dq[:], 0.0))
            for b in range(NB):
                one(nc.gpsimd.affine_select(out=dq[:], in_=dq[:], compare_op=ALU.not_equal, fill=1.0, base=-NQ * b,
                                            pattern=[[-1, NQ]], channel_multiplier=1))
            one(nc.gpsimd.affine_select(out=later[:], in_=ones[:], compare_op=ALU.is_gt, fill=0.0, base=0,
                                        pattern=[[-1, P]], channel_multiplier=1))
            same = later[:].rearrange("p (b n) -> p b n", b=NB)
            one(nc.gpsimd.affine_select(out=same, in_=same, compare_op=ALU.is_ge, fill=0.0, base=NP - 1,
                                        pattern=[[NP, NB], [0, NP]], channel_multiplier=-1))
            assert count[1] == CONSTS1
            pool.dma_start(pages[:], page_table.rearrange("b n -> (b n)").unsqueeze(0)).then_inc(pages_in, 16)
            pool.wait_ge(pages_in, 16)
            for i in range(NB * NP):
                which = pool.value_load(pages[0:1, i:i + 1], min_val=0, max_val=N_PHYS - 1)
                pool.dma_start(lfrow[i:i + 1, :], cache_fox_logf[0, bass.ds(which, 1)].rearrange("o p h -> o (p h)")).then_inc(lf_in, 16)
            pool.wait_ge(c_ready, 1)
            store(new_fox_logf_p[0, 0].rearrange("(t p) h -> p t h", p=P), lf[:, 0:TT, :])
            store(new_fox_logf_s[0].rearrange("b q h -> (b q) h"), lf[0:NS, TT, :])
            pool.wait_ge(hn_done, MP + 1 + 3 * HP)
            store(new_fox_v_p[0, 0].rearrange("(t p) h d -> p t (h d)", p=P), vtok[:, 0:TT, :])
            store(new_fox_v_s[0].rearrange("b q h d -> (b q) (h d)"), vtok[0:NS, TT, :])
            for t in range(TT + 1):
                pool.wait_ge(tr_free, marks["k", t])
                if t < TT:
                    store(new_fox_k_p[0, 0].rearrange("(t p) h d -> t p (h d)", p=P)[t], ktok[:, t % 2, :], k_stored[t % 2])
                else:
                    store(new_fox_k_s[0].rearrange("b q h d -> (b q) (h d)"), ktok[0:NS, t % 2, :], k_stored[t % 2])
            for s in range(2):
                pool.wait_ge(k_stored[s], 16 * ((TT + 2 - s) // 2))
            pool.wait_ge(tr_free, marks["forget"])
            memory(1)
            memory_stores(1)
            pool.wait_ge(w_used, C_MEM1 + N_MEM)
            sample_loads(1, 0)
            pool.wait_ge(at_pv, 2 * len(MEM_UNITS) + GR + 1)
            sample_loads(1, 1)
            assert GR == 2

            assert stores[0] == marks["km stored"]
            pool.wait_ge(w_used, C_WO1)
            pool.wait_ge(tr_free, marks["far"])

            def values(c, first):
                for pp in range(CPG):
                    p = pool.value_load(pages[0:1, bass.ds(first + CPG * c + pp, 1)], min_val=0, max_val=N_PHYS - 1)
                    pool.dma_start(vring[c % RING][:, pp, :], cache_fox_v[0, bass.ds(p, 1)].rearrange("o p h d -> (o p) (h d)"))\
                        .then_inc(v_in[c % RING], 16)
            for c in range(RING):
                values(c, 0)
            with pool.Fori(0, NB - 1) as b:
                for c in range(NCH):
                    pool.wait_ge(v_used, NCH * b + c + 1)
                    values(c + RING, NP * b)
            for c in range(NCH - RING):
                pool.wait_ge(v_used, NCH * (NB - 1) + c + 1)
                values(c + RING, NP * (NB - 1))
            for t in range(TT + 1):
                pool.wait_ge(tr_free, marks["y", t])
                if t < TT:
                    store(y_prompt[0].rearrange("(t p) n -> t p n", p=P)[t], ystage[:, t % 2, :], y_stored[t % 2])
                else:
                    store(y_sample.rearrange("b q n -> (b q) n"), ystage[0:NS, t % 2, :], y_stored[t % 2])
            pool.wait_ge(stored, 16 * stores[0])
            for s in range(2):
                pool.wait_ge(y_stored[s], 16 * ((TT + 2 - s) // 2))


_INS = ['x_prompt', 'x_sample', 'cache_conv', 'cache_fox_k', 'cache_fox_v', 'cache_fox_logf', 'cache_mem_k',
        'cache_mem_v', 'page_table', 'mem_prompt', 'norm1', 'conv_w_in', 'conv_dw', 'conv_dw_b', 'conv_ln_g',
        'conv_ln_b', 'fox_w_in', 'fox_b_f', 'fox_q_norm', 'fox_k_norm', 'mem_norm', 'w_mem_kv', 'mem_q_norm',
        'mem_k_norm', 'w_out', 'norm2', 'w_gate_up', 'w_down']


def kernel(**inputs):
    import numpy as _np
    import concourse.bacc as _bacc
    from concourse import mybir as _mybir
    from concourse.bass_utils import run_bass_kernel_spmd as _run

    nc = _bacc.Bacc("TRN2", target_bir_lowering=False, num_devices=1)
    arrays, args = {}, []
    for name in _INS:
        a = _np.ascontiguousarray(inputs[name])
        arrays[f"in_{name}_dram"] = a
        args.append(nc.dram_tensor(f"in_{name}_dram", a.shape, _mybir.dt.from_np(a.dtype), kind="ExternalInput").ap())
    _, S_, D_ = inputs["x_prompt"].shape
    NB_, NQ_ = inputs["x_sample"].shape[:2]
    _, H_, C_ = inputs["cache_conv"].shape[1:]
    NH_, DH_ = inputs["cache_fox_k"].shape[3:]
    L_, _, NM_, MH_, _ = inputs["cache_mem_k"].shape
    outs = [(1, S_, D_), (NB_, NQ_, D_), (1, 1, H_, C_), (1, 1, S_, NH_, DH_), (1, 1, S_, NH_, DH_), (1, 1, S_, NH_),
            (L_, 1, NM_, MH_, DH_), (L_, 1, NM_, MH_, DH_), (1, NB_, H_, C_), (1, NB_, NQ_, NH_, DH_),
            (1, NB_, NQ_, NH_, DH_), (1, NB_, NQ_, NH_)]
    for i, shape in enumerate(outs):
        args.append(nc.dram_tensor(f"out_{i}_dram", shape, _mybir.dt.float32, kind="ExternalOutput").ap())
    build(nc, *args)
    r = _run(nc, [arrays], core_ids=[0])
    return tuple(r.results[0][f"out_{i}_dram"] for i in range(len(outs)))
```

```python
from contextlib import ExitStack

import concourse.bass as bass
from concourse import mybir

ALU = mybir.AluOpType
ACT = mybir.ActivationFunctionType
F32 = mybir.dt.float32
F32R = mybir.dt.float32r
I32 = mybir.dt.int32
AX_X = mybir.AxisListType.X

P = 128
EPS = 1e-6
NEG = -1e30
ATANH_TERMS = 8


class Steps:

    def __init__(self, semaphore):
        self.semaphore, self.n, self.per_pass, self.i = semaphore, 0, 0, None

    def inc(self, instruction):
        instruction.then_inc(self.semaphore, 1)
        self.n += 1

    def value(self):
        return self.n if self.i is None else self.i * self.per_pass + self.n

    def enter(self, i, per_pass):
        self.i, self.per_pass, self.first = i, per_pass, self.n

    def leave(self, passes):
        assert self.n - self.first == self.per_pass, (self.n - self.first, self.per_pass)
        self.i, self.n = None, self.first + passes * self.per_pass


def build(nc, x_prompt, x_sample, cache_conv, cache_fox_k, cache_fox_v, cache_fox_logf,
          cache_mem_k, cache_mem_v, page_table, mem_prompt, norm1, conv_w_in, conv_dw,
          conv_dw_b, conv_ln_g, conv_ln_b, fox_w_in, fox_b_f, fox_q_norm, fox_k_norm,
          mem_norm, w_mem_kv, mem_q_norm, mem_k_norm, w_out, norm2, w_gate_up, w_down,
          y_prompt, y_sample, new_conv_p, new_fox_k_p, new_fox_v_p, new_fox_logf_p,
          new_mem_k_p, new_mem_v_p, new_conv_s, new_fox_k_s, new_fox_v_s, new_fox_logf_s):
    SEQ, D = x_prompt.shape[1:]
    NB, NQ = x_sample.shape[:2]
    NS = NB * NQ
    T = SEQ + NS
    HT = T // 2
    KD = D // P
    TT = SEQ // P
    W = conv_dw.shape[1]
    H = W - 1
    CH = conv_dw.shape[2]
    KC = CH // P
    DF = w_down.shape[1]
    KF = DF // P
    KF2 = KF // 2
    NH, DH = cache_fox_k.shape[3:]
    HP = NH // 2
    NP, PG = page_table.shape[1], cache_fox_k.shape[2]
    N_PHYS = cache_fox_k.shape[1]
    MH = cache_mem_k.shape[3]
    NM = mem_prompt.shape[1]
    MT = NM // P
    MW = MH * DH
    MP = MH // 2
    GS = 4
    GR = NB // GS
    ROWS = NH * NQ
    QR = 4 * NQ
    NPAST = NP * PG
    CPG = 2
    NCH = NP // CPG
    KEYS = CPG * PG
    PE_TAPS = 8
    RING = 4
    assert P == PG == NB * NP and T % 2 == 0 and HT <= 512 and KF % 2 == 0 and NS <= P and MH == 4
    assert QR == 32 and ROWS == 3 * QR and KC == HP and MP == MT == 2 and KD == KC + MP

    C_CONV = 0
    C_MEM0 = C_CONV + 2 * KC + MP
    N_MEM = 4
    C_WO0 = C_MEM0 + N_MEM
    C_GU0 = C_WO0 + KD
    C_DN0 = C_GU0 + 2 * KF
    C_FOX = C_DN0 + 2 * KD
    N_FOX = 1 + 3 * HP + MP
    C_MEM1 = C_FOX + N_FOX
    C_WO1 = C_MEM1 + N_MEM
    C_GU1 = C_WO1 + KD
    C_DN1 = C_GU1 + 2 * KF
    C_END = C_DN1 + 2 * KD
    C_MEM, C_WO, C_GU, C_DN = (C_MEM0, C_MEM1), (C_WO0, C_WO1), (C_GU0, C_GU1), (C_DN0, C_DN1)
    KM = KD // N_MEM
    SMALL, LARGE = KD * P, KF2 * P
    assert KM * 2 * MW == SMALL

    def chunk_size(n):
        return LARGE if C_DN0 <= n < C_FOX or C_DN1 <= n else SMALL

    VEC_LOADS = 6 + 8 + 1 + 2 + 1
    CONSTS0, CONSTS1 = 9, 14 + NB

    MEM_UNITS = [("mem", hp, t, NM) for hp in range(MP) for t in range(TT)]
    FOX_UNITS = [("fox", hp, t, (t + 1) * P) for hp in range(HP) for t in range(TT)]

    with ExitStack() as ctx:
        def sem(name):
            return ctx.enter_context(nc.semaphore(name))

        top = [nc.sbuf_base + (-nc.sbuf_base) % 32]

        def at(name, shape, offset, dt=F32):
            size = 4
            for n in shape[1:]:
                size *= n
            end = offset + size + (-size) % 32
            assert end <= nc.sbuf_usable_end, (name, end)
            return nc.alloc_sbuf_tensor_at(name, shape, dt, offset=offset), end

        def sb(name, shape, dt=F32):
            buffer, top[0] = at(name, shape, top[0], dt)
            return buffer

        xT = sb("xT", [P, KD, T])
        aH = sb("aH", [P, KD, T], F32R)
        aL = sb("aL", [P, KD, T], F32R)
        ring_at = top[0]
        raw = sb("raw", [P, 2, LARGE])
        wH = [sb(f"wH{s}", [P, LARGE], F32R) for s in range(2)]
        wL = [sb(f"wL{s}", [P, LARGE], F32R) for s in range(2)]
        sq = sb("sq", [P, 2, T])
        tmp = sb("tmp", [P, 2, T])
        rb = sb("rb", [P, T])
        ident = sb("ident", [P, P])
        ones = sb("ones", [P, P])
        blocks = sb("blocks", [P, P])
        after = sb("after", [P, P])
        V_N1, V_N2, V_MEM = 0, 2 * KD, 4 * KD
        V_DWB, V_LNG, V_LNB = 6 * KD, 6 * KD + KC, 6 * KD + 2 * KC
        V_MQ = 6 * KD + 3 * KC
        N_VEC = V_MQ + 4
        vec = sb("vec", [P, N_VEC])
        dw_at = top[0]
        dw = sb("dw", [P, KC, W])
        eps = sb("eps", [P, 3])
        dw2 = sb("dw2", [P, 2, W])
        gk_row = sb("gk_row", [P, 2, DH])
        bf = sb("bf", [NH, 1])
        stat = sb("stat", [P, 64])
        pages = sb("pages", [1, NB * NP], I32)
        BASE = top[0]

        def memory_buffers(n, o, far, rows_at):
            b = {}
            start = o
            for name, shape in (("prob", [P, 2, 2, 512 if n else NM]), ("pT", [P, 2, 4, P]), ("km", [P, MT, MW]),
                                ("vm", [P, MT, MW]), ("kmT", [P, MP, NM]), ("qm", [P, MP, T]),
                                ("qd", [P, GS, MP, QR]), ("o", [P, MW])):
                b[name], o = at(f"{name}{n}", shape, o)
                if name == "vm":
                    parts_end = o
            end = o
            if n:
                b["mem"], rows_end = at(f"mem{n}", [P, MT, D], rows_at)
                b["stage"], _ = at(f"stage{n}", [P, 2, 2 * NM], rows_end)
                b["mH"], o = at(f"mH{n}", [P, KD, NM], start, F32R)
                b["mL"], o = at(f"mL{n}", [P, KD, NM], o, F32R)
                assert o <= parts_end
                o = far
            else:
                b["mem"], o = at(f"mem{n}", [P, MT, D], o)
                b["stage"] = tmp[:, :, 0:2 * NM]
                b["mH"], o = at(f"mH{n}", [P, KD, NM], o, F32R)
                b["mL"], o = at(f"mL{n}", [P, KD, NM], o, F32R)
            b["ks"], o = at(f"ks{n}", [P, GS, MT, MW], o)
            b["vs"], o = at(f"vs{n}", [P, GS, MT, MW], o)
            b["ksT"], o = at(f"ksT{n}", [P, GS, MP, NM], o)
            return b, end, o

        uP, o = at("uP", [P, KC, H + SEQ], BASE)
        uS, o = at("uS", [P, KC, NB, H + NQ], o)
        yc_at = o
        yc, o = at("yc", [P, KC, T], o)
        mb0, _, o0 = memory_buffers(0, o, None, None)
        ks_at = o0 - 3 * 4 * GS * MT * MW
        stP, o = at("stP", [H, CH], ks_at)
        stS, o = at("stS", [GS * H, GR, CH], o)
        usc, o = at("usc", [P, KC, NB, H], o)
        diag, o = at("diag", [P, 2, PE_TAPS, P], o)
        diag2, e_ = at("diag2", [P, 2, PE_TAPS, P], ks_at)
        assert e_ <= ks_at + 4 * CH * (1 + GR)
        assert o <= o0
        xin, o = at("xin", [P, TT + 1, D], yc_at)
        vrow, o = at("vrow", [N_VEC, P], o)
        dwrow, o = at("dwrow", [W, CH], o)
        crow, o = at("crow", [GS * H, GR, CH], o)
        gH, o = at("gH", [P, KF, T], BASE, F32R)
        gL, o = at("gL", [P, KF, T], o, F32R)
        qkT, o = at("qkT", [P, 2 * HP, T], BASE)
        vtok, o = at("vtok", [P, TT + 1, CH], o)
        lf, o = at("lf", [P, TT + 1, NH], o)
        ctok, o = at("ctok", [P, TT + 1, NH], o)
        work, o = at("work", [P, 4, (TT + 1) * NH], o)
        maskd, o = at("maskd", [P, P], o)
        sameq, o = at("sameq", [NS, NS], o)
        mshift, o = at("mshift", [ROWS, NS - NQ + NS], o)
        maskb, o = at("maskb", [ROWS, NS], o)
        mshT, o = at("mshT", [NS - NQ + NS, ROWS], o)
        bm, o = at("bm", [NS, NB], o)
        dq, o = at("dq", [NS, NQ], o)
        cqA, o = at("cqA", [NS, NH, NQ], o)
        cqr, o = at("cqr", [ROWS, NB], o)
        ncx, o = at("ncx", [NS, NH, NQ], o)
        rx, o = at("rx", [P, 2, CPG, NH, NQ], o)
        qx, o = at("qx", [P, HP, QR], o)
        rtok, _ = at("rtok", [P, NH, NB * NP], o)
        lfrow, o = at("lfrow", [NB * NP, PG * NH], o)
        later, _ = at("later", [NB * NP, NB * NP], dw_at)
        assert NB * NP <= KC * W
        lftot, o = at("lftot", [NB * NP, NH], o)
        ncT, o = at("ncT", [P, SEQ], o)
        mix_at = o
        assert mix_at % 32 == 0
        far1 = mix_at + 4 * (2 * 2 * 512 + 2 * 4 * P + 2 * MT * MW + MP * NM + MP * T + GS * MP * QR + MW)
        ktok, o = at("ktok", [P, 2, CH], far1)
        lfd, o = at("lfd", [P, TT, P], o)
        win, o = at("win", [P, 2 * SEQ - P], o)
        mb1, z_end, _ = memory_buffers(1, mix_at, far1, o)
        assert z_end == far1
        kT, o = at("kT", [P, 2, HP, KEYS], mix_at)
        S, o = at("S", [ROWS, NPAST + NS], o)
        pTs, o = at("pTs", [P, NP + 1, ROWS], o)
        lfT, _ = at("lfT", [P, NH, NB * NP], mix_at + 4 * 2 * HP * KEYS)
        ncb, e_ = at("ncb", [P, 2, 2, SEQ], mix_at + 4 * 2 * HP * KEYS)
        assert e_ <= far1
        kring, vring = [], []
        ring_end = ring_at
        for c in range(RING):
            buffer, ring_end = at(f"kring{c}", [P, CPG, CH], ring_end)
            kring.append(buffer)
        for c in range(RING):
            if c == RING - 1:
                buffer, ring_end = at(f"vring{c}", [P, CPG, CH], ring_end)
            else:
                buffer, o = at(f"vring{c}", [P, CPG, CH], o)
            vring.append(buffer)
        assert ring_end <= ring_at + 4 * 6 * LARGE
        os_, o = at("os_", [ROWS, 4 * DH], o)
        ystage, _ = at("ystage", [P, 2, D], BASE)
        MBS = (mb0, mb1)

        ps = ctx.enter_context(nc.psum_tensor("ps", [P, 8, 512], F32))

        def acc(slot):
            return ps[:, 2 * slot:2 * slot + 2, 0:HT]

        def score_bank(u, e, keys):
            return ps[:, 2 * (u % 2) + e, 0:keys]

        def halves(ap):
            return ap.rearrange("p (a n) -> p a n", a=2)

        x_in = [sem(f"x_in{t}") for t in range(TT + 1)]
        vec_in, hist_in, mem_in, pages_in = (sem(n) for n in ("vec_in", "hist_in", "mem_in", "pages_in"))
        raw_in = [sem(f"raw_in{s}") for s in range(2)]
        ks_in, vs_in = sem("ks_in"), sem("vs_in")
        k_in = [sem(f"k_in{s}") for s in range(RING)]
        v_in = [sem(f"v_in{s}") for s in range(RING)]
        lf_in = sem("lf_in")
        hi_done, lo_done, w_used = (sem(n) for n in ("hi_done", "lo_done", "w_used"))
        consts = sem("consts")
        consts1 = sem("consts1")
        vchain = sem("vchain")
        diag_ready, taps_ready, y_begun = sem("diag_ready"), sem("taps_ready"), sem("y_begun")
        ysq_used, swish_done, usc_done = sem("ysq_used"), sem("swish_done"), sem("usc_done")
        x_new, sq_done, sq_used, ss_ready = (sem(n) for n in ("x_new", "sq_done", "sq_used", "ss_ready"))
        sq_added = sem("sq_added")
        v_done, vH_done, a_ready = (sem(n) for n in ("v_done", "vH_done", "a_ready"))
        tr_ready, tr_free = sem("tr_ready"), sem("tr_free")
        sig_done, u_done, y_done, ysq_done, ln_ready = (sem(n) for n in ("sig_done", "u_done", "y_done", "ysq_done", "ln_ready"))
        mean_done, lny_done, mixf_done = sem("mean_done"), sem("lny_done"), sem("mixf_done")
        norm_root, head_root, ln_root, mem_root, kss_done, k_root = (sem(n) for n in ("norm_root", "head_root", "ln_root", "mem_root", "kss_done", "k_root"))
        z_done, hn_ready, hn_done = (sem(n) for n in ("z_done", "hn_ready", "hn_done"))
        ms_done, mn_done, mH_done, mL_done, kvsq_done, kv_done = (sem(n) for n in ("ms_done", "mn_done", "mH_done", "mL_done", "kvsq_done", "kv_done"))
        at_s, at_max, at_exp, at_prob, at_pv, at_hi, at_lo = (sem(n) for n in ("at_s", "at_max", "at_exp", "at_prob", "at_pv", "at_hi", "at_lo"))
        qd_done, oT_ready, oT_hi = sem("qd_done"), sem("oT_ready"), sem("oT_hi")
        silu_done, g_done, gH_done, gL_done = (sem(n) for n in ("silu_done", "g_done", "gH_done", "gL_done"))
        e_done, zab_done, c_ready, c_done, stage_done = (sem(n) for n in ("e_done", "zab_done", "c_ready", "c_done", "stage_done"))
        qx_done, lftot_done, rx_done = (sem(n) for n in ("qx_done", "lftot_done", "rx_done"))
        kt_ready, kt_ev_v, kt_ev_a = (sem(n) for n in ("kt_ready", "kt_ev_v", "kt_ev_a"))
        sc_ready, sc_free, sn_ready = (sem(n) for n in ("sc_ready", "sc_free", "sn_ready"))
        smax_done, sexp_done, pt_ready, pt_free, o_ready, o_done = (sem(n) for n in ("smax_done", "sexp_done", "pt_ready", "pt_free", "o_ready", "o_done"))
        v_used = sem("v_used")
        stored = sem("stored")
        k_stored = [sem(f"k_stored{s}") for s in range(2)]
        y_stored = [sem(f"y_stored{s}") for s in range(2)]

        block = ctx.enter_context(nc.Block())

        marks = {"km stored": 1 + GR + 2 + 2 + 2 + 2}

        def columns(w, start, k0=0, ks=KD):
            return w.rearrange("(k p) n -> p k n", p=P)[:, k0:k0 + ks, bass.ds(start, P)]

        @block.vector
        def _(dve):
            steps = Steps(vchain)
            tr = [0]

            def link(instruction):
                steps.inc(instruction)
                dve.wait_ge(vchain, steps.value())

            def lo(n0, i=0):
                s, size = n0 % 2, chunk_size(n0)
                dve.wait_ge(hi_done, n0 + 1 + 2 * i)
                nc.vector.tensor_tensor(wL[s][:, 0:size], raw[:, s, 0:size], wH[s][:, 0:size].bitcast(F32),
                                        ALU.subtract).then_inc(lo_done, 1)

            def group():
                g = tr[0]
                tr[0] += 1
                dve.wait_ge(tr_ready, g + 1)
                return ps[:, 6 + g % 2, :]

            def norm(r):
                gain = (V_N1, V_N2)[r % 2] + (r // 2) * KD
                dve.wait_ge(norm_root, r + 1)
                link(nc.vector.reciprocal(rb[:], rb[:]))
                for k in range(KD + 1):
                    if k < KD:
                        if KD * r + k >= 2:
                            dve.wait_ge(a_ready, KD * r + k - 1)
                        nc.vector.scalar_tensor_tensor(out=tmp[:, k % 2], in0=xT[:, k], scalar=vec[:, gain + k:gain + k + 1],
                                                       in1=rb[:], op0=ALU.mult, op1=ALU.mult).then_inc(v_done, 1)
                    if k:
                        dve.wait_ge(vH_done, KD * r + k)
                        nc.vector.tensor_tensor(aL[:, k - 1], tmp[:, (k - 1) % 2], aH[:, k - 1].bitcast(F32),
                                                ALU.subtract).then_inc(a_ready, 1)

            def finish_head(z0, out, gain, h0, i=0):
                dve.wait_ge(head_root, h0 + 1 + 2 * i)
                link(nc.vector.reciprocal(rb[:], rb[:]))
                nc.vector.scalar_tensor_tensor(out=out, in0=tmp[:, z0 % 2], scalar=vec[:, gain:gain + 1], in1=rb[:],
                                               op0=ALU.mult, op1=ALU.mult).then_inc(hn_done, 1)

            def memory_rows(l):
                mb = MBS[l]
                dve.wait_ge(mem_root, l + 1)
                link(nc.vector.reciprocal(stat[:, 34:34 + MT], stat[:, 34:34 + MT]))
                for t in range(MT):
                    last = nc.vector.tensor_scalar(mb["mem"][:, t], mb["mem"][:, t], stat[:, 34 + t:35 + t], None, ALU.mult)
                last.then_inc(mn_done, 1)

            def memory_gain(l, g):
                mb = MBS[l]
                bank = group()
                if g >= 2:
                    dve.wait_ge(mL_done, l * KD // 2 + g - 1)
                for k in range(2):
                    gain = V_MEM + l * KD + 2 * g + k
                    last = nc.vector.tensor_scalar(mb["stage"][:, g % 2, k * NM:(k + 1) * NM], bank[:, k * NM:(k + 1) * NM],
                                                   vec[:, gain:gain + 1], None, ALU.mult)
                last.then_inc(tr_free, 1)
                marks["memory", l, g] = tr[0]

            def memory_lo(l, g):
                mb = MBS[l]
                dve.wait_ge(mH_done, l * KD // 2 + g + 1)
                nc.vector.tensor_tensor(mb["mL"][:, 2 * g:2 * g + 2, :].rearrange("p k n -> p (k n)"), mb["stage"][:, g % 2, :],
                                        mb["mH"][:, 2 * g:2 * g + 2, :].rearrange("p k n -> p (k n)").bitcast(F32),
                                        ALU.subtract).then_inc(mL_done, 1)

            def memory_chunks(l, between):
                for i in range(N_MEM):
                    if i < N_MEM - l:
                        lo(C_MEM[l] + 1 + i)
                    between(i)

            def memory_kv(l):
                mb = MBS[l]
                dve.wait_ge(kvsq_done, l + 1)
                nc.vector.tensor_reduce(stat[:, 36:36 + MT * MH].rearrange("p (t h) -> p t h", t=MT),
                                             sq[:, :, 0:MW].rearrange("p t (h d) -> p t h d", h=MH), AX_X, ALU.add).then_inc(kss_done, 1)
                dve.wait_ge(k_root, l + 1)
                link(nc.vector.reciprocal(stat[:, 44:44 + MT * MH], stat[:, 44:44 + MT * MH]))
                for t in range(MT):
                    link(nc.vector.tensor_tensor(mb["km"][:, t].rearrange("p (h d) -> p h d", h=MH),
                                                 ps[:, t, 0:MW].rearrange("p (h d) -> p h d", h=MH),
                                                 stat[:, 44 + MH * t:44 + MH * t + MH].unsqueeze(2).broadcast_to([P, MH, DH]), ALU.mult))
                    last = nc.vector.tensor_tensor(mb["km"][:, t].rearrange("p (h d) -> p h d", h=MH),
                                                   mb["km"][:, t].rearrange("p (h d) -> p h d", h=MH),
                                                   gk_row[:, l:l + 1, :].broadcast_to([P, MH, DH]), ALU.mult)
                last.then_inc(kv_done, 1)
                bank = group()
                nc.vector.tensor_copy(mb["kmT"][:].rearrange("p a n -> p (a n)"), bank).then_inc(tr_free, 1)

            def top_of(u, unit, mb):
                kind, hp, t, keys = unit
                st = stat[:, 8 * (u % 2):8 * (u % 2) + 8]
                dve.wait_ge(at_s, u + 1)
                if kind == "fox":
                    for e in range(2):
                        c_q = ctok[:, t, 2 * hp + e:2 * hp + e + 1]
                        last = nc.vector.scalar_tensor_tensor(out=mb["prob"][:, u % 2, e, 0:keys],
                                                              in0=score_bank(u, e, keys), scalar=c_q,
                                                              in1=ncb[:, hp % 2, e, 0:keys], op0=ALU.add, op1=ALU.add)
                    link(last)
                    diagonal = mb["prob"][:, u % 2, :, keys - P:keys]
                    link(nc.vector.tensor_tensor(diagonal, diagonal, maskd[:].unsqueeze(1).broadcast_to([P, 2, P]), ALU.add))
                    values = mb["prob"][:, u % 2, :, 0:keys]
                else:
                    values = ps[:, 2 * (u % 2):2 * (u % 2) + 2, 0:keys]
                nc.vector.tensor_reduce(st[:, 0:2], values, AX_X, ALU.max, negate=True).then_inc(at_max, 1)

            def attend(u0, units, mb, h0, beside=lambda i: None):
                def out_lo(i):
                    kind, hp, t, keys = units[i]
                    tile, u = (hp if kind == "fox" else KC + hp), u0 + i
                    dve.wait_ge(at_hi, h0 + i + 1)
                    nc.vector.tensor_tensor(aL[:, tile, t * P:(t + 1) * P], ps[:, 4 + u % 2, 0:P],
                                            aH[:, tile, t * P:(t + 1) * P].bitcast(F32), ALU.subtract).then_inc(at_lo, 1)
                def broadcast_c(hp):
                    for e in range(2):
                        bank = group()
                        nc.vector.tensor_copy(ncb[:, hp % 2, e, :], bank).then_inc(tr_free, 1)
                if units[0][0] == "fox":
                    broadcast_c(0)
                    dve.wait_ge(tr_free, tr[0])
                for i in range(2):
                    top_of(u0 + i, units[i], mb)
                def scale(i):
                    u, keys = u0 + i, units[i][3]
                    st = stat[:, 8 * (u % 2):8 * (u % 2) + 8]
                    dve.wait_ge(at_exp, u + 1)
                    link(nc.vector.reciprocal(st[:, 4:6], st[:, 2:4]))
                    for e in range(2):
                        last = nc.vector.tensor_scalar(mb["prob"][:, u % 2, e, 0:keys], mb["prob"][:, u % 2, e, 0:keys],
                                                       st[:, 4 + e:5 + e], None, ALU.mult)
                    last.then_inc(at_prob, 1)
                scale(0)
                for i, (kind, hp, t, keys) in enumerate(units):
                    u = u0 + i
                    if kind == "mem":
                        bank = group()
                        nc.vector.tensor_copy(mb["pT"][:, :, 0:2, :].rearrange("p e k q -> p e (k q)"),
                                              bank.rearrange("p (e n) -> p e n", e=2)).then_inc(tr_free, 1)
                    else:
                        for e in range(2):
                            bank = group()
                            nc.vector.tensor_copy(mb["pT"][:, e, 0:t + 1, :].rearrange("p k q -> p (k q)"),
                                                  bank[:, 0:keys]).then_inc(tr_free, 1)
                    if i:
                        out_lo(i - 1)
                    if i + 1 < len(units):
                        scale(i + 1)
                    if i + 2 < len(units):
                        top_of(u + 2, units[i + 2], mb)
                    if kind == "fox" and t == 1 and hp + 1 < HP:
                        broadcast_c(hp + 1)
                    beside(i)
                out_lo(len(units) - 1)

            def sample_memory(l, u0, beside=lambda G: None):
                mb = MBS[l]
                link(nc.vector.memset(mb["qd"][:], 0.0))
                for G in range(GR):
                    u = u0 + G
                    st = stat[:, 8 * (u % 2):8 * (u % 2) + 8]
                    if G:
                        dve.wait_ge(at_s, u)
                    for hp in range(MP):
                        for e in range(2):
                            r = slice(DH * e, DH * e + DH)
                            col = (2 * hp + e) * NQ
                            src = mb["qm"][r, hp, SEQ + G * GS * NQ:SEQ + (G + 1) * GS * NQ].rearrange("p (b q) -> p b q", b=GS)
                            last = nc.vector.tensor_copy(mb["qd"][r, :, hp, col:col + NQ], src)
                    last.then_inc(qd_done, 1)
                    for b in range(GS):
                        bank = group()
                        nc.vector.tensor_copy(mb["ksT"][:, b].rearrange("p a n -> p (a n)"), bank).then_inc(tr_free, 1)
                    marks["ksT", l, G] = tr[0]
                    beside(G)
                    dve.wait_ge(at_s, u + 1)
                    nc.vector.tensor_reduce(st[:, 0:1], ps[:, u % 2, 0:NM], AX_X, ALU.max, negate=True).then_inc(at_max, 1)
                    dve.wait_ge(at_exp, u + 1)
                    link(nc.vector.reciprocal(st[:, 4:5], st[:, 2:3]))
                    nc.vector.tensor_scalar(mb["prob"][:, u % 2, 0, 0:NM], mb["prob"][:, u % 2, 0, 0:NM], st[:, 4:5], None,
                                            ALU.mult).then_inc(at_prob, 1)
                    bank = group()
                    nc.vector.tensor_copy(mb["pT"][:, 0, 0:MT, :].rearrange("p k q -> p (k q)"), bank[:, 0:MT * P]).then_inc(tr_free, 1)
                    dve.wait_ge(at_pv, u + 1)
                    nc.vector.tensor_copy(mb["o"][:], ps[:, 4 + u % 2, 0:MW]).then_inc(at_lo, 1)
                    marks["sample memory", l, G] = tr[0]
                    bank = group()
                    dve.wait_ge(oT_hi, GR * l + G + 1)
                    for s in range(MP):
                        for e in range(2):
                            r = slice(DH * e, DH * e + DH)
                            src = bank[r, s * P:(s + 1) * P].rearrange("p (b h q) -> p b h q", b=GS, h=MH)[:, :, 2 * s + e, :]
                            to = slice(SEQ + G * GS * NQ, SEQ + (G + 1) * GS * NQ)
                            last = nc.vector.tensor_tensor(aL[r, KC + s, to].rearrange("p (b q) -> p b q", b=GS), src,
                                                           aH[r, KC + s, to].rearrange("p (b q) -> p b q", b=GS).bitcast(F32), ALU.subtract)
                    last.then_inc(tr_free, 1)

            def residual(c0, per_tile, r):
                if r < 4:
                    link(nc.vector.memset(rb[:], 0.0))
                added = (KD - 1) * (r - 1)

                def tile(j0, i):
                    for s in range(per_tile):
                        n0 = c0 + per_tile * j0 + s + 1
                        if n0 < C_END:
                            lo(n0, i if per_tile == 1 else 2 * i)
                    dve.wait_ge(w_used, c0 + per_tile * (j0 + 1) + 2 * per_tile * i)
                    x = xT[:, bass.ds(j0 + 2 * i, 1), :].rearrange("p o (a n) -> p (o a) n", a=2)
                    nc.vector.tensor_tensor(x, x, acc(j0 % 2), ALU.add).then_inc(x_new, 1)
                    if r < 4 and j0:
                        dve.wait_ge(sq_done, KD * r + j0 + 2 * i)
                        if j0 > 1:
                            dve.wait_ge(sq_added, added + j0 - 1 + 2 * i)
                        nc.vector.tensor_tensor(rb[:], rb[:], sq[:, (j0 - 1) % 2], ALU.add).then_inc(sq_added, 1)
                for j in range(2):
                    tile(j, 0)
                with dve.Fori(0, KD // 2 - 2) as i:
                    for j in range(2, 4):
                        tile(j, i)
                for j in range(KD - 2, KD):
                    tile(j, 0)

            def ffn(l):
                c0, g0 = C_GU[l], l * KF

                def tile(f0, i):
                    lo(c0 + 2 * f0 + 1, 2 * i)
                    lo(c0 + 2 * f0 + 2, 2 * i)
                    dve.wait_ge(silu_done, g0 + f0 + 1 + 2 * i)
                    dve.wait_ge(w_used, c0 + 2 * f0 + 2 + 4 * i)
                    if g0 + f0 >= 2:
                        dve.wait_ge(gL_done, g0 + f0 - 1 + 2 * i)
                    nc.vector.tensor_tensor(halves(tmp[:, f0 % 2]), acc(2 * (f0 % 2) + 1), halves(sq[:, f0 % 2]),
                                            ALU.mult).then_inc(g_done, 1)
                    dve.wait_ge(gH_done, g0 + f0 + 1 + 2 * i)
                    f = bass.ds(f0 + 2 * i, 1)
                    nc.vector.tensor_tensor(gL[:, f, :].rearrange("p o n -> p (o n)"), tmp[:, f0 % 2],
                                            gH[:, f, :].rearrange("p o n -> p (o n)").bitcast(F32), ALU.subtract).then_inc(gL_done, 1)
                for f in range(2):
                    tile(f, 0)
                with dve.Fori(0, KF2 - 2) as i:
                    for f in range(2, 4):
                        tile(f, i)
                for f in range(KF - 2, KF):
                    tile(f, 0)

            dve.wait_ge(consts, CONSTS0)
            for t in range(TT + 1):
                rows = P if t < TT else NS
                for q in range(KD // 4):
                    bank = group()
                    last = nc.vector.tensor_copy(xT[:, 4 * q:4 * q + 4, t * P:t * P + rows],
                                                 bank[:, 0:4 * rows].rearrange("p (k n) -> p k n", k=4))
                    last.then_inc(tr_free, 1)
            steps.inc(nc.vector.memset(uP[:, :, 0:H], 0.0))
            bank = group()
            nc.vector.tensor_copy(vec[:], bank[:, 0:N_VEC]).then_inc(tr_free, 1)
            dve.wait_ge(tr_free, tr[0])
            link(nc.vector.tensor_scalar(vec[:, 0:6 * KD], vec[:, 0:6 * KD], float(D) ** 0.5, None, ALU.mult))
            link(nc.vector.tensor_scalar(vec[:, V_MQ + 3:V_MQ + 4], vec[:, V_MQ + 3:V_MQ + 4], float(DH) ** 0.5, None, ALU.mult))
            dve.wait_ge(vec_in, VEC_LOADS * 16)
            link(nc.vector.tensor_scalar(gk_row[:], gk_row[:], float(DH) ** 0.5, None, ALU.mult))
            bank = group()
            nc.vector.tensor_copy(dw[:].rearrange("p c w -> p (c w)"), bank[:, 0:KC * W]).then_inc(tr_free, 1)
            def history(n):
                G, (first, count) = n // 2, ((0, 4), (4, KC - 4))[n % 2]
                bank = group()
                for c in range(count):
                    last = nc.vector.tensor_copy(uS[:, first + c, G * GS:(G + 1) * GS, 0:H],
                                                 bank[:, c * GS * H:(c + 1) * GS * H].rearrange("p (b n) -> p b n", b=GS))
                last.then_inc(tr_free, 1)
            history(0)
            memory_rows(0)
            memory_gain(0, 0)
            for g in range(KD // 2):
                if g + 1 < KD // 2:
                    memory_gain(0, g + 1)
                memory_lo(0, g)
            for n in range(1, 2 * GR):
                history(n)
            marks["start"] = tr[0]
            lo(0)
            dve.wait_ge(mL_done, KD // 2)
            norm(0)

            def glu(c0, i):
                c = bass.ds(c0 + 2 * i, 1)
                dve.wait_ge(sig_done, c0 + 1 + 2 * i)
                a = acc(2 * (c0 % 2))
                sg = halves(sq[:, c0 % 2])
                nc.vector.tensor_tensor(uP[:, c, H:H + HT].rearrange("p o n -> p (o n)"), a[:, 0, :], sg[:, 0, :], ALU.mult)
                nc.vector.tensor_tensor(uP[:, c, H + HT:H + SEQ].rearrange("p o n -> p (o n)"), a[:, 1, 0:SEQ - HT],
                                        sg[:, 1, 0:SEQ - HT], ALU.mult)
                nc.vector.tensor_tensor(uS[:, c, :, H:H + NQ].rearrange("p o b n -> p (o b) n"),
                                        a[:, 1, SEQ - HT:HT].rearrange("p (b n) -> p b n", b=NB),
                                        sg[:, 1, SEQ - HT:HT].rearrange("p (b n) -> p b n", b=NB), ALU.mult).then_inc(u_done, 1)
                dve.wait_ge(u_done, c0 + 1 + 2 * i)

            def taps(c0, i, first, end):
                c = bass.ds(c0 + 2 * i, 1)
                y = yc[:, c, :].rearrange("p o n -> p (o n)")
                begin = 2 * PE_TAPS if c0 >= KC - 2 else PE_TAPS
                if first == begin:
                    link(nc.vector.tensor_copy(dw2[:, c0 % 2, :], dw[:, c, :].rearrange("p o w -> p (o w)")))
                    dve.wait_ge(y_begun, c0 + 1 + 2 * i)
                for j in range(first, end):
                    w = dw2[:, c0 % 2, j:j + 1]
                    uj = uP[:, c, j:j + SEQ].rearrange("p o n -> p (o n)")
                    sj = uS[:, c, :, j:j + NQ].rearrange("p o b n -> p (o b) n")
                    yp, ysm = y[:, 0:SEQ], y[:, SEQ:T].rearrange("p (b n) -> p b n", b=NB)
                    if j > begin:
                        dve.wait_ge(vchain, steps.value() - 1)
                    steps.inc(nc.vector.scalar_tensor_tensor(out=yp, in0=uj, scalar=w, in1=yp, op0=ALU.mult, op1=ALU.add))
                    if j > begin:
                        dve.wait_ge(vchain, steps.value() - 1)
                    last = nc.vector.scalar_tensor_tensor(out=ysm, in0=sj, scalar=w, in1=ysm, op0=ALU.mult, op1=ALU.add)
                    if j < W - 1:
                        steps.inc(last)
                    else:
                        last.then_inc(y_done, 1)

            MIDDLE = (PE_TAPS + W) // 2

            def conv_tile(c0, i=0):
                glu(c0, i)
                lo(C_CONV + 2 * c0 + 3, 2 * i)
                if c0 >= 2:
                    taps(c0 - 2, i, PE_TAPS, MIDDLE)
                lo(C_CONV + 2 * c0 + 4, 2 * i)
                if c0 >= 2:
                    taps(c0 - 2, i, MIDDLE, W)
            for n in range(1, 3):
                lo(C_CONV + n)
            for c in range(2):
                conv_tile(c)
            with dve.Fori(0, KC // 2 - 1) as i:
                steps.enter(i, 4 * (W - PE_TAPS))
                for c in range(2, 4):
                    conv_tile(c, i)
            steps.leave(KC // 2 - 1)
            third = (W - 2 * PE_TAPS) // 3

            def state(n):
                first, count = ((0, 4), (4, KC - 4))[n % 2]
                bank = group()
                if n < 2:
                    nc.vector.tensor_copy(stP[:, first * P:(first + count) * P], bank[0:H, 0:count * P]).then_inc(tr_free, 1)
                else:
                    nc.vector.tensor_copy(stS[:, n // 2 - 1, first * P:(first + count) * P],
                                          bank[0:GS * H, 0:count * P]).then_inc(tr_free, 1)
                marks["conv states"] = tr[0]

            def beside_memory(i):
                if i == 0:
                    finish_head(1, mb0["qm"][:, 1], V_MQ, 1)
                    taps(KC - 2, 0, 2 * PE_TAPS + 3, W)
                else:
                    state(2 * i - 2)
                    state(2 * i - 1)
                    taps(KC - 1, 0, 2 * PE_TAPS + third * (i - 1), 2 * PE_TAPS + third * i if i < 3 else W)
            taps(KC - 2, 0, 2 * PE_TAPS, 2 * PE_TAPS + 3)
            dve.wait_ge(taps_ready, KC)
            finish_head(0, mb0["qm"][:, 0], V_MQ, 0)
            memory_chunks(0, beside_memory)
            memory_kv(0)
            dve.wait_ge(ln_ready, 1)
            nc.vector.tensor_scalar(halves(rb[:]), ps[:, 4:6, 0:HT], 1.0 / CH, None, ALU.mult).then_inc(mean_done, 1)
            dve.wait_ge(mean_done, 1)

            def layer_norm(i):
                squares = tmp[:, 0]
                if i < KC // 2:
                    for c in (2 * i, 2 * i + 1):
                        nc.vector.tensor_tensor(yc[:, c], yc[:, c], rb[:], ALU.subtract).then_inc(lny_done, 1)
                if 0 < i <= KC // 2:
                    for c in (2 * i - 2, 2 * i - 1):
                        dve.wait_ge(ysq_done, c + 1)
                        if c == 0:
                            nc.vector.tensor_copy(squares, sq[:, c % 2]).then_inc(ysq_used, 1)
                        else:
                            dve.wait_ge(ysq_used, c)
                            nc.vector.tensor_tensor(squares, squares, sq[:, c % 2], ALU.add).then_inc(ysq_used, 1)

            def normalise(G):
                if G == 0:
                    dve.wait_ge(ln_root, 1)
                    link(nc.vector.reciprocal(rb[:], rb[:]))
                for c in range(G * KC // GR, (G + 1) * KC // GR):
                    nc.vector.scalar_tensor_tensor(out=yc[:, c], in0=yc[:, c], scalar=vec[:, V_LNG + c:V_LNG + c + 1], in1=rb[:],
                                                   op0=ALU.mult, op1=ALU.mult).then_inc(lny_done, 1)
            attend(0, MEM_UNITS, mb0, 0, layer_norm)
            sample_memory(0, len(MEM_UNITS), normalise)
            u = len(MEM_UNITS) + GR
            for c in range(KC):
                dve.wait_ge(mixf_done, c + 1)
                nc.vector.tensor_tensor(aL[:, c], yc[:, c], aH[:, c].bitcast(F32), ALU.subtract).then_inc(stage_done, 1)
            residual(C_WO0, 1, 1)
            norm(1)
            ffn(0)
            residual(C_DN0, 2, 2)
            norm(2)

            dve.wait_ge(consts1, CONSTS1)
            link(nc.vector.memset(work[:, 0], 0.0))
            link(nc.vector.memset(lfd[:], 0.0))
            link(nc.vector.memset(qx[:], 0.0))
            Z = MP
            lo(C_FOX + 1)
            lo(C_FOX + 2)
            dve.wait_ge(hn_ready, Z + 1)
            nc.vector.tensor_copy(work[:, 0, 0:TT * NH], ps[:, 4, 0:TT * NH])
            nc.vector.tensor_copy(work[0:NS, 0, TT * NH:], ps[0:NS, 4, TT * NH:(TT + 1) * NH]).then_inc(hn_done, 1)
            dve.wait_ge(hn_done, Z + 1)
            nc.vector.scalar_tensor_tensor(out=work[:, 1], in0=work[:, 0], scalar=-1.0, in1=work[:, 0],
                                           op0=ALU.mult, op1=ALU.max).then_inc(zab_done, 1)
            z_, e_, s_, s2 = (work[:, n] for n in range(4))
            dve.wait_ge(e_done, 1)
            link(nc.vector.tensor_scalar(s2, e_, 2.0, None, ALU.add))
            link(nc.vector.reciprocal(s2, s2))
            link(nc.vector.tensor_tensor(s_, e_, s2, ALU.mult))
            link(nc.vector.tensor_tensor(s2, s_, s_, ALU.mult))
            link(nc.vector.tensor_scalar(e_, s2, 1.0 / (2 * ATANH_TERMS - 1), None, ALU.mult))
            for n in range(ATANH_TERMS - 2, 0, -1):
                link(nc.vector.scalar_tensor_tensor(out=e_, in0=e_, scalar=1.0 / (2 * n + 1), in1=s2, op0=ALU.add, op1=ALU.mult))
            link(nc.vector.scalar_tensor_tensor(out=s_, in0=e_, scalar=1.0, in1=s_, op0=ALU.add, op1=ALU.mult))
            link(nc.vector.tensor_scalar(z_, z_, 0.0, None, ALU.min))
            link(nc.vector.scalar_tensor_tensor(out=lf[:].rearrange("p t h -> p (t h)"), in0=s_, scalar=-2.0, in1=z_,
                                                op0=ALU.mult, op1=ALU.add))
            for e in range(2):
                last = nc.vector.tensor_copy(lfd[:, :, DH * e:DH * e + NH], lf[:, 0:TT, :])
            last.then_inc(c_ready, 1)
            memory_rows(1)

            def head_pass(z0, first, gain, i):
                lo(C_FOX - Z + z0 + 2, i)
                finish_head(z0, qkT[:, bass.ds(first + 2 * i, 1), :].rearrange("p o n -> p (o n)"), gain, z0 - 1, i)
            for first, gain in ((0, V_MQ + 2), (HP, V_MQ + 3)):
                with dve.Fori(0, HP // 2) as i:
                    steps.enter(i, 2)
                    for s in range(2):
                        head_pass(Z + 1 + first + s, first + s, gain, i)
                steps.leave(HP // 2)
            for hp in range(HP):
                z = Z + 1 + 2 * HP + hp
                lo(C_FOX - Z + z + 2)
                dve.wait_ge(hn_ready, z + 1)
                nc.vector.tensor_copy(vtok[:, 0:TT, hp * P:(hp + 1) * P], ps[:, 4, 0:TT * P].rearrange("p (t n) -> p t n", t=TT))
                nc.vector.tensor_copy(vtok[0:NS, TT, hp * P:(hp + 1) * P], ps[0:NS, 5, 0:P]).then_inc(hn_done, 1)
                if hp < KD // 2:
                    memory_gain(1, hp)
                    memory_lo(1, hp)
            for hp in range(MP):
                z = Z + 1 + 3 * HP + hp
                if z - Z + C_FOX + 2 <= C_MEM1:
                    lo(C_FOX - Z + z + 2)
                finish_head(z, mb1["qm"][:, hp], V_MQ + 1, MP + 2 * HP + hp)

            def k_rows(t):
                rows = P if t < TT else NS
                if t >= 2:
                    dve.wait_ge(k_stored[t % 2], 16 * (t // 2))
                for first, count in ((0, 4), (4, HP - 4)):
                    bank = group()
                    nc.vector.tensor_copy(ktok[0:rows, t % 2, first * P:(first + count) * P], bank[0:rows, 0:count * P]).then_inc(tr_free, 1)
                marks["k", t] = tr[0]
            memory_chunks(1, k_rows)
            k_rows(TT)
            bank = group()
            nc.vector.tensor_copy(ctok[:, 0:TT, :].rearrange("p t h -> p (t h)"), bank[:, 0:TT * NH])
            nc.vector.tensor_copy(ctok[0:NS, TT, :], bank[0:NS, TT * NH:(TT + 1) * NH]).then_inc(tr_free, 1)
            dve.wait_ge(tr_free, tr[0])
            nc.vector.tensor_scalar(ncx[:], ctok[0:NS, TT, :].unsqueeze(2).broadcast_to([NS, NH, NQ]), -1.0, None, ALU.mult)
            nc.vector.tensor_tensor(cqA[:], ctok[0:NS, TT, :].unsqueeze(2).broadcast_to([NS, NH, NQ]),
                                    dq[:].unsqueeze(1).broadcast_to([NS, NH, NQ]), ALU.mult).then_inc(c_done, 1)
            bank = group()
            nc.vector.tensor_scalar(ncT[:], bank, -1.0, None, ALU.mult).then_inc(tr_free, 1)
            bank = group()
            nc.vector.tensor_copy(cqr[:], bank[0:ROWS, 0:NB])
            nc.vector.tensor_copy(mshift[:], bank[0:ROWS, NB:NB + NS - NQ + NS]).then_inc(tr_free, 1)
            marks["forget"] = tr[0]
            memory_kv(1)
            attend(u, MEM_UNITS, mb1, len(MEM_UNITS))
            sample_memory(1, u + len(MEM_UNITS))
            marks["far"] = tr[0]
            u += len(MEM_UNITS) + GR

            dve.wait_ge(lf_in, 16 * NB * NP)
            nc.vector.tensor_reduce(lftot[:], lfrow[:].rearrange("n (k h) -> n h k", h=NH), AX_X, ALU.add).then_inc(lftot_done, 1)
            dve.wait_ge(stored, 16 * marks["km stored"])
            for g in range(NH // 4):
                bank = group()
                nc.vector.tensor_copy(lfT[:, 4 * g:4 * g + 4, :].rearrange("p h n -> p (h n)"), bank).then_inc(tr_free, 1)
            dve.wait_ge(tr_free, tr[0])
            for g in range(NH // 4):
                bank = group()
                nc.vector.tensor_copy(rtok[:, 4 * g:4 * g + 4, :].rearrange("p h n -> p (h n)"), bank).then_inc(tr_free, 1)
            attend(u, FOX_UNITS, mb1, 2 * len(MEM_UNITS))

            def keys_T(b, c):
                dve.wait_ge(kt_ready, 3 * (NCH * b + c) + 1)
                if c >= 2 or not (isinstance(b, int) and b == 0):
                    dve.wait_ge(sc_ready, NCH * b + c - 1)
                nc.vector.tensor_copy(kT[:, c % 2, 0:2, :].rearrange("p a n -> p (a n)"), ps[:, 0, :]).then_inc(kt_ev_v, 1)
                r = rtok[:, :, bass.ds(NP * b + CPG * c, CPG)].rearrange("p h n -> p n h")
                for pp in range(CPG):
                    last = nc.vector.tensor_copy(rx[:, c % 2, pp], r[:, pp].unsqueeze(2).broadcast_to([P, NH, NQ]))
                last.then_inc(rx_done, 1)

            def begin(b):
                for e in range(2):
                    for odd in range(2):
                        r = slice(DH * e, DH * e + DH)
                        col = (2 * odd + e) * NQ
                        nc.vector.tensor_copy(qx[r, :, col:col + NQ].rearrange("p (a o) q -> p a o q", o=2)[:, :, odd, :],
                                              qkT[r, 0:HP, bass.ds(SEQ + NQ * b, NQ)].rearrange("p (a o) q -> p a o q", o=2)[:, :, odd, :])
                nc.vector.tensor_copy(stat[0:ROWS, 56:57], cqr[:, bass.ds(b, 1)]).then_inc(qx_done, 1)
                for c in range(2):
                    keys_T(b, c)

            def scale_output(b):
                dve.wait_ge(o_ready, b + 1)
                nc.vector.tensor_scalar(os_[:], ps[0:ROWS, 5, 0:4 * DH], stat[0:ROWS, 62:63], None, ALU.mult).then_inc(o_done, 1)

            def output(b):
                dve.wait_ge(oT_hi, GR * 2 + 1 + b)
                for s in range(2):
                    for e in range(2):
                        r = slice(DH * e, DH * e + DH)
                        to = bass.ds(SEQ + NQ * b, NQ)
                        col = (2 * s + e) * NQ
                        src = ps[r, 5, s * ROWS:(s + 1) * ROWS].rearrange("p (j c) -> p j c", c=QR)[:, :, col:col + NQ]
                        last = nc.vector.tensor_tensor(aL[r, 0:HP, to].rearrange("p (j s) q -> p j s q", s=2)[:, :, s, :], src,
                                                       aH[r, 0:HP, to].rearrange("p (j s) q -> p j s q", s=2)[:, :, s, :].bitcast(F32), ALU.subtract)
                last.then_inc(stage_done, 1)

            def sequence(b, first, last_one):
                link(nc.vector.tensor_copy(maskb[:], mshift[:, bass.ds(NS - NQ - NQ * b, NS)]))
                keys_T(b, 2)
                for c in range(NCH):
                    if 2 < c + 1 < NCH:
                        keys_T(b, c + 1)
                    dve.wait_ge(sc_ready, NCH * b + c + 1)
                    nc.vector.tensor_scalar(S[:, c * KEYS:(c + 1) * KEYS], ps[0:ROWS, 3 + c % 2, 0:KEYS], stat[0:ROWS, 56:57], None,
                                            ALU.add).then_inc(sc_free, 1)
                dve.wait_ge(sn_ready, b + 1)
                link(nc.vector.scalar_tensor_tensor(out=S[:, NPAST:NPAST + NS], in0=ps[0:ROWS, 7, 0:NS], scalar=stat[0:ROWS, 56:57],
                                                    in1=maskb[:], op0=ALU.add, op1=ALU.add))
                nc.vector.tensor_reduce(stat[0:ROWS, 60:61], S[:], AX_X, ALU.max, negate=True).then_inc(smax_done, 1)
                if not first:
                    scale_output(b - 1)
                if not last_one:
                    begin(b + 1)
                if not first:
                    output(b - 1)
                dve.wait_ge(sexp_done, b + 1)
                link(nc.vector.reciprocal(stat[0:ROWS, 62:63], stat[0:ROWS, 61:62]))
                for g in range(4):
                    dve.wait_ge(pt_ready, 4 * b + g + 1)
                    n = min(5, NP - 5 * g)
                    last = nc.vector.tensor_copy(pTs[:, 5 * g:5 * g + n, :].rearrange("p k r -> p (k r)"), ps[:, 6 + g % 2, 0:n * ROWS])
                    if g == 3:
                        last = nc.vector.tensor_copy(pTs[0:NS, NP, :], ps[0:NS, 6 + g % 2, n * ROWS:(n + 1) * ROWS])
                    last.then_inc(pt_free, 1)
            begin(0)
            sequence(0, True, False)
            with dve.Fori(0, NB - 2) as i:
                steps.enter(i, 3)
                sequence(i + 1, False, False)
            steps.leave(NB - 2)
            sequence(NB - 1, False, True)
            scale_output(NB - 1)
            output(NB - 1)
            lo(C_WO1)
            residual(C_WO1, 1, 3)
            norm(3)
            ffn(1)
            residual(C_DN1, 2, 4)
            for t in range(TT + 1):
                rows = P if t < TT else NS
                if t >= 2:
                    dve.wait_ge(y_stored[t % 2], 16 * (t // 2))
                for q in range(KD // 4):
                    bank = group()
                    nc.vector.tensor_copy(ystage[0:rows, t % 2, 4 * q * P:4 * (q + 1) * P], bank[0:rows, :]).then_inc(tr_free, 1)
                marks["y", t] = tr[0]

        @block.scalar
        def _(act):
            def hi(n0, i=0):
                s, size = n0 % 2, chunk_size(n0)
                act.wait_ge(raw_in[s], 16 * (n0 // 2 + 1) + 16 * i)
                if n0 >= 2:
                    act.wait_ge(w_used, n0 - 1 + 2 * i)
                nc.scalar.activation(wH[s][:, 0:size], raw[:, s, 0:size], ACT.Copy).then_inc(hi_done, 1)

            def square(r, j0, i=0):
                act.wait_ge(x_new, KD * (r - 1) + j0 + 1 + 2 * i)
                if j0 >= 2:
                    act.wait_ge(sq_added, (KD - 1) * (r - 1) + j0 - 1 + 2 * i)
                x = xT[:, bass.ds(j0 + 2 * i, 1), :].rearrange("p o n -> p (o n)")
                nc.scalar.activation(sq[:, j0 % 2], x, ACT.Square).then_inc(sq_done, 1)

            def norm(r):
                act.wait_ge(ss_ready, r + 1)
                nc.scalar.activation(halves(rb[:]), ps[:, 4:6, 0:HT], ACT.Sqrt, bias=eps[:, 0:1]).then_inc(norm_root, 1)
                for k in range(KD):
                    act.wait_ge(v_done, KD * r + k + 1)
                    nc.scalar.activation(aH[:, k], tmp[:, k % 2], ACT.Copy).then_inc(vH_done, 1)

            def head_tile(z0, i=0):
                chunk = z0 + (2 * KC if z0 < MP else C_FOX - MP)
                act.wait_ge(w_used, chunk + 1 + 2 * i)
                if z0 >= 2:
                    act.wait_ge(hn_done, z0 - 1 + 2 * i)
                nc.scalar.activation(halves(tmp[:, z0 % 2]), acc(z0 % 2), ACT.Copy)
                nc.scalar.activation(halves(sq[:, z0 % 2]), acc(z0 % 2), ACT.Square).then_inc(z_done, 1)

            def head_norm(z0, i=0):
                act.wait_ge(hn_ready, z0 + 1 + 2 * i)
                if z0:
                    act.wait_ge(hn_done, z0 + 2 * i)
                nc.scalar.activation(halves(rb[:]), ps[:, 4:6, 0:HT], ACT.Sqrt, bias=eps[:, 1:2]).then_inc(head_root, 1)

            def memory_rows(l):
                mb = MBS[l]
                act.wait_ge(mem_in, 16 * (l + 1))
                for t in range(MT):
                    nc.scalar.activation(mb["stage"][:, :, :], mb["mem"][:, t].rearrange("p (s n) -> p s n", s=2), ACT.Square,
                                         accum_out=stat[:, 32 + t:33 + t]).then_inc(ms_done, 1)
                    act.wait_ge(ms_done, MT * l + t + 1)
                nc.scalar.activation(stat[:, 34:34 + MT], stat[:, 32:32 + MT], ACT.Sqrt, bias=eps[:, 0:1]).then_inc(mem_root, 1)

            def memory_split(l, g):
                mb = MBS[l]
                act.wait_ge(tr_free, marks["memory", l, g])
                nc.scalar.activation(mb["mH"][:, 2 * g:2 * g + 2, :].rearrange("p k n -> p (k n)"), mb["stage"][:, g % 2, :],
                                     ACT.Copy).then_inc(mH_done, 1)

            def memory_kv(l):
                mb = MBS[l]
                act.wait_ge(w_used, C_MEM[l] + N_MEM)
                nc.scalar.activation(mb["vm"][:], ps[:, 0:MT, MW:2 * MW], ACT.Copy)
                nc.scalar.activation(sq[:, :, 0:MW], ps[:, 0:MT, 0:MW], ACT.Square).then_inc(kvsq_done, 1)
                act.wait_ge(kss_done, l + 1)
                nc.scalar.activation(stat[:, 44:44 + MT * MH], stat[:, 36:36 + MT * MH], ACT.Sqrt, bias=eps[:, 1:2]).then_inc(k_root, 1)

            def exps(u, unit, mb):
                kind, hp, t, keys = unit
                st = stat[:, 8 * (u % 2):8 * (u % 2) + 8]
                act.wait_ge(at_max, u + 1)
                for e in range(2):
                    src = mb["prob"][:, u % 2, e, 0:keys] if kind == "fox" else score_bank(u, e, keys)
                    last = nc.scalar.activation(mb["prob"][:, u % 2, e, 0:keys], src, ACT.Exp, bias=st[:, e:e + 1],
                                                accum_out=st[:, 2 + e:3 + e])
                last.then_inc(at_exp, 1)

            def attend(u0, units, mb, beside=lambda i: None):
                for i in range(2):
                    exps(u0 + i, units[i], mb)
                for i, (kind, hp, t, keys) in enumerate(units):
                    u = u0 + i
                    tile = hp if kind == "fox" else KC + hp
                    act.wait_ge(at_pv, u + 1)
                    nc.scalar.activation(aH[:, tile, t * P:(t + 1) * P], ps[:, 4 + u % 2, 0:P], ACT.Copy).then_inc(at_hi, 1)
                    if i + 2 < len(units):
                        exps(u + 2, units[i + 2], mb)
                    beside(i)

            def sample_memory(l, u0):
                mb = MBS[l]
                for G in range(GR):
                    u = u0 + G
                    st = stat[:, 8 * (u % 2):8 * (u % 2) + 8]
                    act.wait_ge(at_max, u + 1)
                    nc.scalar.activation(mb["prob"][:, u % 2, 0, 0:NM], ps[:, u % 2, 0:NM], ACT.Exp, bias=st[:, 0:1],
                                         accum_out=st[:, 2:3]).then_inc(at_exp, 1)
                    g = marks["sample memory", l, G]
                    act.wait_ge(tr_ready, g + 1)
                    bank = ps[:, 6 + g % 2, :]
                    for s in range(MP):
                        for e in range(2):
                            r = slice(DH * e, DH * e + DH)
                            src = bank[r, s * P:(s + 1) * P].rearrange("p (b h q) -> p b h q", b=GS, h=MH)[:, :, 2 * s + e, :]
                            to = slice(SEQ + G * GS * NQ, SEQ + (G + 1) * GS * NQ)
                            last = nc.scalar.activation(aH[r, KC + s, to].rearrange("p (b q) -> p b q", b=GS), src, ACT.Copy)
                    last.then_inc(oT_hi, 1)

            def residual(c0, per_tile, r):
                def tile(j0, i):
                    for s in range(per_tile):
                        n0 = c0 + per_tile * j0 + s + 1
                        if n0 < C_END:
                            hi(n0, i if per_tile == 1 else 2 * i)
                    if r < 4:
                        square(r, j0, i)
                for j in range(2):
                    tile(j, 0)
                with act.Fori(0, KD // 2 - 2) as i:
                    for j in range(2, 4):
                        tile(j, i)
                for j in range(KD - 2, KD):
                    tile(j, 0)

            def ffn(l):
                c0, g0 = C_GU[l], l * KF

                def tile(f0, i):
                    hi(c0 + 2 * f0 + 1, 2 * i)
                    hi(c0 + 2 * f0 + 2, 2 * i)
                    if g0 + f0 >= 2:
                        act.wait_ge(g_done, g0 + f0 - 1 + 2 * i)
                    nc.scalar.activation(halves(sq[:, f0 % 2]), acc(2 * (f0 % 2)), ACT.Silu).then_inc(silu_done, 1)
                    act.wait_ge(g_done, g0 + f0 + 1 + 2 * i)
                    f = bass.ds(f0 + 2 * i, 1)
                    nc.scalar.activation(gH[:, f, :].rearrange("p o n -> p (o n)"), tmp[:, f0 % 2], ACT.Copy).then_inc(gH_done, 1)
                for f in range(2):
                    tile(f, 0)
                with act.Fori(0, KF2 - 2) as i:
                    for f in range(2, 4):
                        tile(f, i)
                for f in range(KF - 2, KF):
                    tile(f, 0)

            xp = x_prompt[0].rearrange("(t p) n -> p t n", p=P)
            for t in range(TT):
                act.dma_start(xin[:, t], xp[:, t]).then_inc(x_in[t], 16)
            act.dma_start(xin[0:NS, TT], x_sample.rearrange("b q n -> (b q) n")).then_inc(x_in[TT], 16)
            loads = 0
            for at_row, v in ((V_N1, norm1), (V_N2, norm2), (V_MEM, mem_norm), (V_DWB, conv_dw_b), (V_LNG, conv_ln_g), (V_LNB, conv_ln_b)):
                rows = v.rearrange("l (k n) -> (l k) n", n=P)
                act.dma_start(vrow[at_row:at_row + rows.shape[0], :], rows).then_inc(vec_in, 16)
                loads += 1
            for row, v in ((V_MQ, mem_q_norm[0:1]), (V_MQ + 1, mem_q_norm[1:2]), (V_MQ + 2, fox_q_norm), (V_MQ + 3, fox_k_norm)):
                for e in range(2):
                    act.dma_start(vrow[row:row + 1, DH * e:DH * e + DH], v).then_inc(vec_in, 16)
                    loads += 1
            act.dma_start(dwrow[:], conv_dw[0]).then_inc(vec_in, 16)
            for l in range(2):
                act.dma_start(gk_row[:, l, :], mem_k_norm[l:l + 1, :].broadcast_to([P, DH])).then_inc(vec_in, 16)
            act.dma_start(bf[:], fox_b_f.rearrange("o h -> h o")).then_inc(vec_in, 16)
            assert loads + 4 == VEC_LOADS
            for G in range(GR):
                act.dma_start(crow[:, G, :], cache_conv[0, G * GS:(G + 1) * GS].rearrange("b n c -> (b n) c")).then_inc(hist_in, 16)

            act.wait_ge(consts, CONSTS0)
            hi(0)
            memory_rows(0)
            for j in range(KD):
                act.wait_ge(tr_free, 2 * (TT + 1))
                if j >= 2:
                    act.wait_ge(sq_used, j - 1)
                nc.scalar.activation(sq[:, j % 2], xT[:, j], ACT.Square).then_inc(sq_done, 1)
                if j >= 4:
                    memory_split(0, j - 4)
            norm(0)

            def y_begin(c0, i=0):
                c = c0 + 2 * i
                act.wait_ge(taps_ready, c0 + 1 + 2 * i)
                bias = vec[:, bass.ds(V_DWB + c0 + 2 * i, 1)]
                y = yc[:, bass.ds(c, 1), :].rearrange("p o n -> p (o n)")
                nc.scalar.activation(y[:, 0:SEQ], ps[:, 4 * (c0 % 2), 0:SEQ], ACT.Identity, bias=bias)
                nc.scalar.activation(y[:, SEQ:T], ps[:, 4 * (c0 % 2) + 1, 0:NS], ACT.Identity, bias=bias).then_inc(y_begun, 1)

            def gate(c0, i=0):
                act.wait_ge(w_used, 2 * c0 + 2 + 4 * i)
                if c0 >= 2:
                    act.wait_ge(u_done, c0 - 1 + 2 * i)
                nc.scalar.activation(halves(sq[:, c0 % 2]), acc(2 * (c0 % 2) + 1), ACT.Sigmoid).then_inc(sig_done, 1)
                hi(C_CONV + 2 * c0 + 3, 2 * i)
                if c0:
                    y_begin(c0 - 1, i)
                if c0 < KC - 1:
                    hi(C_CONV + 2 * c0 + 4, 2 * i)
            for n in range(1, 3):
                hi(C_CONV + n)
            for c in range(2):
                gate(c)
            with act.Fori(0, KC // 2 - 2) as i:
                for c in range(2, 4):
                    gate(c, i)
            gate(KC - 2)
            gate(KC - 1)
            y_begin(KC - 1)
            hi(C_CONV + 2 * KC + 2)
            act.wait_ge(u_done, KC)
            for z in range(MP):
                head_tile(z)
            head_norm(0)
            hi(C_MEM0 + 1)
            for c in range(KC):
                last = nc.scalar.activation(usc[:, c], uS[:, c, :, NQ:NQ + H], ACT.Copy)
            last.then_inc(usc_done, 1)
            head_norm(1)
            for i in range(1, N_MEM):
                hi(C_MEM0 + 1 + i)
            memory_kv(0)
            def layer_norm(i):
                if i < KC // 2:
                    for c in (2 * i, 2 * i + 1):
                        act.wait_ge(lny_done, c + 1)
                        if c >= 2:
                            act.wait_ge(ysq_used, c - 1)
                        nc.scalar.activation(sq[:, c % 2], yc[:, c], ACT.Square).then_inc(ysq_done, 1)
            attend(0, MEM_UNITS, mb0, layer_norm)
            act.wait_ge(ln_ready, 2)
            nc.scalar.activation(halves(rb[:]), ps[:, 2:4, 0:HT], ACT.Sqrt, bias=eps[:, 2:3], scale=1.0 / CH).then_inc(ln_root, 1)
            sample_memory(0, len(MEM_UNITS))
            for c in range(KC):
                act.wait_ge(lny_done, KC + c + 1)
                nc.scalar.activation(yc[:, c], yc[:, c], ACT.Silu, bias=vec[:, V_LNB + c:V_LNB + c + 1]).then_inc(swish_done, 1)
                act.wait_ge(swish_done, c + 1)
                nc.scalar.activation(aH[:, c], yc[:, c], ACT.Copy).then_inc(mixf_done, 1)
            residual(C_WO0, 1, 1)
            norm(1)
            ffn(0)
            residual(C_DN0, 2, 2)
            norm(2)

            Z = MP
            hi(C_FOX + 1)
            act.wait_ge(w_used, C_FOX + 1)
            nc.scalar.activation(tmp[0:NH, Z % 2, :].rearrange("p (a n) -> p a n", a=2), acc(Z % 2)[0:NH], ACT.Identity,
                                 bias=bf[:, 0:1]).then_inc(z_done, 1)
            hi(C_FOX + 2)
            head_tile(Z + 1)
            act.wait_ge(zab_done, 1)
            nc.scalar.activation(work[:, 1], work[:, 1], ACT.Exp, scale=-1.0).then_inc(e_done, 1)
            memory_rows(1)

            def head_pass(z0, i=0):
                hi(z0 - Z + C_FOX + 1, i)
                head_tile(z0, i)
                head_norm(z0 - 1, i)
            with act.Fori(0, HP) as i:
                for z in range(2):
                    head_pass(Z + 2 + z, i)
            for n in range(2 * HP + 2, N_FOX):
                if n - 1 <= 3 * HP:
                    hi(C_FOX + n + 1)
                    head_tile(Z + n)
                else:
                    head_pass(Z + n)
                if n - 2 * HP - 2 < KD // 2:
                    memory_split(1, n - 2 * HP - 2)
            for i in range(N_MEM - 1):
                hi(C_MEM1 + 1 + i)
                if i == 0:
                    head_norm(Z + N_FOX - 1)
            memory_kv(1)
            u = len(MEM_UNITS) + GR
            attend(u, MEM_UNITS, mb1)
            sample_memory(1, u + len(MEM_UNITS))
            u += len(MEM_UNITS) + GR
            attend(u, FOX_UNITS, mb1)

            def keys_T(b, c):
                for g in (1, 2):
                    act.wait_ge(kt_ready, 3 * (NCH * b + c) + g + 1)
                    if g == 1 and (c >= 2 or not (isinstance(b, int) and b == 0)):
                        act.wait_ge(sc_ready, NCH * b + c - 1)
                    nc.scalar.activation(kT[:, c % 2, 2 * g:2 * g + 2, :].rearrange("p a n -> p (a n)"), ps[:, g, :],
                                         ACT.Copy).then_inc(kt_ev_a, 1)

            def output(b):
                act.wait_ge(oT_ready, b + 1)
                for s in range(2):
                    for e in range(2):
                        r = slice(DH * e, DH * e + DH)
                        to = bass.ds(SEQ + NQ * b, NQ)
                        col = (2 * s + e) * NQ
                        src = ps[r, 5, s * ROWS:(s + 1) * ROWS].rearrange("p (j c) -> p j c", c=QR)[:, :, col:col + NQ]
                        last = nc.scalar.activation(aH[r, 0:HP, to].rearrange("p (j s) q -> p j s q", s=2)[:, :, s, :], src, ACT.Copy)
                last.then_inc(oT_hi, 1)

            def sequence(b, first, last_one):
                for c in range(2, NCH):
                    keys_T(b, c)
                if not last_one:
                    keys_T(b + 1, 0)
                act.wait_ge(smax_done, b + 1)
                nc.scalar.activation(S[:], S[:], ACT.Exp, bias=stat[0:ROWS, 60:61],
                                     accum_out=stat[0:ROWS, 61:62]).then_inc(sexp_done, 1)
                if not last_one:
                    keys_T(b + 1, 1)
                if not first:
                    output(b - 1)
            for c in range(2):
                keys_T(0, c)
            sequence(0, True, False)
            with act.Fori(0, NB - 2) as i:
                sequence(i + 1, False, False)
            sequence(NB - 1, False, True)
            output(NB - 1)
            hi(C_WO1)
            residual(C_WO1, 1, 3)
            norm(3)
            ffn(1)
            residual(C_DN1, 2, 4)

        @block.tensor
        def _(pe):
            tr = [0]

            def transposes(jobs):
                g = tr[0]
                tr[0] += 1
                if g >= 2:
                    pe.wait_ge(tr_free, g - 1)
                col = 0
                for src in jobs:
                    n, m = src.shape[0], 1
                    for x in src.shape[1:]:
                        m *= x
                    last = nc.tensor.transpose(ps[0:m, 6 + g % 2, col:col + n], src, ident[0:n, 0:n])
                    col += n
                last.then_inc(tr_ready, 1)
                return g

            def product(n0, i, slot, H_, L_, k0, ks, first, last, ready=None):
                s = n0 % 2
                pe.wait_ge(lo_done, n0 + 1 + 2 * i)
                for k in range(ks):
                    if ready is not None:
                        limit = KC if ready[0] is stage_done else KD
                        pe.wait_ge(ready[0], ready[1] + min(k + 1, limit))
                    w = slice(k * P, (k + 1) * P)
                    for weights, acts in ((wH[s], (H_, L_)), (wL[s], (H_,))):
                        for a in acts:
                            for h in range(2):
                                mm = nc.tensor.matmul(ps[:, 2 * slot + h, 0:HT], weights[:, w], a[:, k0 + k, h * HT:(h + 1) * HT],
                                                      start=(first and k == 0 and weights is wH[s] and a is H_),
                                                      stop=(last and k == ks - 1 and weights is wL[s]))
                mm.then_inc(w_used, 1)

            def sum_squares(r):
                pe.wait_ge(sq_added, (KD - 1) * r)
                pe.wait_ge(sq_done, KD * (r + 1))
                for n, src in enumerate((rb[:], sq[:, (KD - 1) % 2])):
                    for h in range(2):
                        mm = nc.tensor.matmul(ps[:, 4 + h, 0:HT], ones[:], src[:, h * HT:(h + 1) * HT], start=(n == 0), stop=(n == 1))
                mm.then_inc(ss_ready, 1)

            def residual(c0, per_tile, r, k0s, ready=None):
                def tile(j0, i=0, ready=None):
                    if j0 >= 2:
                        pe.wait_ge(x_new, KD * (r - 1) + j0 - 1 + 2 * i)
                    H_, L_ = (aH, aL) if per_tile == 1 else (gH, gL)
                    for s in range(per_tile):
                        product(c0 + per_tile * j0 + s, i if per_tile == 1 else 2 * i, j0 % 2, H_, L_, k0s[s],
                                KD if per_tile == 1 else KF2, s == 0, s == per_tile - 1, ready)
                tile(0, ready=ready)
                tile(1)
                with pe.Fori(0, KD // 2 - 1) as i:
                    for j in range(2, 4):
                        tile(j, i)
                if r < 4:
                    sum_squares(r)

            def ffn(l):
                c0, g0 = C_GU[l], l * KF

                def tile(f0, i=0, ready=None):
                    if g0 + f0 >= 2:
                        pe.wait_ge(g_done, g0 + f0 - 1 + 2 * i)
                    for s in range(2):
                        product(c0 + 2 * f0 + s, 2 * i, 2 * (f0 % 2) + s, aH, aL, 0, KD, True, True, None if s else ready)
                tile(0, ready=(a_ready, KD * (2 * l + 1)))
                tile(1)
                with pe.Fori(0, KF2 - 1) as i:
                    for f in range(2, 4):
                        tile(f, i)
                pe.wait_ge(gL_done, KF * (l + 1))

            def head_sums(z0, i=0):
                pe.wait_ge(z_done, z0 + 1 + 2 * i)
                if z0:
                    pe.wait_ge(hn_done, z0 + 2 * i)
                for h in range(2):
                    mm = nc.tensor.matmul(ps[:, 4 + h, 0:HT], blocks[:], sq[:, z0 % 2, h * HT:(h + 1) * HT], start=True, stop=True)
                mm.then_inc(hn_ready, 1)

            def memory_rows(l, g):
                mb = MBS[l]
                pe.wait_ge(mn_done, l + 1)
                transposes([mb["mem"][:, t, k * P:(k + 1) * P] for k in (2 * g, 2 * g + 1) for t in range(MT)])

            def memory_chunks(l, between):
                mb = MBS[l]
                for i in range(N_MEM):
                    n = C_MEM[l] + i
                    pe.wait_ge(lo_done, n + 1)
                    pe.wait_ge(mL_done, l * KD // 2 + (KM * i + KM - 1) // 2 + 1)
                    for kk in range(KM):
                        k = KM * i + kk
                        w = slice(kk * 2 * MW, (kk + 1) * 2 * MW)
                        for t in range(MT):
                            for m_, w_ in ((mb["mH"], wH), (mb["mH"], wL), (mb["mL"], wH)):
                                mm = nc.tensor.matmul(ps[:, t, :], m_[:, k, t * P:(t + 1) * P], w_[n % 2][:, w],
                                                      start=(k == 0 and m_ is mb["mH"] and w_ is wH),
                                                      stop=(k == KD - 1 and m_ is mb["mL"]))
                    mm.then_inc(w_used, 1)
                    between(i)

            def memory_kv(l):
                mb = MBS[l]
                pe.wait_ge(kv_done, l + 1)
                transposes([mb["km"][:, t, hp * P:(hp + 1) * P] for hp in range(MP) for t in range(MT)])

            def scores(u, unit, mb):
                kind, hp, t, keys = unit
                if u >= 2:
                    pe.wait_ge(at_exp, u - 1)
                for e in range(2):
                    r = slice(DH * e, DH * e + DH)
                    q = qkT[r, hp, t * P:(t + 1) * P] if kind == "fox" else mb["qm"][r, hp, t * P:(t + 1) * P]
                    k = qkT[r, HP + hp, 0:keys] if kind == "fox" else mb["kmT"][r, hp, :]
                    mm = nc.tensor.matmul(score_bank(u, e, keys), q, k, start=True, stop=True)
                mm.then_inc(at_s, 1)

            def broadcast_c(hp):
                for e in range(2):
                    pe.wait_ge(tr_free, tr[0] - 1)
                    h = 2 * hp + e
                    nc.tensor.matmul(ps[:, 6 + tr[0] % 2, :], ident[0:DH, h:h + 1].broadcast_to([DH, P]), ncT[0:DH, :],
                                     start=True, stop=True).then_inc(tr_ready, 1)
                    tr[0] += 1

            def attend(u0, units, mb, beside=lambda i: None):
                if units[0][0] == "fox":
                    broadcast_c(0)
                for i in range(2):
                    scores(u0 + i, units[i], mb)
                for i, (kind, hp, t, keys) in enumerate(units):
                    u = u0 + i
                    pe.wait_ge(at_prob, u + 1)
                    if kind == "mem":
                        transposes([mb["prob"][:, u % 2, e, k * P:(k + 1) * P] for e in range(2) for k in range(MT)])
                    else:
                        for e in range(2):
                            transposes([mb["prob"][:, u % 2, e, k * P:(k + 1) * P] for k in range(t + 1)])
                    if i + 2 < len(units):
                        scores(u + 2, units[i + 2], mb)
                    pe.wait_ge(tr_free, tr[0])
                    if u >= 2:
                        pe.wait_ge(at_lo, u - 1)
                    n = keys // P
                    for k in range(n):
                        for e in range(2):
                            head = slice((2 * hp + e) * DH, (2 * hp + e + 1) * DH)
                            v = vtok[:, k, head] if kind == "fox" else mb["vm"][:, k, head]
                            mm = nc.tensor.matmul(ps[DH * e:DH * e + DH, 4 + u % 2, 0:P], v, mb["pT"][:, e, k, :],
                                                  start=(k == 0), stop=(k == n - 1))
                    mm.then_inc(at_pv, 1)
                    if kind == "fox" and t == 1 and hp + 1 < HP:
                        broadcast_c(hp + 1)
                    beside(i)

            def sample_memory(l, u0):
                mb = MBS[l]
                for G in range(GR):
                    u = u0 + G
                    pe.wait_ge(ks_in, 16 * (GR * l + G + 1))
                    for b in range(GS):
                        transposes([mb["ks"][:, b, k, hp * P:(hp + 1) * P] for hp in range(MP) for k in range(MT)])
                    pe.wait_ge(qd_done, GR * l + G + 1)
                    pe.wait_ge(tr_free, tr[0])
                    pe.wait_ge(at_exp, u - 1)
                    for hp in range(MP):
                        for b in range(GS):
                            mm = nc.tensor.matmul(ps[QR * b:QR * b + QR, u % 2, 0:NM], mb["qd"][:, b, hp, :], mb["ksT"][:, b, hp, :],
                                                  start=(hp == 0), stop=(hp == MP - 1), skip_group_check=True, tile_position=(0, QR * b))
                    mm.then_inc(at_s, 1)
                    pe.wait_ge(at_prob, u + 1)
                    transposes([mb["prob"][:, u % 2, 0, k * P:(k + 1) * P] for k in range(MT)])
                    pe.wait_ge(tr_free, tr[0])
                    pe.wait_ge(at_lo, u - 1)
                    pe.wait_ge(vs_in, 16 * (GR * l + G + 1))
                    for k in range(MT):
                        for b in range(GS):
                            mm = nc.tensor.matmul(ps[QR * b:QR * b + QR, 4 + u % 2, 0:MW], mb["pT"][:, 0, k, QR * b:QR * b + QR],
                                                  mb["vs"][:, b, k, :], start=(k == 0), stop=(k == MT - 1), skip_group_check=True,
                                                  tile_position=(0, QR * b))
                    mm.then_inc(at_pv, 1)
                    pe.wait_ge(at_lo, u + 1)
                    transposes([mb["o"][:, s * P:(s + 1) * P] for s in range(MP)])

            pe.wait_ge(consts, CONSTS0)
            for t in range(TT + 1):
                pe.wait_ge(x_in[t], 16)
                rows = P if t < TT else NS
                for q in range(KD // 4):
                    transposes([xin[0:rows, t, k * P:(k + 1) * P] for k in range(4 * q, 4 * q + 4)])
            def history(n):
                G, (first, count) = n // 2, ((0, 4), (4, KC - 4))[n % 2]
                pe.wait_ge(hist_in, 16 * GR)
                transposes([crow[:, G, c * P:(c + 1) * P] for c in range(first, first + count)])

            for j in range(KD):
                pe.wait_ge(sq_done, j + 1)
                for h in range(2):
                    mm = nc.tensor.matmul(ps[:, 4 + h, 0:HT], ones[:], sq[:, j % 2, h * HT:(h + 1) * HT], start=(j == 0), stop=(j == KD - 1))
                mm.then_inc(sq_used if j < KD - 1 else ss_ready, 1)
                if j == 0:
                    pe.wait_ge(vec_in, 16 * VEC_LOADS)
                    transposes([vrow[:]])
                elif j == 1:
                    transposes([dwrow[:, c * P:(c + 1) * P] for c in range(KC)])
                elif j == 2:
                    history(0)
                elif j < 7:
                    memory_rows(0, j - 3)
                else:
                    history(1)
            for n in range(2, 2 * GR):
                history(n)


            def conv_tile(c0, i=0, ready=None):
                if c0 >= 2:
                    pe.wait_ge(y_begun, c0 - 1 + 2 * i)
                for s in range(2):
                    product(C_CONV + 2 * c0 + s, 2 * i, 2 * (c0 % 2) + s, aH, aL, 0, KD, True, True, None if s else ready)

            def taps(c0, i=0):
                pe.wait_ge(u_done, c0 + 1 + 2 * i)
                pe.wait_ge(diag_ready, c0 + 1 + 2 * i)
                c = bass.ds(c0 + 2 * i, 1)
                n = 2 * PE_TAPS if c0 >= KC - 2 else PE_TAPS
                for j in range(n):
                    uj = uP[:, c, j:j + SEQ].rearrange("p o n -> p (o n)")
                    sj = uS[:, c, :, j:j + NQ].rearrange("p o b n -> p (o b) n")
                    w = (diag, diag2)[j // PE_TAPS][:, c0 % 2, j % PE_TAPS]
                    nc.tensor.matmul(ps[:, 4 * (c0 % 2), 0:SEQ], w, uj, start=(j == 0), stop=(j == n - 1))
                    mm = nc.tensor.matmul(ps[:, 4 * (c0 % 2) + 1, 0:NS].rearrange("p (b n) -> p b n", b=NB), w, sj,
                                          start=(j == 0), stop=(j == n - 1))
                mm.then_inc(taps_ready, 1)
            conv_tile(0, ready=(a_ready, 0))
            pe.wait_ge(tr_free, tr[0])
            conv_tile(1)
            taps(0)
            with pe.Fori(0, KC // 2 - 2) as i:
                for c in range(2, 4):
                    conv_tile(c, i)
                    taps(c - 1, i)
            for c in range(KC - 2, KC):
                conv_tile(c)
                taps(c - 1)
            taps(KC - 1)
            pe.wait_ge(y_begun, KC)
            for z in range(MP):
                product(C_CONV + 2 * KC + z, 0, z % 2, aH, aL, 0, KD, True, True)
            head_sums(0)
            pe.wait_ge(z_done, MP)

            def state(n):
                first, count = ((0, 4), (4, KC - 4))[n % 2]
                if n < 2:
                    transposes([uP[:, c, SEQ:SEQ + H] for c in range(first, first + count)])
                else:
                    G = n // 2 - 1
                    pe.wait_ge(usc_done, 1)
                    transposes([usc[:, c, G * GS:(G + 1) * GS, :].rearrange("p b n -> p (b n)") for c in range(first, first + count)])

            def beside_memory(i):
                if i == 0:
                    head_sums(1)
                else:
                    state(2 * i - 2)
                    state(2 * i - 1)
            memory_chunks(0, beside_memory)
            memory_kv(0)
            pe.wait_ge(hn_done, MP)
            pe.wait_ge(tr_free, tr[0])
            pe.wait_ge(y_done, KC)
            for c in range(KC):
                for h in range(2):
                    mm = nc.tensor.matmul(ps[:, 4 + h, 0:HT], ones[:], yc[:, c, h * HT:(h + 1) * HT], start=(c == 0), stop=(c == KC - 1))
            mm.then_inc(ln_ready, 1)
            pe.wait_ge(mean_done, 1)
            attend(0, MEM_UNITS, mb0)
            pe.wait_ge(ysq_used, KC)
            pe.wait_ge(at_exp, len(MEM_UNITS))
            for h in range(2):
                mm = nc.tensor.matmul(ps[:, 2 + h, 0:HT], ones[:], tmp[:, 0, h * HT:(h + 1) * HT], start=True, stop=True)
            mm.then_inc(ln_ready, 1)
            sample_memory(0, len(MEM_UNITS))
            pe.wait_ge(at_exp, len(MEM_UNITS) + GR)
            pe.wait_ge(at_lo, len(MEM_UNITS) + GR)
            pe.wait_ge(tr_free, tr[0])
            residual(C_WO0, 1, 1, (0,), (stage_done, 0))
            ffn(0)
            residual(C_DN0, 2, 2, (0, KF2))

            Z = MP

            def tile(z0, i=0, ready=None):
                pe.wait_ge(z_done, z0 - 1 + 2 * i)
                product(C_FOX - Z + z0, i, z0 % 2, aH, aL, 0, KD, True, True, ready)
            tile(Z, ready=(a_ready, KD * 2))
            tile(Z + 1)
            pe.wait_ge(z_done, Z + 1)
            pe.wait_ge(hn_done, Z)
            for t in range(TT + 1):
                n = P if t < TT else NS
                mm = nc.tensor.transpose(ps[0:n, 4, t * NH:(t + 1) * NH], tmp[0:NH, Z % 2, t * P:t * P + n], ident[0:NH, 0:NH])
            mm.then_inc(hn_ready, 1)
            with pe.Fori(0, HP - 1) as i:
                for n in range(2, 4):
                    tile(Z + n, i)
                    head_sums(Z + n - 1, i)
            tile(Z + 2 * HP)
            head_sums(Z + 2 * HP - 1)
            for n in range(2 * HP + 1, N_FOX + 1):
                if n < N_FOX:
                    tile(Z + n)
                z = Z + n - 1
                if n - 1 in range(2 * HP + 1, 3 * HP + 1):
                    pe.wait_ge(z_done, z + 1)
                    pe.wait_ge(hn_done, z)
                    for t in range(TT + 1):
                        m = P if t < TT else NS
                        mm = nc.tensor.transpose(ps[0:m, 4 + t // TT, (t % TT) * P:(t % TT + 1) * P],
                                                 tmp[:, z % 2, t * P:t * P + m], ident[:])
                    mm.then_inc(hn_ready, 1)
                    if n - 1 - (2 * HP + 1) < KD // 2:
                        memory_rows(1, n - 1 - (2 * HP + 1))
                elif n < N_FOX:
                    head_sums(z)
            def k_rows(t):
                n = P if t < TT else NS
                if t == 0:
                    head_sums(Z + N_FOX - 1)
                    pe.wait_ge(hn_done, Z + 2 * HP + 1)
                for first, count in ((0, 4), (4, HP - 4)):
                    transposes([qkT[:, HP + hp, t * P:t * P + n] for hp in range(first, first + count)])
            pe.wait_ge(z_done, Z + N_FOX)
            memory_chunks(1, k_rows)
            k_rows(TT)
            pe.wait_ge(c_ready, 1)
            pe.wait_ge(tr_free, tr[0] - 1)
            out = ps[:, 6 + tr[0] % 2, :]
            tr[0] += 1
            for t in range(TT):
                for s in range(t + 1):
                    mm = nc.tensor.matmul(out[:, t * NH:(t + 1) * NH], win[:, (TT - 1 - s + t) * P:(TT - s + t) * P], lf[:, s, :],
                                          start=(s == 0), stop=(s == t))
            nc.tensor.matmul(out[0:NS, TT * NH:(TT + 1) * NH], sameq[:], lf[0:NS, TT, :], start=True, stop=True).then_inc(tr_ready, 1)
            pe.wait_ge(tr_free, tr[0] - 1)
            out = ps[:, 6 + tr[0] % 2, :]
            tr[0] += 1
            for s in range(TT):
                mm = nc.tensor.matmul(out, lfd[:, s, :], win[:, (TT - 1 - s) * P:(TT - 1 - s) * P + SEQ], start=(s == 0), stop=(s == TT - 1))
            mm.then_inc(tr_ready, 1)
            pe.wait_ge(c_done, 1)
            pe.wait_ge(tr_free, tr[0] - 1)
            out = ps[:, 6 + tr[0] % 2, :]
            tr[0] += 1
            nc.tensor.matmul(out[0:ROWS, 0:NB], cqA[:].rearrange("p h q -> p (h q)"), bm[:], start=True, stop=True)
            nc.tensor.transpose(out[0:ROWS, NB:NB + 2 * NS - NQ], mshT[:], ident[0:2 * NS - NQ, 0:2 * NS - NQ]).then_inc(tr_ready, 1)
            memory_kv(1)
            pe.wait_ge(hn_done, Z + N_FOX)
            pe.wait_ge(tr_free, tr[0])
            u = len(MEM_UNITS) + GR
            attend(u, MEM_UNITS, mb1)
            sample_memory(1, u + len(MEM_UNITS))
            u += len(MEM_UNITS) + GR
            pe.wait_ge(lf_in, 16 * NB * NP)
            for g in range(NH // 4):
                transposes([lfrow[:].rearrange("n (k h) -> n h k", h=NH)[:, h, :] for h in range(4 * g, 4 * g + 4)])
            pe.wait_ge(tr_free, tr[0])
            pe.wait_ge(lftot_done, 1)
            for g in range(NH // 4):
                pe.wait_ge(tr_free, tr[0] - 1)
                out = ps[:, 6 + tr[0] % 2, :]
                tr[0] += 1
                for h in range(4):
                    nc.tensor.matmul(out[:, h * P:(h + 1) * P], after[:], lfT[:, 4 * g + h, :], start=True, stop=False)
                    mm = nc.tensor.matmul(out[:, h * P:(h + 1) * P], lftot[:, 4 * g + h:4 * g + h + 1].broadcast_to([P, P]), later[:],
                                          start=False, stop=True)
                mm.then_inc(tr_ready, 1)
            attend(u, FOX_UNITS, mb1)
            pe.wait_ge(at_lo, u + len(FOX_UNITS))
            pe.wait_ge(tr_free, tr[0])

            def keys_T(b, c):
                pe.wait_ge(k_in[c % RING], 32 * (NCH // RING * b + c // RING + 1))
                if c or not (isinstance(b, int) and b == 0):
                    pe.wait_ge(kt_ev_v, NCH * b + c)
                    pe.wait_ge(kt_ev_a, 2 * (NCH * b + c))
                for g in range(3):
                    for n in range(4):
                        hp, pp = (4 * g + n) // 2, n % 2
                        mm = nc.tensor.transpose(ps[:, g, n * P:(n + 1) * P], kring[c % RING][:, pp, hp * P:(hp + 1) * P], ident[:])
                    mm.then_inc(kt_ready, 1)

            def step_scores(b, c):
                pe.wait_ge(kt_ev_v, NCH * b + c + 1)
                pe.wait_ge(kt_ev_a, 2 * (NCH * b + c + 1))
                pe.wait_ge(rx_done, NCH * b + c + 1)
                if c >= 2 or not (isinstance(b, int) and b == 0):
                    pe.wait_ge(sc_free, NCH * b + c - 1)
                for odd in range(2):
                    for j in range(3):
                        mm = nc.tensor.matmul(ps[QR * j:QR * j + QR, 3 + c % 2, 0:KEYS], qx[:, 2 * j + odd, :], kT[:, c % 2, 2 * j + odd, :],
                                              start=(odd == 0), stop=False, skip_group_check=True, tile_position=(0, QR * j))
                for pp in range(CPG):
                    for j in range(3):
                        r = rx[:, c % 2, pp, 4 * j:4 * j + 4, :].rearrange("p h q -> p (h q)")
                        mm = nc.tensor.matmul(ps[QR * j:QR * j + QR, 3 + c % 2, pp * P:(pp + 1) * P], r, ident[:],
                                              start=False, stop=(pp == CPG - 1), skip_group_check=True, tile_position=(0, QR * j))
                mm.then_inc(sc_ready, 1)

            def begin(b):
                keys_T(b, 0)
                keys_T(b, 1)
                pe.wait_ge(qx_done, b + 1)
                step_scores(b, 0)
                step_scores(b, 1)

            def values_step(b, c):
                pe.wait_ge(v_in[c % RING], 32 * (NCH // RING * b + c // RING + 1))
                if c == 0:
                    pe.wait_ge(pt_free, 4 * b + 4)
                    if not (isinstance(b, int) and b == 0):
                        pe.wait_ge(stage_done, KC + b)
                for pp in range(CPG):
                    for j in range(3):
                        k = CPG * c + pp
                        mm = nc.tensor.matmul(ps[QR * j:QR * j + QR, 5, 0:4 * DH], pTs[:, k, QR * j:QR * j + QR],
                                              vring[c % RING][:, pp, 4 * DH * j:4 * DH * (j + 1)], start=(k == 0), stop=False,
                                              skip_group_check=True, tile_position=(0, QR * j))
                mm.then_inc(v_used, 1)
                if c == NCH - 1:
                    for j in range(3):
                        mm = nc.tensor.matmul(ps[QR * j:QR * j + QR, 5, 0:4 * DH], pTs[0:NS, NP, QR * j:QR * j + QR],
                                              vtok[0:NS, TT, 4 * DH * j:4 * DH * (j + 1)], start=False, stop=True,
                                              skip_group_check=True, tile_position=(0, QR * j))
                    mm.then_inc(o_ready, 1)

            def output(b):
                pe.wait_ge(o_done, b + 1)
                for s in range(2):
                    mm = nc.tensor.transpose(ps[:, 5, s * ROWS:(s + 1) * ROWS], os_[:, s * P:(s + 1) * P], ident[0:ROWS, 0:ROWS])
                mm.then_inc(oT_ready, 1)

            def sequence(b, first, last_one):
                keys_T(b, 2)
                for c in range(2, NCH):
                    if c + 1 < NCH:
                        keys_T(b, c + 1)
                    step_scores(b, c)
                    if not first:
                        values_step(b - 1, c - 2)
                if not first:
                    pe.wait_ge(pt_free, 4 * b)
                for odd in range(2):
                    for j in range(3):
                        nc.tensor.matmul(ps[QR * j:QR * j + QR, 7, 0:NS], qx[:, 2 * j + odd, :], qkT[:, HP + 2 * j + odd, SEQ:T],
                                         start=(odd == 0), stop=False, skip_group_check=True, tile_position=(0, QR * j))
                for j in range(3):
                    c_k = ncx[:, 4 * j:4 * j + 4, :].rearrange("p h q -> p (h q)")
                    mm = nc.tensor.matmul(ps[QR * j:QR * j + QR, 7, 0:NS], c_k, ident[0:NS, 0:NS], start=False, stop=True,
                                          skip_group_check=True, tile_position=(0, QR * j))
                mm.then_inc(sn_ready, 1)
                if not first:
                    for c in range(NCH - 2, NCH):
                        values_step(b - 1, c)
                if not last_one:
                    begin(b + 1)
                if not first:
                    output(b - 1)
                pe.wait_ge(sexp_done, b + 1)
                for g in range(4):
                    if g >= 2:
                        pe.wait_ge(pt_free, 4 * b + g - 1)
                    n = min(5, NP - 5 * g)
                    for x in range(n):
                        k = 5 * g + x
                        mm = nc.tensor.transpose(ps[:, 6 + g % 2, x * ROWS:(x + 1) * ROWS], S[:, k * P:(k + 1) * P], ident[0:ROWS, 0:ROWS])
                    if g == 3:
                        mm = nc.tensor.transpose(ps[0:NS, 6 + g % 2, n * ROWS:(n + 1) * ROWS], S[:, NPAST:NPAST + NS], ident[0:ROWS, 0:ROWS])
                    mm.then_inc(pt_ready, 1)
            begin(0)
            sequence(0, True, False)
            with pe.Fori(0, NB - 2) as i:
                sequence(i + 1, False, False)
            sequence(NB - 1, False, True)
            for c in range(NCH):
                values_step(NB - 1, c)
            output(NB - 1)
            pe.wait_ge(stage_done, KC + NB)
            residual(C_WO1, 1, 3, (0,))
            ffn(1)
            residual(C_DN1, 2, 4, (0, KF2))
            pe.wait_ge(x_new, KD * 4)
            for t in range(TT + 1):
                n = P if t < TT else NS
                for q in range(KD // 4):
                    transposes([xT[:, k, t * P:t * P + n] for k in range(4 * q, 4 * q + 4)])

        @block.sync
        def _(sp):
            def load(n0, src, i=0):
                s = n0 % 2
                if n0 >= 2:
                    sp.wait_ge(lo_done, n0 - 1 + 2 * i)
                size = src.shape[1] * src.shape[2]
                sp.dma_start(raw[:, s, 0:size].rearrange("p (k n) -> p k n", k=src.shape[1]), src).then_inc(raw_in[s], 16)

            def mem_chunks(l):
                for i in range(N_MEM):
                    load(C_MEM[l] + i, w_mem_kv[l].rearrange("(k p) n -> p k n", p=P)[:, KM * i:KM * i + KM, :])

            def out_chunks(l):
                with sp.Fori(0, KD // 2) as i:
                    for j in range(2):
                        load(C_WO[l] + j, columns(w_out[l], j * P + 2 * P * i), i)

            def ffn_chunks(l):
                with sp.Fori(0, KF) as f:
                    load(C_GU[l], columns(w_gate_up[l], P * f), f)
                    load(C_GU[l] + 1, columns(w_gate_up[l], DF + P * f), f)
                with sp.Fori(0, KD) as j:
                    for s in range(2):
                        load(C_DN[l] + s, columns(w_down[l], P * j, s * KF2, KF2), j)

            def conv_pair(c0, i):
                load(C_CONV + 2 * c0, columns(conv_w_in[0], c0 * P + P * i), i)
                load(C_CONV + 2 * c0 + 1, columns(conv_w_in[0], CH + c0 * P + P * i), i)
            conv_pair(0, 0)
            with sp.Fori(0, KC - 1) as i:
                conv_pair(1, i)
            for z in range(MP):
                load(C_CONV + 2 * KC + z, columns(conv_w_in[0], 2 * CH + z * P))
            mem_chunks(0)
            out_chunks(0)
            ffn_chunks(0)
            w = fox_w_in[0]
            load(C_FOX, columns(w, 3 * CH))
            with sp.Fori(0, 3 * HP // 2) as i:
                for j in range(2):
                    load(C_FOX + 1 + j, columns(w, j * P + 2 * P * i), i)
            for z in range(MP):
                load(C_FOX + 1 + 3 * HP + z, columns(w, 3 * CH + NH + z * P))
            mem_chunks(1)
            sp.wait_ge(pages_in, 16)
            sp.wait_ge(w_used, C_WO1)

            def keys(c, first, read=None):
                which = [sp.value_load(pages[0:1, bass.ds(first + CPG * c + pp, 1)], min_val=0, max_val=N_PHYS - 1) for pp in range(CPG)]
                if read is not None:
                    sp.wait_ge(kt_ready, read)
                for pp in range(CPG):
                    sp.dma_start(kring[c % RING][:, pp, :], cache_fox_k[0, bass.ds(which[pp], 1)].rearrange("o p h d -> (o p) (h d)"))\
                      .then_inc(k_in[c % RING], 16)
            for c in range(RING):
                keys(c, 0)
            with sp.Fori(0, NB - 1) as b:
                for c in range(NCH):
                    keys(c + RING, NP * b, 3 * NCH * b + 3 * (c + 1))
            for c in range(NCH - RING):
                keys(c + RING, NP * (NB - 1), 3 * NCH * (NB - 1) + 3 * (c + 1))
            sp.wait_ge(kt_ready, 3 * NCH * NB)
            load(C_WO1, columns(w_out[1], 0))
            load(C_WO1 + 1, columns(w_out[1], P))
            with sp.Fori(0, KD // 2 - 1) as i:
                for j in range(2, 4):
                    load(C_WO1 + j, columns(w_out[1], j * P + 2 * P * i), i)
            ffn_chunks(1)

        @block.gpsimd
        def _(pool):
            count = [0, 0]

            def step(instruction, semaphore=None, which=0):
                instruction.then_inc((consts, consts1)[which], 1)
                count[which] += 1
                pool.wait_ge((consts, consts1)[which], count[which])

            for n, value in enumerate((D * EPS, DH * EPS, EPS)):
                step(nc.gpsimd.memset(eps[:, n:n + 1], value))
            step(nc.gpsimd.memset(ones[:], 1.0))
            step(nc.gpsimd.memset(blocks[:], 0.0))
            step(nc.gpsimd.memset(blocks[0:DH, 0:DH], 1.0))
            step(nc.gpsimd.memset(blocks[DH:P, DH:P], 1.0))
            step(nc.gpsimd.affine_select(out=ident[:], in_=ones[:], compare_op=ALU.is_equal, fill=0.0, base=0,
                                         pattern=[[-1, P]], channel_multiplier=1))
            step(nc.gpsimd.affine_select(out=after[:], in_=ones[:], compare_op=ALU.is_gt, fill=0.0, base=0,
                                         pattern=[[-1, P]], channel_multiplier=1))
            assert count[0] == CONSTS0
            stores = [0]

            def store(dst, src, semaphore=stored):
                pool.dma_start(dst, src).then_inc(semaphore, 16)
                stores[0] += semaphore is stored

            def memory(l):
                mb = MBS[l]
                pool.dma_start(mb["mem"][:], mem_prompt[0].rearrange("(t p) n -> p t n", p=P)).then_inc(mem_in, 16)

            def sample_loads(l, G):
                mb = MBS[l]
                for name, cache, semaphore in (("ks", cache_mem_k, ks_in), ("vs", cache_mem_v, vs_in)):
                    if G and name == "ks":
                        pool.wait_ge(tr_free, marks["ksT", l, G - 1])
                    elif G:
                        pool.wait_ge(at_pv, (l + 1) * len(MEM_UNITS) + GR * l + G)
                    pool.dma_start(mb[name][:].rearrange("p b t n -> p (b t) n"),
                                   cache[l, G * GS:(G + 1) * GS].rearrange("b (t p) h d -> p (b t) (h d)", p=P)).then_inc(semaphore, 16)

            def memory_stores(l):
                pool.wait_ge(kv_done, l + 1)
                for t, b in ((new_mem_k_p, "km"), (new_mem_v_p, "vm")):
                    store(t[l, 0].rearrange("(t p) h d -> p t (h d)", p=P), MBS[l][b][:])

            def diagonals(c):
                if c >= 2:
                    pool.wait_ge(taps_ready, c - 1)
                for n in range(2 if c >= KC - 2 else 1):
                    last = nc.gpsimd.affine_select(
                        out=(diag, diag2)[n][:, c % 2],
                        in_=dw[:, c, n * PE_TAPS:(n + 1) * PE_TAPS].unsqueeze(2).broadcast_to([P, PE_TAPS, P]),
                        compare_op=ALU.is_equal, fill=0.0, base=0, pattern=[[0, PE_TAPS], [-1, P]], channel_multiplier=1)
                last.then_inc(diag_ready, 1)
            memory(0)
            pool.wait_ge(tr_free, marks["start"])
            for c in range(KC):
                diagonals(c)
            pool.wait_ge(tr_free, marks["conv states"])
            store(new_conv_p[0, 0], stP[:])
            for G in range(GR):
                store(new_conv_s[0, G * GS:(G + 1) * GS].rearrange("b n c -> (b n) c"), stS[:, G, :])
            pool.wait_ge(stored, 16 * stores[0])
            sample_loads(0, 0)
            memory_stores(0)
            for G in range(1, GR):
                sample_loads(0, G)

            pool.wait_ge(w_used, C_FOX)
            one = lambda instruction: step(instruction, which=1)
            one(nc.gpsimd.memset(win[:], 1.0))
            one(nc.gpsimd.affine_select(out=win[:], in_=win[:], compare_op=ALU.is_ge, fill=0.0, base=-(SEQ - P),
                                        pattern=[[1, 2 * SEQ - P]], channel_multiplier=-1))
            one(nc.gpsimd.memset(maskd[:], 0.0))
            one(nc.gpsimd.affine_select(out=maskd[:], in_=maskd[:], compare_op=ALU.is_ge, fill=NEG, base=0,
                                        pattern=[[-1, P]], channel_multiplier=1))
            one(nc.gpsimd.memset(bm[:], 1.0))
            one(nc.gpsimd.affine_select(out=bm[:], in_=bm[:], compare_op=ALU.is_ge, fill=0.0, base=0,
                                        pattern=[[-NQ, NB]], channel_multiplier=1))
            one(nc.gpsimd.affine_select(out=bm[:], in_=bm[:], compare_op=ALU.is_ge, fill=0.0, base=NQ - 1,
                                        pattern=[[NQ, NB]], channel_multiplier=-1))
            one(nc.gpsimd.affine_select(out=sameq[:], in_=bm[:].unsqueeze(2).broadcast_to([NS, NB, NQ]), compare_op=ALU.is_ge,
                                        fill=0.0, base=0, pattern=[[NQ, NB], [1, NQ]], channel_multiplier=-1))
            one(nc.gpsimd.memset(mshT[:], 0.0))
            m = mshT[:].rearrange("j (h q) -> j h q", h=NH)
            one(nc.gpsimd.affine_select(out=m, in_=m, compare_op=ALU.is_ge, fill=NEG, base=-(NS - NQ),
                                        pattern=[[0, NH], [0, NQ]], channel_multiplier=1))
            one(nc.gpsimd.affine_select(out=m, in_=m, compare_op=ALU.is_ge, fill=NEG, base=NS - NQ,
                                        pattern=[[0, NH], [1, NQ]], channel_multiplier=-1))
            one(nc.gpsimd.memset(dq[:], 0.0))
            for b in range(NB):
                one(nc.gpsimd.affine_select(out=dq[:], in_=dq[:], compare_op=ALU.not_equal, fill=1.0, base=-NQ * b,
                                            pattern=[[-1, NQ]], channel_multiplier=1))
            one(nc.gpsimd.affine_select(out=later[:], in_=ones[:], compare_op=ALU.is_gt, fill=0.0, base=0,
                                        pattern=[[-1, P]], channel_multiplier=1))
            same = later[:].rearrange("p (b n) -> p b n", b=NB)
            one(nc.gpsimd.affine_select(out=same, in_=same, compare_op=ALU.is_ge, fill=0.0, base=NP - 1,
                                        pattern=[[NP, NB], [0, NP]], channel_multiplier=-1))
            assert count[1] == CONSTS1
            memory(1)
            pool.dma_start(pages[:], page_table.rearrange("b n -> (b n)").unsqueeze(0)).then_inc(pages_in, 16)
            pool.wait_ge(pages_in, 16)
            for i in range(NB * NP):
                which = pool.value_load(pages[0:1, i:i + 1], min_val=0, max_val=N_PHYS - 1)
                pool.dma_start(lfrow[i:i + 1, :], cache_fox_logf[0, bass.ds(which, 1)].rearrange("o p h -> o (p h)")).then_inc(lf_in, 16)
            pool.wait_ge(c_ready, 1)
            store(new_fox_logf_p[0, 0].rearrange("(t p) h -> p t h", p=P), lf[:, 0:TT, :])
            store(new_fox_logf_s[0].rearrange("b q h -> (b q) h"), lf[0:NS, TT, :])
            pool.wait_ge(hn_done, MP + 1 + 3 * HP)
            store(new_fox_v_p[0, 0].rearrange("(t p) h d -> p t (h d)", p=P), vtok[:, 0:TT, :])
            store(new_fox_v_s[0].rearrange("b q h d -> (b q) (h d)"), vtok[0:NS, TT, :])
            for t in range(TT + 1):
                pool.wait_ge(tr_free, marks["k", t])
                if t < TT:
                    store(new_fox_k_p[0, 0].rearrange("(t p) h d -> t p (h d)", p=P)[t], ktok[:, t % 2, :], k_stored[t % 2])
                else:
                    store(new_fox_k_s[0].rearrange("b q h d -> (b q) (h d)"), ktok[0:NS, t % 2, :], k_stored[t % 2])
            for s in range(2):
                pool.wait_ge(k_stored[s], 16 * ((TT + 2 - s) // 2))
            pool.wait_ge(tr_free, marks["forget"])
            memory_stores(1)
            pool.wait_ge(w_used, C_MEM1 + N_MEM)
            sample_loads(1, 0)
            sample_loads(1, 1)
            assert GR == 2

            assert stores[0] == marks["km stored"]
            pool.wait_ge(w_used, C_WO1)
            pool.wait_ge(tr_free, marks["far"])

            def values(c, first):
                for pp in range(CPG):
                    p = pool.value_load(pages[0:1, bass.ds(first + CPG * c + pp, 1)], min_val=0, max_val=N_PHYS - 1)
                    pool.dma_start(vring[c % RING][:, pp, :], cache_fox_v[0, bass.ds(p, 1)].rearrange("o p h d -> (o p) (h d)"))\
                        .then_inc(v_in[c % RING], 16)
            for c in range(RING):
                values(c, 0)
            with pool.Fori(0, NB - 1) as b:
                for c in range(NCH):
                    pool.wait_ge(v_used, NCH * b + c + 1)
                    values(c + RING, NP * b)
            for c in range(NCH - RING):
                pool.wait_ge(v_used, NCH * (NB - 1) + c + 1)
                values(c + RING, NP * (NB - 1))
            for t in range(TT + 1):
                pool.wait_ge(tr_free, marks["y", t])
                if t < TT:
                    store(y_prompt[0].rearrange("(t p) n -> t p n", p=P)[t], ystage[:, t % 2, :], y_stored[t % 2])
                else:
                    store(y_sample.rearrange("b q n -> (b q) n"), ystage[0:NS, t % 2, :], y_stored[t % 2])
            pool.wait_ge(stored, 16 * stores[0])
            for s in range(2):
                pool.wait_ge(y_stored[s], 16 * ((TT + 2 - s) // 2))


_INS = ['x_prompt', 'x_sample', 'cache_conv', 'cache_fox_k', 'cache_fox_v', 'cache_fox_logf', 'cache_mem_k',
        'cache_mem_v', 'page_table', 'mem_prompt', 'norm1', 'conv_w_in', 'conv_dw', 'conv_dw_b', 'conv_ln_g',
        'conv_ln_b', 'fox_w_in', 'fox_b_f', 'fox_q_norm', 'fox_k_norm', 'mem_norm', 'w_mem_kv', 'mem_q_norm',
        'mem_k_norm', 'w_out', 'norm2', 'w_gate_up', 'w_down']


def kernel(**inputs):
    import numpy as _np
    import concourse.bacc as _bacc
    from concourse import mybir as _mybir
    from concourse.bass_utils import run_bass_kernel_spmd as _run

    nc = _bacc.Bacc("TRN2", target_bir_lowering=False, num_devices=1)
    arrays, args = {}, []
    for name in _INS:
        a = _np.ascontiguousarray(inputs[name])
        arrays[f"in_{name}_dram"] = a
        args.append(nc.dram_tensor(f"in_{name}_dram", a.shape, _mybir.dt.from_np(a.dtype), kind="ExternalInput").ap())
    _, S_, D_ = inputs["x_prompt"].shape
    NB_, NQ_ = inputs["x_sample"].shape[:2]
    _, H_, C_ = inputs["cache_conv"].shape[1:]
    NH_, DH_ = inputs["cache_fox_k"].shape[3:]
    L_, _, NM_, MH_, _ = inputs["cache_mem_k"].shape
    outs = [(1, S_, D_), (NB_, NQ_, D_), (1, 1, H_, C_), (1, 1, S_, NH_, DH_), (1, 1, S_, NH_, DH_), (1, 1, S_, NH_),
            (L_, 1, NM_, MH_, DH_), (L_, 1, NM_, MH_, DH_), (1, NB_, H_, C_), (1, NB_, NQ_, NH_, DH_),
            (1, NB_, NQ_, NH_, DH_), (1, NB_, NQ_, NH_)]
    for i, shape in enumerate(outs):
        args.append(nc.dram_tensor(f"out_{i}_dram", shape, _mybir.dt.float32, kind="ExternalOutput").ap())
    build(nc, *args)
    r = _run(nc, [arrays], core_ids=[0])
    return tuple(r.results[0][f"out_{i}_dram"] for i in range(len(outs)))
```
